# Optimizing a Trainium2 kernel written in Bass

```python
import math
import jax, jax.numpy as jnp
from jax import lax
import numpy as np
import jax
import jax.numpy as jnp

D_MODEL = 1024
BATCH = 1
SEQ = 512
DEPTH = 2

CHUNK = 64
N_META = 16
Q_BLOCK = 128
ROPE_THETA = 500000.0
NORM_EPS = 1e-6

POOL_WINDOWS = (2, 4, 8, 16)
POOL_GROUP = D_MODEL // 8
POOL_WIDTH = POOL_GROUP * len(POOL_WINDOWS)

DA_HEADS = 4
DA_DIM = 64
DA_VDIM = 2 * DA_DIM
DA_QK = DA_HEADS * 2 * DA_DIM
DA_WIDTH = DA_HEADS * DA_VDIM
DA_ROPE = DA_DIM // 4
DA_SUBLN_EPS = 1e-5

RW_HEAD = 64
RW_WIDTH = D_MODEL // 2
RW_HEADS = RW_WIDTH // RW_HEAD
RW_DECAY_LORA = 64
RW_A_LORA = 64
RW_GATE_LORA = 128
RW_SHIFT_WIDTH = 3 * RW_WIDTH + RW_DECAY_LORA + RW_A_LORA + RW_GATE_LORA
RW_SPLITS = (RW_WIDTH, 2 * RW_WIDTH, 3 * RW_WIDTH, 3 * RW_WIDTH + RW_DECAY_LORA,
             3 * RW_WIDTH + RW_DECAY_LORA + RW_A_LORA)
RW_GN_EPS = 64e-5

N_BRANCH = 3
BRANCH_WIDTH = 512
IN_PARTS = (POOL_WIDTH, DA_QK, DA_QK, DA_WIDTH, RW_SHIFT_WIDTH, N_BRANCH * D_MODEL)
IN_WIDTH = sum(IN_PARTS)
IN_SPLITS = tuple(int(s) for s in np.cumsum(IN_PARTS)[:-1])

D_FF = 2816
CONV_WIDTH = 3


def rms_norm(x, g, eps=NORM_EPS):
    xf = x.astype(jnp.float32)
    y = xf * lax.rsqrt(jnp.mean(xf * xf, axis=-1, keepdims=True) + eps)
    return (y * g.astype(jnp.float32)).astype(x.dtype)

def rope_tables(n):
    pos = jnp.arange(n, dtype=jnp.float32)
    inv = ROPE_THETA ** (-jnp.arange(0, DA_ROPE, 2, dtype=jnp.float32) / DA_ROPE)
    ang = pos[:, None] * inv[None, :]
    return jnp.cos(ang), jnp.sin(ang)

def partial_rope(t, cos, sin):
    half = DA_ROPE // 2
    c = cos[None, :, None, None, :].astype(t.dtype)
    s = sin[None, :, None, None, :].astype(t.dtype)
    t1 = t[..., :half]
    t2 = t[..., half:DA_ROPE]
    return jnp.concatenate([t1 * c - t2 * s, t2 * c + t1 * s, t[..., DA_ROPE:]], axis=-1)

def pool_mixer(u, w_group, scale):
    B, L, _ = u.shape
    uf = u.astype(jnp.float32).reshape(B, L, len(POOL_WINDOWS), POOL_GROUP)
    cs = jnp.cumsum(uf, axis=1)
    t1 = jnp.arange(1, L + 1, dtype=jnp.float32)
    outs = []
    for g, w in enumerate(POOL_WINDOWS):
        c = cs[:, :, g]
        lag = jnp.pad(c, ((0, 0), (w, 0), (0, 0)))[:, :L]
        cnt = jnp.minimum(t1, float(w))[None, :, None]
        outs.append((c - lag) / cnt - uf[:, :, g])
    pooled = jnp.stack(outs, axis=2).astype(u.dtype)
    mixed = jnp.einsum('blgc,gcd->blgd', pooled, w_group)
    return mixed.reshape(B, L, POOL_WIDTH) * scale

def diff_attention(q, k, v, lam, lambda_init, subln_w):
    B, L = q.shape[:2]
    n_blk = -(-L // Q_BLOCK)
    Lp = n_blk * Q_BLOCK
    pad5 = ((0, 0), (0, Lp - L), (0, 0), (0, 0), (0, 0))
    q = jnp.pad(q, pad5)
    k = jnp.pad(k, pad5)
    v = jnp.pad(v, pad5[:4])
    chunk = (jnp.arange(Lp) - N_META) // CHUNK
    qb = q.reshape(B, n_blk, Q_BLOCK, DA_HEADS, 2, DA_DIM).transpose(1, 0, 2, 3, 4, 5)
    cb = chunk.reshape(n_blk, Q_BLOCK)
    scale = DA_DIM ** -0.5

    def block(args):
        qi, ci = args
        s = jnp.einsum('bqhcd,bkhcd->bhcqk', qi, k).astype(jnp.float32) * scale
        mask = chunk[None, :] <= ci[:, None]
        s = jnp.where(mask, s, -jnp.inf)
        p = jax.nn.softmax(s, axis=-1)
        a = p[:, :, 0] - lam * p[:, :, 1]
        return jnp.einsum('bhqk,bkhe->bqhe', a.astype(v.dtype), v)

    o = lax.map(block, (qb, cb))
    o = o.transpose(1, 0, 2, 3, 4).reshape(B, Lp, DA_HEADS, DA_VDIM)[:, :L]
    o = rms_norm(o, subln_w, DA_SUBLN_EPS) * (1.0 - lambda_init)
    return o.reshape(B, L, DA_WIDTH)

def token_shift(t):
    return jnp.pad(t, ((0, 0), (1, 0), (0, 0)))[:, :-1]

def rwkv7_mixer(p, mu, w0, w2, a0, a2, g2, k_k, k_a, r_k, lnx_w, lnx_b):
    B, L, _ = p.shape
    f32 = jnp.float32
    p = p + mu * (token_shift(p) - p)
    r, k, v, wl, al, gl = jnp.split(p, RW_SPLITS, axis=-1)
    w_log = -jax.nn.softplus(-(w0 + jnp.tanh(wl) @ w2)) - 0.5
    decay = jnp.exp(-jnp.exp(w_log.astype(f32)))
    a = jax.nn.sigmoid(a0 + al @ a2)
    g = jax.nn.sigmoid(gl) @ g2
    heads = lambda t: t.reshape(B, L, RW_HEADS, RW_HEAD).astype(f32)
    kk = heads(k * k_k)
    kk = kk / jnp.maximum(jnp.sqrt(jnp.sum(kk * kk, axis=-1, keepdims=True)), 1e-12)
    k = k * (1.0 + (a - 1.0) * k_a)
    rh, kh, vh, ah, dh = heads(r), heads(k), heads(v), heads(a), heads(decay)
    rem = -kk
    rep = kk * ah

    def step(S, inp):
        r_t, w_t, k_t, v_t, a_t, b_t = inp
        S = (S * w_t[:, :, None, :]
             + jnp.einsum('bhvk,bhk->bhv', S, a_t)[..., None] * b_t[:, :, None, :]
             + v_t[..., None] * k_t[:, :, None, :])
        return S, jnp.einsum('bhvk,bhk->bhv', S, r_t)

    xs = tuple(t.transpose(1, 0, 2, 3) for t in (rh, dh, kh, vh, rem, rep))
    S0 = jnp.zeros((B, RW_HEADS, RW_HEAD, RW_HEAD), f32)
    _, y = lax.scan(step, S0, xs)
    y = y.transpose(1, 0, 2, 3)
    mean = jnp.mean(y, axis=-1, keepdims=True)
    var = jnp.mean(jnp.square(y - mean), axis=-1, keepdims=True)
    y = ((y - mean) * lax.rsqrt(var + RW_GN_EPS)).reshape(B, L, RW_WIDTH)
    y = y * lnx_w.astype(f32) + lnx_b.astype(f32)
    bonus = jnp.sum(rh * kh * r_k.astype(f32), axis=-1, keepdims=True) * vh
    y = (y + bonus.reshape(B, L, RW_WIDTH)) * g.astype(f32)
    return y.astype(p.dtype)

def conv_glu_ffn(h, w_up, conv_w, w_down):
    u = h @ w_up
    C = u.shape[-1]
    u = lax.conv_general_dilated(u, conv_w[:, None, :].astype(u.dtype), window_strides=(1,),
                                 padding=[(CONV_WIDTH - 1, 0)],
                                 dimension_numbers=('NWC', 'WIO', 'NWC'),
                                 feature_group_count=C)
    gate, up = jnp.split(u, 2, axis=-1)
    return (jax.nn.silu(gate) * up) @ w_down

def first_inputs(seed: int = 0) -> dict:
    key = jax.random.key(seed)
    ks = iter(jax.random.split(key, 32))
    f32 = jnp.float32
    nrm = lambda shape, s: jax.random.normal(next(ks), shape, f32) * s
    uni = lambda shape, lo, hi: jax.random.uniform(next(ks), shape, f32, lo, hi)
    Ld = DEPTH
    return {
        "x": nrm((BATCH, SEQ, D_MODEL), 1.0),
        "meta_tokens": nrm((N_META, D_MODEL), 1.0),
        "norm_mix": 1.0 + nrm((Ld, D_MODEL), 0.02),
        "norm_ffn": 1.0 + nrm((Ld, D_MODEL), 0.02),
        "norm_final": 1.0 + nrm((D_MODEL,), 0.02),
        "w_in": nrm((Ld, D_MODEL, IN_WIDTH), D_MODEL ** -0.5),
        "pool_w": nrm((Ld, len(POOL_WINDOWS), POOL_GROUP, POOL_GROUP), POOL_GROUP ** -0.5),
        "pool_scale": 1.0 + nrm((Ld, POOL_WIDTH), 0.02),
        "da_lambda": nrm((Ld, 4, DA_DIM), 0.1),
        "da_subln": 1.0 + nrm((Ld, DA_VDIM), 0.02),
        "rw_mu": uni((Ld, RW_SHIFT_WIDTH), 0.0, 1.0),
        "rw_w0": uni((Ld, RW_WIDTH), -5.0, 1.0),
        "rw_w2": nrm((Ld, RW_DECAY_LORA, RW_WIDTH), 0.05),
        "rw_a0": nrm((Ld, RW_WIDTH), 0.5),
        "rw_a2": nrm((Ld, RW_A_LORA, RW_WIDTH), 0.1),
        "rw_g2": nrm((Ld, RW_GATE_LORA, RW_WIDTH), RW_GATE_LORA ** -0.5),
        "rw_k_k": 0.85 + nrm((Ld, RW_WIDTH), 0.05),
        "rw_k_a": 1.0 + nrm((Ld, RW_WIDTH), 0.05),
        "rw_r_k": nrm((Ld, RW_HEADS, RW_HEAD), 0.1),
        "rw_lnx_w": 1.0 + nrm((Ld, RW_WIDTH), 0.02),
        "rw_lnx_b": nrm((Ld, RW_WIDTH), 0.02),
        "w_branch": nrm((Ld, N_BRANCH, BRANCH_WIDTH, D_MODEL), BRANCH_WIDTH ** -0.5),
        "w_out": nrm((Ld, D_MODEL, D_MODEL), D_MODEL ** -0.5),
        "ffn_up": nrm((Ld, D_MODEL, 2 * D_FF), D_MODEL ** -0.5),
        "ffn_conv": nrm((Ld, CONV_WIDTH, 2 * D_FF), 0.5),
        "ffn_down": nrm((Ld, D_FF, D_MODEL), D_FF ** -0.5),
    }

def first_block(x, meta_tokens, norm_mix, norm_ffn, norm_final, w_in, pool_w, pool_scale,
              da_lambda, da_subln, rw_mu, rw_w0, rw_w2, rw_a0, rw_a2, rw_g2, rw_k_k, rw_k_a,
              rw_r_k, rw_lnx_w, rw_lnx_b, w_branch, w_out, ffn_up, ffn_conv, ffn_down):
    B = x.shape[0]
    meta = jnp.broadcast_to(meta_tokens[None].astype(x.dtype), (B, N_META, D_MODEL))
    x = jnp.concatenate([meta, x], axis=1)
    L = x.shape[1]
    cos, sin = rope_tables(L)
    for l in range(DEPTH):
        lambda_init = 0.8 - 0.6 * math.exp(-0.3 * l)
        h = rms_norm(x, norm_mix[l])
        proj = h @ w_in[l]
        u_pool, q, k, v, p_rw, gate_logits = jnp.split(proj, IN_SPLITS, axis=-1)
        b_pool = pool_mixer(u_pool, pool_w[l], pool_scale[l])
        q = partial_rope(q.reshape(B, L, DA_HEADS, 2, DA_DIM), cos, sin)
        k = partial_rope(k.reshape(B, L, DA_HEADS, 2, DA_DIM), cos, sin)
        v = v.reshape(B, L, DA_HEADS, DA_VDIM)
        lq1, lk1, lq2, lk2 = [da_lambda[l, i].astype(jnp.float32) for i in range(4)]
        lam = jnp.exp(jnp.sum(lq1 * lk1)) - jnp.exp(jnp.sum(lq2 * lk2)) + lambda_init
        b_da = diff_attention(q, k, v, lam, lambda_init, da_subln[l])
        b_rw = rwkv7_mixer(p_rw, rw_mu[l], rw_w0[l], rw_w2[l], rw_a0[l], rw_a2[l], rw_g2[l],
                           rw_k_k[l], rw_k_a[l], rw_r_k[l], rw_lnx_w[l], rw_lnx_b[l])
        branches = jnp.stack([b_pool, b_da, b_rw], axis=2)
        up = jnp.einsum('blnc,ncd->blnd', branches, w_branch[l])
        gates = jax.nn.sigmoid(gate_logits.reshape(B, L, N_BRANCH, D_MODEL).astype(jnp.float32))
        merged = jnp.sum(gates.astype(up.dtype) * up, axis=2)
        x = x + merged @ w_out[l]
        x = x + conv_glu_ffn(rms_norm(x, norm_ffn[l]), ffn_up[l], ffn_conv[l], ffn_down[l])
    return rms_norm(x, norm_final)[:, N_META:]


_first_inputs = first_inputs


def first_inputs(seed=0):
    import zlib

    import numpy as np

    out = dict(_first_inputs(seed))
    spreads = {}
    factors = {'norm_ffn': 4.229,
     'norm_final': 2.877,
     'pool_scale': 5.05,
     'da_subln': 5.236,
     'rw_w2': 5.842,
     'rw_k_k': 4.387,
     'rw_k_a': 2.88,
     'rw_lnx_w': 8.0,
     'rw_lnx_b': 7.01}
    for name, (base, spread) in spreads.items():
        noise = np.random.default_rng([zlib.crc32(name.encode()), seed]).standard_normal(out[name].shape)
        drawn = base * np.exp(spread * noise) if base else spread * noise
        out[name] = __import__('jax').numpy.asarray(drawn.astype(out[name].dtype))
    for name, factor in factors.items():
        out[name] = (out[name] * factor).astype(out[name].dtype)
    return out


_narrow_inputs = first_inputs


def first_inputs(seed=0):

    out = dict(_narrow_inputs(seed))
    wider = {'norm_final': 3.24,
     'pool_scale': 3.08,
     'da_subln': 3.14,
     'rw_lnx_w': 3.12,
     'rw_lnx_b': 3.32}
    for name, times in wider.items():
        mean = out[name].mean()
        out[name] = (mean + times * (out[name] - mean)).astype(out[name].dtype)
    return out


DEPTH_2 = 1

HGRN_WIDTH = D_MODEL // 2
CONV_WIDTH_2 = D_MODEL - HGRN_WIDTH
HGRN_EXPAND = 128
HGRN_HEADS = HGRN_WIDTH // HGRN_EXPAND
HGRN_HEAD_V = HGRN_WIDTH // HGRN_HEADS
CONV_KERNEL = 31
IN_COLS = 4 * HGRN_WIDTH + 2 * CONV_WIDTH_2
N_EXPERTS = 16
N_EXPERT_GROUPS = 4
EXPERTS_PER_GROUP = N_EXPERTS // N_EXPERT_GROUPS
TOP_K = 2
D_EXPERT = D_MODEL // 2
ALPHA = (2 * DEPTH_2) ** 0.25
BETA = (8 * DEPTH_2) ** -0.25
EPS = 1e-5


def _layernorm(x):
    xf = x.astype(jnp.float32)
    mu = jnp.mean(xf, axis=-1, keepdims=True)
    var = jnp.mean(jnp.square(xf - mu), axis=-1, keepdims=True)
    return (xf - mu) * lax.rsqrt(var + EPS)

def _modulate(x, shift, scale):
    return (_layernorm(x) * (1.0 + scale) + shift).astype(x.dtype)

def _post_ln(z, g, b):
    return (_layernorm(z) * g + b).astype(z.dtype)

def _layer_lower_bounds(lb_param):
    p = jax.nn.softmax(lb_param.astype(jnp.float32), axis=0)
    cs = jnp.cumsum(p, axis=0)
    return cs - cs[0:1]

def _hgrn2(q, f_logit, i, lb):
    B, T = q.shape[0], q.shape[1]
    n = T // CHUNK
    f32 = jnp.float32
    lbf = lb.astype(f32)
    g = jnp.logaddexp(jnp.log(lbf), jnp.log1p(-lbf) + jax.nn.log_sigmoid(f_logit.astype(f32)))
    k = -jnp.expm1(g)
    qf = jax.nn.silu(q.astype(f32))
    vf = i.astype(f32)

    def to_chunks(t):
        return t.reshape(B, n, CHUNK, t.shape[2], t.shape[3]).transpose(1, 0, 3, 2, 4)

    causal = jnp.tril(jnp.ones((CHUNK, CHUNK), dtype=bool))

    def step(S, inp):
        qc, kc, vc, gc = inp
        b = jnp.cumsum(gc, axis=2)
        diff = b[:, :, :, None, :] - b[:, :, None, :, :]
        decay = jnp.exp(jnp.where(causal[:, :, None], diff, -jnp.inf))
        scores = jnp.einsum('bhtk,bhsk,bhtsk->bhts', qc, kc, decay)
        o = (jnp.einsum('bhts,bhsv->bhtv', scores, vc)
             + jnp.einsum('bhtk,bhkv->bhtv', qc * jnp.exp(b), S))
        b_last = b[:, :, -1, :]
        S_new = (jnp.exp(b_last)[..., None] * S
                 + jnp.einsum('bhsk,bhsv->bhkv', kc * jnp.exp(b_last[:, :, None, :] - b), vc))
        return S_new, o

    S0 = jnp.zeros((B, HGRN_HEADS, HGRN_EXPAND, HGRN_HEAD_V), f32)
    _, o = lax.scan(step, S0, (to_chunks(qf), to_chunks(k), to_chunks(vf), to_chunks(g)))
    return o.transpose(1, 0, 3, 2, 4).reshape(B, T, HGRN_HEADS, HGRN_HEAD_V)

def _mixer(u, w_in, b_in, lb, norm_w, conv_w, conv_b, conv_g, conv_bb, w_out, b_out):
    B, T, _ = u.shape
    dt = u.dtype
    proj = u @ w_in + b_in
    H, C = HGRN_WIDTH, CONV_WIDTH_2
    q, f, i, og, ca, cgt = jnp.split(proj, [H, 2 * H, 3 * H, 4 * H, 4 * H + C], axis=-1)
    hs = (B, T, HGRN_HEADS, HGRN_EXPAND)
    o = _hgrn2(q.reshape(hs), f.reshape(hs), i.reshape(B, T, HGRN_HEADS, HGRN_HEAD_V),
               lb.reshape(HGRN_HEADS, HGRN_EXPAND))
    o = o * lax.rsqrt(jnp.mean(jnp.square(o), axis=-1, keepdims=True) + EPS) * norm_w
    h_a = (o.reshape(B, T, H) * jax.nn.silu(og.astype(jnp.float32))).astype(dt)
    a = ca * jax.nn.sigmoid(cgt)
    a = lax.conv_general_dilated(a, conv_w[:, None, :], window_strides=(1,),
                                 padding=[(CONV_KERNEL - 1, 0)],
                                 dimension_numbers=('NWC', 'WIO', 'NWC'),
                                 feature_group_count=CONV_WIDTH_2) + conv_b
    h_b = jax.nn.silu(_layernorm(a) * conv_g + conv_bb).astype(dt)
    return jnp.concatenate([h_a, h_b], axis=-1) @ w_out + b_out

def _moe(u, router_w, router_bias, w_gate, w_up, w_down):
    B, T, D = u.shape
    dt = u.dtype
    t = u.reshape(B * T, D)
    s = jax.nn.sigmoid((t @ router_w).astype(jnp.float32))
    sb = s + router_bias.astype(jnp.float32)
    grp_score = jnp.sum(lax.top_k(sb.reshape(-1, N_EXPERT_GROUPS, EXPERTS_PER_GROUP), TOP_K)[0], axis=-1)
    gsel = jnp.argmax(grp_score, axis=-1)
    in_group = (jnp.arange(N_EXPERTS) // EXPERTS_PER_GROUP)[None, :] == gsel[:, None]
    _, idx = lax.top_k(jnp.where(in_group, sb, -jnp.inf), TOP_K)
    w_sel = jnp.take_along_axis(s, idx, axis=-1)
    w_sel = w_sel / jnp.sum(w_sel, axis=-1, keepdims=True)
    combine = jnp.sum(jax.nn.one_hot(idx, N_EXPERTS, dtype=jnp.float32) * w_sel[..., None], axis=1).astype(dt)
    y = jnp.zeros_like(t)
    for e in range(N_EXPERTS):
        h = jax.nn.silu(t @ w_gate[e]) * (t @ w_up[e])
        y = y + combine[:, e:e + 1] * (h @ w_down[e])
    return y.reshape(B, T, D)

def second_inputs(seed: int = 0) -> dict:
    key = jax.random.key(seed)
    ks = jax.random.split(key, 24)
    f32 = jnp.float32
    D = D_MODEL

    def nrm(k, shape, s):
        return jax.random.normal(k, shape, f32) * s

    return {
        "x": nrm(ks[0], (BATCH, SEQ, D), 1.0),
        "c": nrm(ks[1], (BATCH, D), 1.0),
        "ada_w": nrm(ks[2], (DEPTH_2, D, 6 * D), 0.5 * D ** -0.5),
        "ada_b": nrm(ks[3], (DEPTH_2, 6 * D), 0.01),
        "w_in": nrm(ks[4], (DEPTH_2, D, IN_COLS), D ** -0.5),
        "b_in": nrm(ks[5], (DEPTH_2, IN_COLS), 0.01),
        "hgrn_lb": nrm(ks[6], (DEPTH_2, HGRN_WIDTH), 0.5),
        "hgrn_norm_w": 1.0 + nrm(ks[7], (DEPTH_2, HGRN_HEAD_V), 0.01),
        "conv_w": nrm(ks[8], (DEPTH_2, CONV_KERNEL, CONV_WIDTH_2), CONV_KERNEL ** -0.5),
        "conv_b": nrm(ks[9], (DEPTH_2, CONV_WIDTH_2), 0.01),
        "conv_ln_g": 1.0 + nrm(ks[10], (DEPTH_2, CONV_WIDTH_2), 0.01),
        "conv_ln_b": nrm(ks[11], (DEPTH_2, CONV_WIDTH_2), 0.01),
        "w_out": nrm(ks[12], (DEPTH_2, HGRN_WIDTH + CONV_WIDTH_2, D), BETA * D ** -0.5),
        "b_out": nrm(ks[13], (DEPTH_2, D), 0.01),
        "ln1_g": 1.0 + nrm(ks[14], (DEPTH_2, D), 0.01),
        "ln1_b": nrm(ks[15], (DEPTH_2, D), 0.01),
        "router_w": nrm(ks[16], (D, N_EXPERTS), D ** -0.5),
        "router_bias": nrm(ks[17], (N_EXPERTS,), 0.01),
        "w_gate": nrm(ks[18], (DEPTH_2, N_EXPERTS, D, D_EXPERT), D ** -0.5),
        "w_up": nrm(ks[19], (DEPTH_2, N_EXPERTS, D, D_EXPERT), D ** -0.5),
        "w_down": nrm(ks[20], (DEPTH_2, N_EXPERTS, D_EXPERT, D), BETA * D_EXPERT ** -0.5),
        "ln2_g": 1.0 + nrm(ks[21], (DEPTH_2, D), 0.01),
        "ln2_b": nrm(ks[22], (DEPTH_2, D), 0.01),
    }

def second_block(x, c, ada_w, ada_b, w_in, b_in, hgrn_lb, hgrn_norm_w, conv_w, conv_b,
              conv_ln_g, conv_ln_b, w_out, b_out, ln1_g, ln1_b, router_w, router_bias,
              w_gate, w_up, w_down, ln2_g, ln2_b):
    lb_all = _layer_lower_bounds(hgrn_lb)
    cond = jax.nn.silu(c)
    for l in range(DEPTH_2):
        mod = cond @ ada_w[l] + ada_b[l]
        sh1, sc1, g1, sh2, sc2, g2 = jnp.split(mod[:, None, :], 6, axis=-1)
        u = _modulate(x, sh1, sc1)
        y = _mixer(u, w_in[l], b_in[l], lb_all[l], hgrn_norm_w[l], conv_w[l], conv_b[l],
                   conv_ln_g[l], conv_ln_b[l], w_out[l], b_out[l])
        x = _post_ln(ALPHA * x + g1 * y, ln1_g[l], ln1_b[l])
        u = _modulate(x, sh2, sc2)
        y = _moe(u, router_w, router_bias, w_gate[l], w_up[l], w_down[l])
        x = _post_ln(ALPHA * x + g2 * y, ln2_g[l], ln2_b[l])
    return x


_first_inputs_2 = second_inputs


def second_inputs(seed=0):
    import zlib

    import numpy as np

    out = dict(_first_inputs_2(seed))
    spreads = {}
    factors = {'ada_b': 4.091,
     'b_in': 8.0,
     'hgrn_norm_w': 64.0,
     'conv_b': 8.0,
     'conv_ln_g': 64.0,
     'conv_ln_b': 64.0,
     'b_out': 28.136,
     'ln1_g': 22.742,
     'ln1_b': 22.305,
     'router_bias': 25.456,
     'ln2_g': 30.206,
     'ln2_b': 30.998,
     'router_w': 3.294,
     'w_gate': 3.206,
     'w_up': 2.994,
     'w_down': 3.003}
    for name, (base, spread) in spreads.items():
        noise = np.random.default_rng([zlib.crc32(name.encode()), seed]).standard_normal(out[name].shape)
        drawn = base * np.exp(spread * noise) if base else spread * noise
        out[name] = jnp.asarray(drawn.astype(out[name].dtype))
    for name, factor in factors.items():
        out[name] = (out[name] * factor).astype(out[name].dtype)
    return out


_narrow_inputs_2 = second_inputs


def second_inputs(seed=0):

    out = dict(_narrow_inputs_2(seed))
    wider = {'hgrn_norm_w': 5.04,
     'conv_ln_g': 4.69,
     'conv_ln_b': 5.53,
     'b_out': 4.06,
     'ln1_g': 3.93,
     'ln1_b': 4.0,
     'ln2_g': 6.21,
     'ln2_b': 6.19}
    for name, times in wider.items():
        mean = out[name].mean()
        out[name] = (mean + times * (out[name] - mean)).astype(out[name].dtype)
    return out


def setup_inputs(seed=0):
    out = dict(first_inputs(seed))
    for name, value in second_inputs(seed + 1).items():
        if name != "x":
            out[name + "_2"] = value
    return out


def reference(
    x, meta_tokens, norm_mix, norm_ffn, norm_final, w_in, pool_w, pool_scale, da_lambda,
    da_subln, rw_mu, rw_w0, rw_w2, rw_a0, rw_a2, rw_g2, rw_k_k, rw_k_a, rw_r_k, rw_lnx_w,
    rw_lnx_b, w_branch, w_out, ffn_up, ffn_conv, ffn_down, c_2, ada_w_2, ada_b_2, w_in_2,
    b_in_2, hgrn_lb_2, hgrn_norm_w_2, conv_w_2, conv_b_2, conv_ln_g_2, conv_ln_b_2, w_out_2,
    b_out_2, ln1_g_2, ln1_b_2, router_w_2, router_bias_2, w_gate_2, w_up_2, w_down_2, ln2_g_2,
    ln2_b_2,
):
    x = first_block(
        x, meta_tokens, norm_mix, norm_ffn, norm_final, w_in, pool_w, pool_scale, da_lambda,
        da_subln, rw_mu, rw_w0, rw_w2, rw_a0, rw_a2, rw_g2, rw_k_k, rw_k_a, rw_r_k, rw_lnx_w,
        rw_lnx_b, w_branch, w_out, ffn_up, ffn_conv, ffn_down,
    )
    return second_block(
        x, c_2, ada_w_2, ada_b_2, w_in_2, b_in_2, hgrn_lb_2, hgrn_norm_w_2, conv_w_2, conv_b_2,
        conv_ln_g_2, conv_ln_b_2, w_out_2, b_out_2, ln1_g_2, ln1_b_2, router_w_2, router_bias_2,
        w_gate_2, w_up_2, w_down_2, ln2_g_2, ln2_b_2,
    )


_drawn_inputs = setup_inputs


def setup_inputs(seed=0):
    import zlib

    import numpy as np

    out = dict(_drawn_inputs(seed))
    spreads = {}
    factors = {}
    for name, (base, spread) in spreads.items():
        noise = np.random.default_rng([zlib.crc32(name.encode()), seed]).standard_normal(out[name].shape)
        drawn = base * np.exp(spread * noise) if base else spread * noise
        out[name] = jnp.asarray(drawn.astype(out[name].dtype))
    for name, factor in factors.items():
        out[name] = (out[name] * factor).astype(out[name].dtype)
    return out
```

```python
import math
import numpy as np
import concourse.bass as bass
from concourse import mybir
from contextlib import ExitStack

F32 = mybir.dt.float32
ALU = mybir.AluOpType
ACT = mybir.ActivationFunctionType
AX = mybir.AxisListType
MUL, ADD, SUB, MAX, MIN = ALU.mult, ALU.add, ALU.subtract, ALU.max, ALU.min

T = 528
TILES = [(0, 16), (16, 128), (144, 128), (272, 128), (400, 128)]
HALVES = {528: [(0, 264), (264, 264)], 512: [(0, 512)]}
ALPHA = 2.0 ** 0.25
NFF = 22



def col_plan():
    at, n = {}, 0

    def add(name, w):
        nonlocal n
        at[name] = n
        n += w

    for l in range(2):
        for name, w in (("norm_mix", 8), ("norm_ffn", 8), ("pool_scale", 4), ("da_subln", 1), ("rw_mu", 14),
                        ("rw_w0", 4), ("rw_a0", 4), ("rw_k_k", 4), ("rw_k_a", 4), ("rw_r_k", 4),
                        ("rw_lnx_w", 4), ("rw_lnx_b", 4), ("ffn_conv", 132), ("da_lambda", 4)):
            add((name, l), w)
    for name, w in (("norm_final", 8), ("c_2", 8), ("ada_b_2", 48), ("b_in_2", 24), ("hgrn_lb_2", 4),
                    ("hgrn_norm_w_2", 1), ("conv_w_2", 124), ("conv_b_2", 4), ("conv_ln_g_2", 4),
                    ("conv_ln_b_2", 4), ("b_out_2", 8), ("ln1_g_2", 8), ("ln1_b_2", 8), ("ln2_g_2", 8),
                    ("ln2_b_2", 8), ("router_bias_2", 16), ("router_w_2", 128)):
        add(name, w)
    return at, n


def const_plan():
    at, n = {}, 0
    for name, w in (("id", 128), ("one", 128), ("blk", 128), ("mA", 128), ("mAT", 128), ("mO", 128),
                    ("mUs", 128), ("mUi", 128), ("rot", 128), ("cos", T), ("sin", T), ("am", 64),
                    ("ic", 64), ("rs", T), ("hrs", 512), ("hm", 1024)):
        at[name] = (n, w)
        n += w
    return at, n


def consts():
    at, n = const_plan()
    c = np.zeros((128, n), np.float32)

    def put(name, a):
        o, w = at[name]
        c[:, o:o + w] = a

    p = np.arange(128)[:, None]
    q = np.arange(128)[None, :]
    put("id", p == q)
    put("one", 1.0)
    put("blk", p // 64 == q // 64)
    put("mA", (q < p) & (p // 16 == q // 16))
    put("mAT", (q > p) & (p // 16 == q // 16))
    put("mO", (q < p) & (p // 16 != q // 16) & (p // 64 == q // 64))
    put("mUs", (q > p) & (p // 64 == q // 64))
    put("mUi", (q >= p) & (p // 64 == q // 64))
    d, m = p % 64, q % 64
    same = p // 64 == q // 64
    put("rot", -1.0 * (same & (m < 8) & (d == m + 8)) + 1.0 * (same & (m >= 8) & (m < 16) & (d == m - 8)))
    pos = np.arange(T, dtype=np.float32)
    inv = np.float32(500000.0) ** (-np.arange(0, 16, 2, dtype=np.float32) / np.float32(16))
    ang = pos[:, None] * inv[None, :].astype(np.float32)
    C = np.ones((128, T), np.float32)
    S = np.zeros((128, T), np.float32)
    for b in (0, 64):
        for i in range(16):
            C[b + i] = np.cos(ang[:, i % 8])
            S[b + i] = np.sin(ang[:, i % 8])
    put("cos", C)
    put("sin", S)
    put("am", np.where(p < 64, -1e30, 0.0))
    ic = np.zeros((4, 16), np.float32)
    for g, w in enumerate((2, 4, 8, 16)):
        ic[g] = np.float32(1) / np.minimum(np.arange(1, 17), w).astype(np.float32)
    put("ic", ic.reshape(1, 64))
    t = np.arange(T)
    put("rs", np.where((t == 0) | ((t >= 16) & ((t - 16) % 64 == 0)), 0.0, 1.0)[None, :])
    t = np.arange(512)
    put("hrs", np.where(t % 128 == 0, 0.0, 1.0)[None, :])
    hm = np.zeros((128, 8, 128))
    for i in range(7):
        m_ = 64 >> i
        hm[:, i] = (p // (2 * m_) == q // (2 * m_)) & (p % (2 * m_) < m_) & (q % (2 * m_) >= m_)
    hm[:, 7] = p == q
    put("hm", hm.reshape(128, 1024))
    return c




class Queue:

    def __init__(self, name):
        self.name, self.items, self.n, self.seen = name, [], 0, {}

    def need(self, *toks):
        for t in toks:
            if t is None:
                continue
            if isinstance(t, list):
                self.need(*t)
                continue
            s, v = t
            if self.seen.get(s, 0) < v:
                self.seen[s] = v
                self.items.append((None, s, v))

    def do(self, fn, *toks, mark=True):
        self.need(*toks)
        if mark:
            self.n += 1
        self.items.append((fn, mark, None))
        return (self.name, self.n)

    def last(self):
        return (self.name, self.n)


class Banks:

    def __init__(self):
        self.at, self.free, self.busy = 0, [[] for _ in range(8)], [False] * 8

    def take(self, n=1):
        if n > 1 and self.at % n:
            self.at += n - self.at % n
        b = self.at % 8
        self.at = b + n
        for i in range(b, b + n):
            assert not self.busy[i], "bank still in use"
            self.busy[i] = True
        return b, [self.free[i] for i in range(b, b + n)]

    def give(self, b, n, *toks):
        for i in range(b, b + n):
            self.busy[i] = False
            self.free[i] = list(toks)


NRING = 6
SLAB = 2048


class Program:
    def __init__(self, stop=None):
        self.P, self.V, self.S, self.G, self.D = (Queue(n) for n in ("pe", "dve", "act", "pool", "sp"))
        self.ps = Banks()
        self.slabs = []
        self.slab_end = 0
        self.ring_use = [None] * NRING
        self.stop = stop
        self.fixed = []

    def slab(self, pieces):
        i = len(self.slabs)
        slot = i % NRING
        assert self.ring_use[slot] != "open"
        n = sum(p[3] * p[5] for p in pieces)
        assert n <= SLAB
        off = self.slab_end
        self.slab_end += 128 * n
        self.slabs.append(pieces)
        freed = self.ring_use[slot]
        self.ring_use[slot] = "open"
        ring = self.ring
        w = self

        def load(eng, slot=slot, n=n, off=off):
            return eng.dma_start(ring[:, slot, 0:n],
                                 w.wts[off:off + 128 * n].rearrange("(p n) -> p n", n=n)).then_inc(w.sems[f"w{slot}"], 16)

        self.D.need(freed)
        self.D.items.append((load, False, None))
        tok = (f"w{slot}", 16 * (i // NRING + 1))
        views, o = [], 0
        for (_, _, _, nk, _, nc_) in pieces:
            views.append(ring[:, slot, o:o + nk * nc_].rearrange("p (k c) -> p k c", k=nk))
            o += nk * nc_
        return views, tok, slot

    def used(self, slot, tok):
        self.ring_use[slot] = tok

    def mm(self, out, lhsT, rhs, start, stop, *toks, mark=False):
        return self.P.do(lambda e: e.matmul(out, lhsT, rhs, start=start, stop=stop, skip_group_check=True), *toks, mark=mark)

    def tr(self, out, in_, k, *toks, mark=False):
        idn = self.c("id")[0:k, 0:k]
        return self.P.do(lambda e: e.transpose(out, in_, idn), *toks, mark=mark)

    def tt(self, E, out, a, b, op, *toks):
        return E.do(lambda e: e.tensor_tensor(out, a, b, op), *toks)

    def ts(self, E, out, a, s1, op0, s2=None, op1=None, *toks):
        if op1 is None:
            return E.do(lambda e: e.tensor_scalar(out, a, s1, None, op0), *toks)
        return E.do(lambda e: e.tensor_scalar(out, a, s1, s2, op0, op1), *toks)

    def stt(self, out, a, s, b, op0, op1, *toks):
        return self.V.do(lambda e: e.scalar_tensor_tensor(out=out, in0=a, scalar=s, in1=b, op0=op0, op1=op1), *toks)

    def act(self, out, a, f, *toks, bias=0.0, scale=1.0, accum=None):
        kw = {} if accum is None else {"accum_out": accum}
        return self.S.do(lambda e: e.activation(out, a, f, bias=bias, scale=scale, **kw), *toks)

    def copy(self, E, out, a, *toks):
        if E is self.S:
            return E.do(lambda e: e.copy(out, a), *toks)
        return E.do(lambda e: e.tensor_copy(out, a), *toks)

    def zero(self, E, out, *toks):
        return E.do(lambda e: e.memset(out, 0.0), *toks)

    def recip(self, out, a, *toks):
        return self.V.do(lambda e: e.reciprocal(out, a), *toks)

    def c(self, name):
        o, w = self.cat[name]
        return self.K[:, o:o + w]

    def col(self, name, i=0, l=None):
        o = self.cols_at[name if l is None else (name, l)] + i
        return self.COLS[:, o:o + 1]

    def colr(self, name, a, b, l=None):
        o = self.cols_at[name if l is None else (name, l)]
        return self.COLS[:, o + a:o + b]

    def pv(self, b, n):
        return self.PSUM[:, b:b + 2, 0:264] if n == T else self.PSUM[:, b, 0:n]

    def tv(self, ap, n):
        return ap.rearrange("p (a b) -> p a b", a=2) if n == T else ap

    def nb(self, n):
        return 2 if n == T else 1

    def proj(self, w, m0, rhs, n, toks, b=None, free=None, first=True, last=True):
        if b is None:
            b, free = self.ps.take(self.nb(n))
        nk = w.shape[1]
        tok = None
        for hi, (a, ln) in enumerate(HALVES[n]):
            for k in range(nk):
                tok = self.mm(self.PSUM[:, b + hi, 0:ln], w[:, k, m0:m0 + 128], rhs(k, a, ln),
                              first and k == 0, last and k == nk - 1, toks, free,
                              mark=(k == nk - 1 and hi == len(HALVES[n]) - 1))
        return b, tok

    def fence(self):
        return [q.last() for q in (self.P, self.V, self.S, self.G)]

    def all_wait(self, toks=None):
        toks = toks or self.fence()
        for q in (self.P, self.V, self.S, self.G):
            q.need(toks)

    def colsum(self, mat, srcs, n, toks):
        b, free = self.ps.take(self.nb(n))
        tok = None
        for k, s in enumerate(srcs):
            for hi, (a, ln) in enumerate(HALVES[n]):
                tok = self.mm(self.PSUM[:, b + hi, 0:ln], mat, s[:, a:a + ln], k == 0, k == len(srcs) - 1,
                              toks[k], free, mark=(hi == len(HALVES[n]) - 1))
        return b, tok

    def rstd(self, out, b, n, scale, eps, tok, *toks):
        t = self.ts(self.V, self.tv(out, n), self.pv(b, n), scale, MUL, eps, ADD, tok, *toks)
        self.ps.give(b, self.nb(n), t)
        t = self.act(out, out, ACT.Sqrt, t)
        return self.recip(out, out, t)

    def rms(self, src, dst, n, gname, l, toks, rs):
        sq = [self.act(dst(k), src(k), ACT.Square, toks[k]) for k in range(8)]
        b, t = self.colsum(self.c("one"), [dst(k) for k in range(8)], n, sq)
        r = self.rstd(rs, b, n, 1.0 / 1024, 1e-6, t)
        return [self.stt(dst(k), src(k), self.col(gname, k, l), rs, MUL, MUL, r) for k in range(8)]

    def ln(self, src, dst, nt, tmp, rs, toks, scale, shift, width, func=None):
        b, t = self.colsum(self.c("one"), [src(k) for k in range(nt)], 512, toks)
        ctr, sqt = [], []
        bb, fr = None, None
        for k in range(nt):
            c_ = self.stt(dst(k), self.PSUM[:, b, 0:512], -1.0 / width, src(k), MUL, ADD, t)
            ctr.append(c_)
        self.ps.give(b, 1, ctr[-1])
        bb, fr = self.ps.take(1)
        done = [None, None]
        for k in range(nt):
            s_ = self.act(tmp(k % 2), dst(k), ACT.Square, ctr[k], done[k % 2])
            done[k % 2] = self.mm(self.PSUM[:, bb, 0:512], self.c("one"), tmp(k % 2), k == 0, k == nt - 1, s_, fr, mark=True)
        r = self.rstd(rs, bb, 512, 1.0 / width, 1e-5, done[(nt - 1) % 2])
        out = []
        for k in range(nt):
            m = self.tt(self.V, dst(k), dst(k), rs, MUL, r, ctr[k])
            out.append(self.act(dst(k), dst(k), func or ACT.Identity, m, scale=scale(k), bias=shift(k)))
        return out




def rwkv(p, l, hx, htok):
    V, S, G, P, ps = p.V, p.S, p.G, p.P, p.ps
    A = p.arena

    def R4(o):
        return A[:, o:o + 2112].rearrange("p (a t) -> p a t", a=4)

    oR, oK, oV, oBV, oAH, oBH, oT1, oLD, oAA, oT2, oT3, oBB, oWA, oGL = [2112 * i for i in range(12)] + [25344, 25872]
    Rf, Kf, Vf, BV, AH, BH, T1, LD, AA, T2, T3, BB = [R4(2112 * i) for i in range(12)]
    WA, GL = A[:, oWA:oWA + T], A[:, oGL:oGL + T]
    full = {i: A[:, 2112 * i:2112 * i + 2112] for i in range(12)}
    fR, fK, fV, fBV, fAH, fBH, fT1, fLD, fAA, fT2, fT3, fBB = [full[i] for i in range(12)]

    raw = [A[:, oT3 + 530 * i:oT3 + 530 * i + 529] for i in range(2)]
    dif = [A[:, oT2 + 530 * i:oT2 + 530 * i + T] for i in range(2)]
    z = [p.zero(V, raw[i][:, 0:1]) for i in range(2)]
    ptok = []
    dst = [Rf[:, i] for i in range(4)] + [Kf[:, i] for i in range(4)] + [Vf[:, i] for i in range(4)] + [WA, GL]
    mixed = [None, None]
    for m in range(14):
        if m % 2 == 0:
            (w,), wt, slot = p.slab([("w_in", (l,), 0, 8, 2048 + m * 128, 256)])
        b, t = p.proj(w, (m % 2) * 128, hx, T, [wt, htok])
        if m % 2 == 1:
            p.used(slot, t)
        r = raw[m % 2]
        c1 = p.copy(S, p.tv(r[:, 1:529], T), p.pv(b, T), t, mixed[m % 2], z[m % 2])
        ps.give(b, 2, c1)
        d = p.tt(V, dif[m % 2], r[:, 0:T], r[:, 1:529], SUB, c1)
        o = p.stt(dst[m], dif[m % 2], p.col("rw_mu", m, l), r[:, 1:529], MUL, ADD, d)
        mixed[m % 2] = o
        ptok.append(o)
    tr_, tk_, tv_ = ptok[3], ptok[7], ptok[11]
    (ww, gw), wt, slot = p.slab([("wa2", (l,), 0, 1, 0, 512), ("rw_g2", (l,), 0, 1, 0, 512)])
    th = p.act(WA[0:64, :], WA[0:64, :], ACT.Tanh, ptok[12])
    gs = p.act(GL, GL, ACT.Sigmoid, ptok[13])
    sg, ag = [], []
    for n in range(4):
        for part, (lo, name, out, acc) in enumerate(((0, "rw_w0", LD, sg), (64, "rw_a0", AA, ag))):
            b, fr = ps.take(2)
            for hi, (a, ln) in enumerate(HALVES[T]):
                t = p.mm(p.PSUM[:, b + hi, 0:ln], ww[lo:lo + 64, 0, n * 128:n * 128 + 128], WA[lo:lo + 64, a:a + ln],
                         True, True, wt, fr, th, ptok[12], mark=True)
            s_ = p.act(p.tv(out[:, n], T), p.pv(b, T), ACT.Sigmoid, t, bias=p.col(name, n, l))
            ps.give(b, 2, s_)
            acc.append(s_)
    ld = p.ts(V, fLD, fLD, -math.exp(-0.5), MUL, None, None, sg[-1])
    bt = [V.do(lambda e, n=n: e.tensor_tensor_scan(BB[:, n], p.c("rs"), LD[:, n], 0.0, MUL, ADD), ld) for n in range(4)][-1]
    kk = [p.ts(V, T1[:, n], Kf[:, n], p.col("rw_k_k", n, l), MUL, None, None, tk_) for n in range(4)]
    sq = [p.act(T2[:, n], T1[:, n], ACT.Square, kk[n], ptok[13]) for n in range(4)]
    mx = []
    for n in range(4):
        b, t = p.colsum(p.c("blk"), [T2[:, n]], T, [sq[n]])
        t = p.ts(V, p.tv(T2[:, n], T), p.pv(b, T), 1e-24, MAX, None, None, t)
        ps.give(b, 2, t)
        mx.append(t)
    t = p.act(fT2, fT2, ACT.Sqrt, mx[-1])
    t = p.recip(fT2, fT2, t)
    kkn = p.tt(V, fT1, fT1, fT2, MUL, t)
    k1 = []
    for n in range(4):
        t = p.ts(V, T3[:, n], AA[:, n], -1.0, ADD, p.col("rw_k_a", n, l), MUL, ag[-1], mixed)
        k1.append(p.stt(Kf[:, n], T3[:, n], 1.0, Kf[:, n], ADD, MUL, t))
    bo = []
    for n in range(4):
        t = p.stt(T2[:, n], Rf[:, n], p.col("rw_r_k", n, l), Kf[:, n], MUL, MUL, k1[n], kkn, tr_)
        b, t = p.colsum(p.c("blk"), [T2[:, n]], T, [t])
        t2 = p.tt(V, p.tv(BV[:, n], T), p.pv(b, T), p.tv(Vf[:, n], T), MUL, t, tv_)
        ps.give(b, 2, t2)
        bo.append(t2)
    sb = p.tt(V, fT3, fBB, fLD, SUB, bt, k1[-1])
    e1 = p.act(fT3, fT3, ACT.Exp, sb)
    ah = p.stt(fAH, fT1, -1.0, fT3, MUL, MUL, e1, kkn)
    be = p.tt(V, fT1, fT1, fAA, MUL, ah)
    e2 = p.act(fT2, fBB, ACT.Exp, bo[-1], scale=-1.0)
    bh = p.tt(V, fBH, fT1, fT2, MUL, e2, be)
    kh = p.tt(V, fK, fK, fT2, MUL, e2, bo[-1])
    e3 = p.act(fLD, fBB, ACT.Exp, sb)
    rh = p.tt(V, fR, fR, fLD, MUL, e3, bo[-1])
    DE = p.small[:, 0:36].rearrange("p (a c) -> p a c", a=4)
    de = p.copy(V, DE, LD[:, :, 15::64], e3)
    ready = [ah, bh, kh, rh, de]

    o = oT1
    names = {}

    def buf(name, n=512):
        nonlocal o
        names[name] = A[:, o:o + n]
        o += n
        return names[name]

    bA, bAT, bO, bPT, bNT, bQT, bC, bD, bP, bQ, bE, bET = [buf(x).rearrange("p (a t) -> p a t", a=4) for x in
                                                             "A AT O PT NT QT C D P Q E ET".split()]
    BT, KT, VT = [buf(x).rearrange("p (a t) -> p a t", a=4) for x in ("BT", "KT", "VT")]
    U = [buf(f"U{i}", 1024).rearrange("p (a b c d) -> p a b c d", a=4, b=2, c=2) for i in range(2)]
    FT, HT, GT, Y0 = [buf(x).rearrange("p (a t) -> p a t", a=4) for x in ("FT", "HT", "GT", "Y0")]
    SB = [buf(f"SB{i}").rearrange("p (a t) -> p a t", a=4) for i in range(2)]
    assert o <= oGL
    p.all_wait()

    def bc(ap, n):
        return ap.unsqueeze(1).broadcast_to([ap.shape[0], 4, n])

    st = p.zero(G, SB[0])
    cur = 0
    s_read = [None, None]
    last_mm = None
    for j, (t0, n) in enumerate(TILES):
        tk = slice(t0, t0 + n)
        pf = P.last()

        def group4(pairs, *toks):
            b, fr = ps.take(1)
            t = None
            for q in range(4):
                lst = pairs(q)
                for i, (lh, rh_) in enumerate(lst):
                    w_ = rh_.shape[-1] if len(rh_.shape) == 2 else rh_.shape[-1] * rh_.shape[-2]
                    t = p.mm(p.PSUM[0:lh.shape[-1], b, q * 128:q * 128 + w_], lh, rh_, i == 0, i == len(lst) - 1,
                             fr, *toks, mark=(q == 3 and i == len(lst) - 1))
            return b, t

        def view(b, m=n, w=n):
            return p.PSUM[0:m, b, :].rearrange("p (a t) -> p a t", a=4)[:, :, 0:w]

        tmt = []
        for src, kind in ((BH, 0), (Kf, 1), (Vf, 2), (AH, 3)):
            b, fr = ps.take(1)
            for q in range(4):
                t = p.tr(p.PSUM[0:n, b, q * 128:q * 128 + 128], src[:, q, tk], 128, fr, ready, tv_, mark=(q == 3))
            if kind < 3:
                t = p.copy(S, (BT, KT, VT)[kind][0:n], view(b, n, 128), t, last_mm)
            else:
                for g in range(2):
                    t = p.copy(V, U[0][0:n, :, 0, g, :], view(b, n, 128)[:, :, 64 * g:64 * g + 64], t, last_mm)
            ps.give(b, 1, t)
            tmt.append(t)
        gt_last = None
        for g in range(2):
            lo = 64 * g
            fm = lambda X, q: X[lo:lo + 64, q, tk]
            pr = P.last()
            b, t = group4(lambda q: [(fm(AH, q), fm(BH, q))], ready)
            tA = p.tt(V, bA[0:n, :, 0:n], view(b), bc(p.c("mA")[0:n, 0:n], n), MUL, t, pr)
            tO = p.tt(V, bO[0:n, :, 0:n], view(b), bc(p.c("mO")[0:n, 0:n], n), MUL, t, pr)
            ps.give(b, 1, tO)
            b, t = group4(lambda q: [(fm(BH, q), fm(AH, q))])
            tAT = p.tt(V, bAT[0:n, :, 0:n], view(b), bc(p.c("mAT")[0:n, 0:n], n), MUL, t)
            ps.give(b, 1, tAT)
            b, t = group4(lambda q: [(fm(Kf, q), fm(AH, q))])
            tNT = p.tt(V, bNT[0:n, :, 0:n], view(b), bc(p.c("mUs")[0:n, 0:n], n), MUL, t)
            ps.give(b, 1, tNT)
            b2, t2 = group4(lambda q: [(bA[0:n, q, 0:n], bAT[0:n, q, 0:n])], tAT)
            b1, t1 = group4(lambda q: [(bAT[0:n, q, 0:n], bA[0:n, q, 0:n])], tAT)
            tP = p.tt(V, bP[0:n, :, 0:n], bAT[0:n, :, 0:n], bc(p.c("id")[0:n, 0:n], n), ADD, tAT)
            tD = p.copy(S, bD[0:n, :, 0:n], view(b2), t2, pr)
            ps.give(b2, 1, tD)
            tC = p.copy(V, bC[0:n, :, 0:n], view(b1), t1)
            ps.give(b1, 1, tC)
            b, t = group4(lambda q: [(bNT[0:n, q, 0:n], VT[0:n, q, lo:lo + 64])], tNT, tmt[2])
            tnv = p.copy(S, U[0][0:n, :, 1, g, :], view(b, n, 64), t, last_mm)
            ps.give(b, 1, tnv)
            b3, t3 = group4(lambda q: [(bC[0:n, q, 0:n], bP[0:n, q, 0:n])], tC, tP)
            b2, t2 = group4(lambda q: [(bD[0:n, q, 0:n], bC[0:n, q, 0:n])], tD)
            b1, t1 = group4(lambda q: [(bC[0:n, q, 0:n], bD[0:n, q, 0:n])])
            tQ = p.tt(V, bQ[0:n, :, 0:n], view(b3), bP[0:n, :, 0:n], ADD, t3, tP)
            ps.give(b3, 1, tQ)
            tA4 = p.copy(V, bA[0:n, :, 0:n], view(b2), t2)
            ps.give(b2, 1, tA4)
            tAT4 = p.copy(S, bAT[0:n, :, 0:n], view(b1), t1, tP)
            ps.give(b1, 1, tAT4)
            b, t = group4(lambda q: [(fm(BH, q), fm(Rf, q))])
            tPT = p.tt(V, bPT[0:n, :, 0:n], view(b), bc(p.c("mUi")[0:n, 0:n], n), MUL, t)
            ps.give(b, 1, tPT)
            b, t = group4(lambda q: [(fm(Kf, q), fm(Rf, q))])
            tQT = p.tt(V, bQT[0:n, :, 0:n], view(b), bc(p.c("mUi")[0:n, 0:n], n), MUL, t)
            ps.give(b, 1, tQT)
            b3, t3 = group4(lambda q: [(bA[0:n, q, 0:n], bQ[0:n, q, 0:n])], tA4, tQ)
            b2, t2 = group4(lambda q: [(bAT[0:n, q, 0:n], bA[0:n, q, 0:n])], tAT4)
            tP = p.tt(V, bP[0:n, :, 0:n], view(b3), bQ[0:n, :, 0:n], ADD, t3, tQ)
            ps.give(b3, 1, tP)
            tC = p.copy(S, bC[0:n, :, 0:n], view(b2), t2)
            ps.give(b2, 1, tC)
            b3, t3 = group4(lambda q: [(bC[0:n, q, 0:n], bP[0:n, q, 0:n])], tC, tP)
            tQ = p.tt(V, bQ[0:n, :, 0:n], view(b3), bP[0:n, :, 0:n], ADD, t3, tP)
            ps.give(b3, 1, tQ)
            b1, t1 = group4(lambda q: [(bO[0:n, q, 0:n], bQ[0:n, q, 0:n])], tQ, tO)
            b2, t2 = group4(lambda q: [(bQ[0:n, q, 0:n], bO[0:n, q, 0:n])])
            tET = p.copy(V, bET[0:n, :, 0:n], view(b1), t1)
            ps.give(b1, 1, tET)
            tE = p.copy(S, bE[0:n, :, 0:n], view(b2), t2, pr)
            ps.give(b2, 1, tE)
            rhs = lambda i: (lambda q: U[i][0:n, q, :, g, :])
            b3, t3 = group4(lambda q: [(bQ[0:n, q, 0:n], rhs(0)(q))], tnv, tmt[3])
            uv = lambda b: p.PSUM[0:n, b, :].rearrange("p (a b d) -> p a b d", a=4, b=2)
            us = lambda i: U[i][0:n, :, :, g, :]
            tR = p.copy(S, us(1), uv(b3), t3, last_mm)
            ps.give(b3, 1, tR)
            b2, t2 = group4(lambda q: [(bE[0:n, q, 0:n], bET[0:n, q, 0:n])], tE, tET)
            tD = p.copy(V, bD[0:n, :, 0:n], view(b2), t2)
            ps.give(b2, 1, tD)
            b3, t3 = group4(lambda q: [(bD[0:n, q, 0:n], rhs(1)(q))], tD, tR)
            tR2 = p.tt(V, us(0), uv(b3), us(1), ADD, t3, tR)
            ps.give(b3, 1, tR2)
            b3, t3 = group4(lambda q: [(bET[0:n, q, 0:n], rhs(0)(q))], tR2)
            tR3 = p.tt(V, us(1), uv(b3), us(0), ADD, t3, tR2)
            ps.give(b3, 1, tR3)
            b, fr = ps.take(1)
            for q in range(4):
                t = p.mm(p.PSUM[lo:lo + 64, b, q * 128:q * 128 + n], U[1][0:n, q, 0, g, :], bPT[0:n, q, 0:n],
                         True, True, fr, tR3, tPT, mark=True)
            pvw = p.PSUM[lo:lo + 64, b, :].rearrange("p (a t) -> p a t", a=4)[:, :, 0:n]
            tG = p.tt(V, GT[lo:lo + 64, :, 0:n], pvw, Rf[lo:lo + 64, :, tk], ADD, t, last_mm)
            ps.give(b, 1, tG)
            b, fr = ps.take(1)
            for q in range(4):
                p.mm(p.PSUM[lo:lo + 64, b, q * 128:q * 128 + n], U[1][0:n, q, 1, g, :], bPT[0:n, q, 0:n], True, False, fr)
                t = p.mm(p.PSUM[lo:lo + 64, b, q * 128:q * 128 + n], VT[0:n, q, lo:lo + 64], bQT[0:n, q, 0:n],
                         False, True, tQT, mark=True)
            pvw = p.PSUM[lo:lo + 64, b, :].rearrange("p (a t) -> p a t", a=4)[:, :, 0:n]
            tY = p.copy(S, Y0[lo:lo + 64, :, 0:n], pvw, t, last_mm, V.last())
            ps.give(b, 1, tY)
            gt_last = [gt_last, tG, tY, tR3]
        for ci in range(max(1, n // 64)):
            w = min(n, 64)
            r0 = 64 * ci
            cidx = 0 if j == 0 else 2 * j - 1 + ci
            rows = slice(r0, r0 + w)
            b, fr = ps.take(1)
            for q in range(4):
                t = p.mm(p.PSUM[:, b, q * 128:q * 128 + 128], U[1][rows, q, 0, :, :].rearrange("p g d -> p (g d)"),
                         BT[rows, q, :], True, True, fr, gt_last, tmt[0], mark=(q == 3))
            vb = p.PSUM[:, b, :].rearrange("p (a t) -> p a t", a=4)
            t = p.tt(V, FT, vb, bc(p.c("blk"), 128), MUL, t, last_mm)
            ps.give(b, 1, t)
            tF = p.tt(V, FT, FT, bc(p.c("id"), 128), ADD, t)
            b, fr = ps.take(1)
            for q in range(4):
                p.mm(p.PSUM[:, b, q * 128:q * 128 + 128], BT[rows, q, :], U[1][rows, q, 1, :, :].rearrange("p g d -> p (g d)"),
                     True, False, fr)
                t = p.mm(p.PSUM[:, b, q * 128:q * 128 + 128], KT[rows, q, :], VT[rows, q, :], False, True, tmt[1], tmt[2], mark=(q == 3))
            vb = p.PSUM[:, b, :].rearrange("p (a t) -> p a t", a=4)
            tH = p.tt(V, HT, vb, bc(p.c("blk"), 128), MUL, t)
            ps.give(b, 1, tH)
            b, fr = ps.take(1)
            for q in range(4):
                t = p.mm(p.PSUM[:, b, q * 128:q * 128 + w], SB[cur][:, q, :], GT[:, q, rows], True, True, fr, st, mark=(q == 3))
            vb = p.PSUM[:, b, :].rearrange("p (a t) -> p a t", a=4)[:, :, 0:w]
            ty = p.tt(V, AH[:, :, t0 + r0:t0 + r0 + w], vb, Y0[:, :, rows], ADD, t)
            ps.give(b, 1, ty)
            b, fr = ps.take(1)
            for q in range(4):
                t = p.mm(p.PSUM[:, b, q * 128:q * 128 + 128], FT[:, q, :], SB[cur][:, q, :], True, True, fr, tF, mark=(q == 3))
            vb = p.PSUM[:, b, :].rearrange("p (a t) -> p a t", a=4)
            nx = 1 - cur
            t1 = p.tt(V, SB[nx], vb, HT, ADD, t, tH)
            ps.give(b, 1, t1)
            dcol = DE[:, :, cidx:cidx + 1].broadcast_to([128, 4, 128])
            st = p.tt(V, SB[nx], SB[nx], dcol, MUL, t1)
            cur = nx
            last_mm = [P.last(), V.last()]
    p.all_wait()
    Yf = AH
    p1 = []
    for n in range(4):
        b, t = p.colsum(p.c("blk"), [Yf[:, n]], T, [None])
        t = p.stt(p.tv(T1[:, n], T), p.pv(b, T), -1.0 / 64, p.tv(Yf[:, n], T), MUL, ADD, t)
        ps.give(b, 2, t)
        p1.append(t)
    sq = [p.act(T2[:, n], T1[:, n], ACT.Square, p1[n]) for n in range(4)]
    rr = []
    for n in range(4):
        b, t = p.colsum(p.c("blk"), [T2[:, n]], T, [sq[n]])
        t = p.ts(V, p.tv(T3[:, n], T), p.pv(b, T), 1.0 / 64, MUL, 64e-5, ADD, t)
        ps.give(b, 2, t)
        rr.append(t)
    t = p.act(fT3, fT3, ACT.Sqrt, rr[-1])
    t = p.recip(fT3, fT3, t)
    yn = p.tt(V, fT1, fT1, fT3, MUL, t)
    outs = []
    for n in range(4):
        b, fr = ps.take(2)
        for hi, (a, ln) in enumerate(HALVES[T]):
            t = p.mm(p.PSUM[:, b + hi, 0:ln], gw[:, 0, n * 128:n * 128 + 128], GL[:, a:a + ln], True, True, fr, gs, mark=True)
        u = p.ts(V, T1[:, n], T1[:, n], p.col("rw_lnx_w", n, l), MUL, p.col("rw_lnx_b", n, l), ADD, yn)
        u = p.tt(V, T1[:, n], T1[:, n], BV[:, n], ADD, u)
        u = p.tt(V, p.tv(Rf[:, n], T), p.pv(b, T), p.tv(T1[:, n], T), MUL, u, t)
        ps.give(b, 2, u)
        outs.append(u)
    p.used(slot, P.last())
    return Rf, outs[-1]


def attention(p, l, hx, htok):
    V, S, G, P, ps = p.V, p.S, p.G, p.P, p.ps
    A = p.arena
    o = 2112

    def buf(n):
        nonlocal o
        o += n
        return A[:, o - n:o]

    BD = buf(2112).rearrange("p (a t) -> p a t", a=4)
    Qf = buf(2112).rearrange("p (a t) -> p a t", a=4)
    Kf = buf(2112).rearrange("p (a t) -> p a t", a=4)
    VT = buf(2560).rearrange("p (a t) -> p a t", a=5)
    raw = [buf(T) for _ in range(2)]
    rt = [buf(T) for _ in range(2)]
    EE = [buf(1056) for _ in range(2)]
    AB = [buf(T) for _ in range(2)]
    AT = [buf(640).rearrange("p (a t) -> p a t", a=5) for _ in range(2)]
    SC = buf(64)
    lam = p.small[:, 40:41]
    lp = p.small[:, 41:43]
    le = p.small[:, 43:45]
    lc = p.colr("da_lambda", 0, 4, l)
    t = p.tt(V, lp, lc[:, 0:4:2], lc[:, 1:4:2], MUL, V.last())
    b, fr = ps.take(1)
    t = p.mm(p.PSUM[:, b, 0:2], p.c("one"), lp, True, True, fr, t, mark=True)
    t = p.act(le, p.PSUM[:, b, 0:2], ACT.Exp, t)
    ps.give(b, 1, t)
    t = p.tt(V, lam, le[:, 0:1], le[:, 1:2], SUB, t)
    linit = 0.8 - 0.6 * math.exp(-0.3 * l)
    tlam = p.ts(V, lam, lam, linit, ADD, None, None, t)

    rdone = [None, None]
    qk = []
    for m in range(8):
        if m % 2 == 0:
            (w,), wt, slot = p.slab([("w_in", (l,), 0, 8, 512 + m * 128, 256)])
        b, t = p.proj(w, (m % 2) * 128, hx, T, [wt, htok])
        if m % 2 == 1:
            p.used(slot, t)
        i = m % 2
        c1 = p.copy(S, p.tv(raw[i], T), p.pv(b, T), t, rdone[i])
        ps.give(b, 2, c1)
        b, t = p.colsum(p.c("rot"), [raw[i]], T, [c1])
        d = p.tt(V, p.tv(rt[i], T), p.pv(b, T), p.tv(p.c("sin"), T), MUL, t)
        ps.give(b, 2, d)
        dst = (Qf if m < 4 else Kf)[:, m % 4]
        e = p.tt(G, dst, raw[i], p.c("cos"), MUL, c1)
        rdone[i] = p.tt(V, dst, dst, rt[i], ADD, d, e)
        qk.append(rdone[i])
    vt = []
    for half in range(2):
        (w,), wt, slot = p.slab([("w_in", (l,), 0, 8, 1536 + half * 256, 256)])
        for j, (t0, n) in enumerate(TILES):
            b, fr = ps.take(1)
            for k in range(8):
                t = p.mm(p.PSUM[0:n, b, 0:256], hx(k, t0, n), w[:, k, :], k == 0, k == 7, wt, htok, fr, mark=(k == 7))
            c1 = p.copy(S if j % 2 else V, VT[0:n, j, half * 256:half * 256 + 256], p.PSUM[0:n, b, 0:256], t)
            ps.give(b, 1, c1)
            vt.append(c1)
        p.used(slot, t)

    units = [(j, h) for j in range(5) for h in range(4)]
    e_free, a_free, at_free = [None, None], [None, None], [None, None]
    ot = []
    pend = None

    def scores(u):
        j, h = units[u]
        t0, n = TILES[j]
        nk = t0 + n
        nbk = 4 if nk > 512 else 2
        b, fr = ps.take(nbk)
        for c in range(2):
            for s in range(nbk // 2):
                w_ = nk // (nbk // 2)
                t = p.mm(p.PSUM[0:n, b + c * (nbk // 2) + s, 0:w_], Qf[64 * c:64 * c + 64, h, t0:t0 + n],
                         Kf[64 * c:64 * c + 64, h, s * w_:s * w_ + w_], True, True, fr, qk, mark=True)
        return b, nbk, t

    def soft(u, b, nbk, t):
        j, h = units[u]
        t0, n = TILES[j]
        nk = t0 + n
        w_ = nk // (nbk // 2)
        i = u % 2
        sc = SC[:, 16 * i:16 * i + 16]
        if j > 0:
            vw = p.PSUM[0:64, b + nbk // 2 - 1:b + nbk:nbk // 2, w_ - 64:w_]
            m_ = p.c("am")[0:64, :].unsqueeze(1).broadcast_to([64, 2, 64])
            t = p.tt(V, vw, vw, m_, ADD, t)
        sv = p.PSUM[0:n, b:b + nbk, 0:w_]
        t = V.do(lambda e: e.tensor_reduce(sc[0:n, 0:nbk], sv, AX.X, MAX), t)
        if nbk == 4:
            t = p.tt(V, sc[0:n, 4:6], sc[0:n, 0:4:2], sc[0:n, 1:4:2], MAX, t)
            mxv = sc[0:n, 4:6]
        else:
            mxv = sc[0:n, 0:2]
        t = p.ts(V, sc[0:n, 6:8], mxv, -0.125, MUL, None, None, t)
        et = []
        for c in range(2):
            hb = nbk // 2
            src = p.PSUM[0:n, b + c * hb:b + c * hb + hb, 0:w_] if hb == 2 else p.PSUM[0:n, b + c, 0:w_]
            dst = EE[i][0:n, c * T:c * T + nk]
            if hb == 2:
                dst = dst.rearrange("p (a b) -> p a b", a=2)
            et.append(p.act(dst, src, ACT.Exp, t, e_free[i], bias=sc[0:n, 6 + c:7 + c], scale=0.125,
                            accum=sc[0:n, 8 + c:9 + c]))
        ps.give(b, nbk, et[-1])
        t = p.recip(sc[0:n, 10:12], sc[0:n, 8:10], et[-1])
        t = p.tt(V, sc[0:n, 12:13], sc[0:n, 11:12], lam[0:n, :], MUL, t, tlam)
        t = p.ts(V, EE[i][0:n, T:T + nk], EE[i][0:n, T:T + nk], sc[0:n, 12:13], MUL, None, None, t)
        t = p.stt(AB[i][0:n, 0:nk], EE[i][0:n, 0:nk], sc[0:n, 10:11], EE[i][0:n, T:T + nk], MUL, SUB, t, a_free[i])
        e_free[i] = t
        return t

    def pvs(u, t):
        j, h = units[u]
        t0, n = TILES[j]
        i = u % 2
        b, fr = ps.take(2)
        for kt in range(j + 1):
            k0, kn = TILES[kt]
            out = p.PSUM[0:kn, b + 1, 0:n] if kt == 0 else p.PSUM[0:kn, b, (kt - 1) * 128:(kt - 1) * 128 + n]
            tq = p.tr(out, AB[i][0:n, k0:k0 + kn], n, fr, t, mark=(kt == j))
        a_free[i] = tq
        ca = p.copy(S, AT[i][0:16, 0, 0:n], p.PSUM[0:16, b + 1, 0:n], tq, at_free[i])
        if j > 0:
            src = p.PSUM[:, b, 0:128 * j].rearrange("p (a t) -> p a t", a=j)
            ca = [ca, p.copy(S, AT[i][:, 1:j + 1, 0:n], src, tq, at_free[i])]
        ps.give(b, 2, ca)
        b, fr = ps.take(1)
        for kt in range(j + 1):
            kn = TILES[kt][1]
            tq = p.mm(p.PSUM[:, b, 0:n], VT[0:kn, kt, h * 128:h * 128 + 128], AT[i][0:kn, kt, 0:n],
                      kt == 0, kt == j, fr, ca, vt, mark=(kt == j))
        at_free[i] = tq
        c1 = p.copy(S, BD[:, h, t0:t0 + n], p.PSUM[:, b, 0:n], tq)
        ps.give(b, 1, c1)
        ot.append(c1)

    prev = None
    for u in range(len(units)):
        sb_ = scores(u)
        tx = soft(u, *sb_)
        if prev is not None:
            pvs(u - 1, prev)
        prev = tx
    pvs(len(units) - 1, prev)
    outs = []
    tb = ot[-1]
    sq = [p.act(Qf[:, h], BD[:, h], ACT.Square, tb, P.last()) for h in range(4)]
    for h in range(4):
        b, t = p.colsum(p.c("one"), [Qf[:, h]], T, [sq[h]])
        t = p.rstd(Kf[:, h], b, T, 1.0 / 128, 1e-5, t)
        t = p.ts(V, Kf[:, h], Kf[:, h], p.col("da_subln", 0, l), MUL, 1.0 - linit, MUL, t)
        outs.append(p.tt(V, BD[:, h], BD[:, h], Kf[:, h], MUL, t))
    return BD, outs[-1]


def pool(p, l, hx, htok):
    V, S, G, P, ps = p.V, p.S, p.G, p.P, p.ps
    A = p.arena
    BP = A[:, 4224:6336].rearrange("p (a t) -> p a t", a=4)
    o = 6336
    UU = [A[:, o + 544 * i:o + 544 * i + 544] for i in range(4)]
    o += 544 * 4
    W = [A[:, o + 544 * i:o + 544 * i + 544] for i in range(8)]
    p.all_wait()
    z = [p.zero(V, x[:, 0:16]) for x in UU + W][-1]
    (pw,), pwt, pslot = p.slab([("pool_w", (l,), 0, 4, 0, 128)])
    outs = []
    for g in range(4):
        if g % 2 == 0:
            (w,), wt, slot = p.slab([("w_in", (l,), 0, 8, g * 128, 256)])
        b, t = p.proj(w, (g % 2) * 128, hx, T, [wt, htok])
        if g % 2 == 1:
            p.used(slot, t)
        u = UU[g]
        c1 = p.copy(S, p.tv(u[:, 16:544], T), p.pv(b, T), t)
        ps.give(b, 2, c1)
        src, t = u, c1
        E = V
        for s in range(g + 1):
            d = W[2 * g + s % 2]
            sh = 1 << s
            t = p.tt(E, d[:, 16:544], src[:, 16:544], src[:, 16 - sh:544 - sh], ADD, t, z)
            src = d
        sm = src
        dst = W[2 * g + (g + 1) % 2]
        hd = p.tt(V, sm[:, 0:16], sm[:, 16:32], p.c("ic")[:, 16 * g:16 * g + 16], MUL, t)
        t = p.stt(dst[:, 16:544], sm[:, 16:544], 1.0 / (2 << g), u[:, 16:544], MUL, SUB, t, hd)
        t = p.tt(V, dst[:, 16:32], sm[:, 0:16], u[:, 16:32], SUB, t)
        b, fr = ps.take(2)
        for hi, (a, ln) in enumerate(HALVES[T]):
            t2 = p.mm(p.PSUM[:, b + hi, 0:ln], pw[:, g, :], dst[:, 16 + a:16 + a + ln], True, True, fr, t, pwt, mark=True)
        t = p.act(p.tv(BP[:, g], T), p.pv(b, T), ACT.Copy, t2, scale=p.col("pool_scale", g, l))
        ps.give(b, 2, t)
        outs.append(t)
    p.used(pslot, t2)
    return BP, outs[-1]


def first_layer(p, l, X, H, xtok):
    V, S, G, P, ps = p.V, p.S, p.G, p.P, p.ps
    A = p.arena
    rs = p.small[:, 64:64 + T]
    ht = p.rms(lambda k: X[:, k], lambda k: H[:, k], T, "norm_mix", l, xtok, rs)
    hx = lambda k, a, n: H[:, k, a:a + n]
    br, brt = rwkv(p, l, hx, ht[-1])
    p.dump(f"rw{l}", br, [brt])
    p.all_wait()
    bd, bdt = attention(p, l, hx, ht[-1])
    p.dump(f"da{l}", bd, [bdt])
    bp, bpt = pool(p, l, hx, ht[-1])
    p.dump(f"bp{l}", bp, [bpt])
    o = 6336
    MG = A[:, o:o + 4224].rearrange("p (a t) -> p a t", a=8)
    o += 4224
    SG = [A[:, o + T * i:o + T * i + T] for i in range(2)]
    TM = [A[:, o + T * (2 + i):o + T * (2 + i) + T] for i in range(2)]
    p.all_wait()
    brs = (bp, bd, br)
    sfree, tfree = [None, None], [None, None]
    mt = []
    it = 0
    for m in range(8):
        for n in range(3):
            (gw, uw), wt, slot = p.slab([("w_in", (l,), 0, 8, 3840 + n * 1024 + m * 128, 128),
                                         ("w_branch", (l, n), 0, 4, m * 128, 128)])
            b1, t1 = p.proj(gw, 0, hx, T, [wt])
            b2, t2 = p.proj(uw, 0, lambda k, a, ln: brs[n][:, k, a:a + ln], T, [brt, bdt, bpt])
            p.used(slot, t2)
            i = it % 2
            it += 1
            s_ = p.act(p.tv(SG[i], T), p.pv(b1, T), ACT.Sigmoid, t1, sfree[i])
            ps.give(b1, 2, s_)
            if n == 0:
                d = p.tt(V, p.tv(MG[:, m], T), p.pv(b2, T), p.tv(SG[i], T), MUL, s_, t2)
                ps.give(b2, 2, d)
                last = d
            else:
                d = p.tt(V, p.tv(TM[i], T), p.pv(b2, T), p.tv(SG[i], T), MUL, s_, t2, tfree[i])
                ps.give(b2, 2, d)
                last = p.tt(G, MG[:, m], MG[:, m], TM[i], ADD, d, last)
                tfree[i] = last
            sfree[i] = d
        mt.append(last)
    xt = []
    for m in range(8):
        if m % 2 == 0:
            (w,), wt, slot = p.slab([("w_out", (l,), 0, 8, m * 128, 256)])
        b, t = p.proj(w, (m % 2) * 128, lambda k, a, ln: MG[:, k, a:a + ln], T, [wt, mt])
        if m % 2 == 1:
            p.used(slot, t)
        x_ = p.tt(V, p.tv(X[:, m], T), p.pv(b, T), p.tv(X[:, m], T), ADD, t)
        ps.give(b, 2, x_)
        xt.append(x_)
    p.dump(f"x{l}m", X, xt)
    p.all_wait()
    ht = p.rms(lambda k: X[:, k], lambda k: H[:, k], T, "norm_ffn", l, xt, rs)
    HF = A[:, 0:NFF * T].rearrange("p (a t) -> p a t", a=NFF)
    o = NFF * T
    RW = [[A[:, o + 530 * (2 * i + s):o + 530 * (2 * i + s) + 530] for s in range(2)] for i in range(2)]
    o += 4 * 530
    CV = [[A[:, o + T * (2 * i + s):o + T * (2 * i + s) + T] for s in range(2)] for i in range(2)]
    z = [p.zero(V, RW[i][s][:, 0:2]) for i in range(2) for s in range(2)][-1]
    rfree = [[None, None], [None, None]]
    cfree = [None, None]
    hf = []
    for f in range(NFF):
        (gw, uw), wt, slot = p.slab([("ffn_up", (l,), 0, 8, f * 128, 128), ("ffn_up", (l,), 0, 8, 2816 + f * 128, 128)])
        i = f % 2
        cc = []
        for s, w in enumerate((gw, uw)):
            b, t = p.proj(w, 0, hx, T, [wt, ht[-1]])
            r, cv = RW[i][s], CV[i][s]
            c1 = p.copy(S, p.tv(r[:, 2:530], T), p.pv(b, T), t, rfree[i][s], z)
            ps.give(b, 2, c1)
            tap = lambda q: p.col("ffn_conv", q * 44 + s * 22 + f, l)
            t3 = p.ts(V, cv, r[:, 2:530], tap(2), MUL, None, None, c1, cfree[i])
            t3 = p.stt(cv, r[:, 1:529], tap(1), cv, MUL, ADD, t3)
            t3 = p.stt(cv, r[:, 0:528], tap(0), cv, MUL, ADD, t3)
            rfree[i][s] = t3
            cc.append(t3)
        p.used(slot, t)
        s_ = p.act(CV[i][0], CV[i][0], ACT.Silu, cc[0])
        cfree[i] = p.tt(G, HF[:, f], CV[i][0], CV[i][1], MUL, s_, cc[1])
        hf.append(cfree[i])
    xt = []
    for m in range(8):
        b, fr = ps.take(2)
        for part in range(2):
            (w,), wt, slot = p.slab([("ffn_down", (l,), 11 * part, 11, m * 128, 128)])
            _, t = p.proj(w, 0, lambda k, a, ln: HF[:, 11 * part + k, a:a + ln], T, [wt, hf], b, fr,
                          first=part == 0, last=part == 1)
            p.used(slot, t)
        x_ = p.tt(V, p.tv(X[:, m], T), p.pv(b, T), p.tv(X[:, m], T), ADD, t)
        ps.give(b, 2, x_)
        xt.append(x_)
    p.all_wait()
    p.dump(f"x{l}", X, xt)
    return xt




def ada(p, MOD):
    V, S, P, ps = p.V, p.S, p.P, p.ps
    CD = p.small[:, 600:608]
    t0 = p.act(CD, p.colr("c_2", 0, 8), ACT.Silu)
    out = None
    for s in range(24):
        (w,), wt, slot = p.slab([("ada_w_2", (0,), 0, 8, 256 * s, 256)])
        b, fr = ps.take(1)
        for i in range(2):
            for k in range(8):
                t = p.mm(p.PSUM[:, b, i:i + 1], w[:, k, i * 128:i * 128 + 128], CD[:, k:k + 1], k == 0, k == 7,
                         wt, fr, t0, mark=(k == 7))
        p.used(slot, t)
        out = p.tt(V, MOD[:, 2 * s:2 * s + 2], p.PSUM[:, b, 0:2], p.colr("ada_b_2", 2 * s, 2 * s + 2), ADD, t)
        ps.give(b, 1, out)
    for o in (8, 32):
        out = p.ts(V, MOD[:, o:o + 8], MOD[:, o:o + 8], 1.0, ADD, None, None, out)
    return out


def mixer2(p, XX, UU, xtok, MOD, mtok):
    V, S, G, P, ps = p.V, p.S, p.G, p.P, p.ps
    A = p.arena
    o = 0

    def buf(n):
        nonlocal o
        o += n
        return A[:, o - n:o]

    def f4(n=512):
        return buf(4 * n).rearrange("p (a t) -> p a t", a=4)

    QF, SF, KF, IF, OG, BB = [f4() for _ in range(6)]
    CVI = f4(542)
    CVO = f4()
    OO = f4()
    QL, KL = f4(), f4()
    WK = [buf(512) for _ in range(4)]
    RS = buf(512)
    NB = p.small[:, 610:620]
    ut = p.ln(lambda k: XX[:, k], lambda k: UU[:, k], 8, lambda i: WK[i], RS, xtok,
              lambda k: MOD[:, 8 + k:9 + k], lambda k: MOD[:, k:k + 1], 1024)
    LB = p.small[:, 620:640].rearrange("p (a c) -> p a c", a=5)
    lb0 = p.colr("hgrn_lb_2", 0, 4)
    t = p.tt(V, LB[:, 0], lb0, lb0, SUB)
    t = p.act(LB[:, 0], LB[:, 0], ACT.Exp, t)
    t = p.recip(LB[:, 1], LB[:, 0], t)
    t = p.tt(V, LB[:, 2], LB[:, 0], LB[:, 1], MUL, t)
    tlb = p.tt(V, LB[:, 3], LB[:, 2], LB[:, 2], SUB, t)
    t1lb = p.ts(V, LB[:, 4], LB[:, 3], -1.0, MUL, 1.0, ADD, tlb)
    tnb = p.ts(V, NB[:, 0:4], p.colr("b_in_2", 4, 8), -1.0, MUL)
    ux = lambda k, a, n: UU[:, k, a:a + n]
    z = p.zero(V, CVI[:, :, 0:30])
    tk = {}
    for m in list(range(16, 24)) + list(range(16)):
        if m % 2 == 0:
            (w,), wt, slot = p.slab([("w_in_2", (0,), 0, 8, m * 128, 256)])
        b, t = p.proj(w, (m % 2) * 128, ux, 512, [wt, ut])
        if m % 2 == 1:
            p.used(slot, t)
        src = p.PSUM[:, b, 0:512]
        bias = p.col("b_in_2", m)
        q, kind = m % 4, m // 4
        if kind == 0:
            r = p.act(QF[:, q], src, ACT.Silu, t, bias=bias)
        elif kind == 1:
            p.act(SF[:, q], src, ACT.Sigmoid, t, bias=bias)
            r = p.act(KF[:, q], src, ACT.Sigmoid, t, tnb, bias=NB[:, q:q + 1], scale=-1.0)
        elif kind == 2:
            r = p.ts(V, IF[:, q], src, bias, ADD, None, None, t)
        elif kind == 3:
            r = p.act(OG[:, q], src, ACT.Silu, t, bias=bias)
        elif kind == 4:
            r = p.ts(V, CVI[:, q, 30:542], src, bias, ADD, None, None, t, z)
        else:
            s_ = p.act(CVO[:, q], src, ACT.Sigmoid, t, bias=bias)
            r = s_
            cv = p.tt(V, CVI[:, q, 30:542], CVI[:, q, 30:542], CVO[:, q], MUL, s_, tk[(4, q)])
            tk[(6, q)] = cv
        ps.give(b, 1, r)
        tk[(kind, q)] = r
    gb = []
    for q in range(4):
        t = p.ts(V, SF[:, q], SF[:, q], LB[:, 4, q:q + 1], MUL, LB[:, 3, q:q + 1], ADD, tk[(1, q)], t1lb)
        t = p.ts(V, SF[:, q], SF[:, q], 2.0 ** -64, MAX, None, None, t)
        t2 = p.ts(V, KF[:, q], KF[:, q], LB[:, 4, q:q + 1], MUL, None, None, tk[(1, q)])
        t = p.act(SF[:, q], SF[:, q], ACT.Ln, t)
        gb.append(V.do(lambda e, q=q: e.tensor_tensor_scan(BB[:, q], p.c("hrs"), SF[:, q], 0.0, MUL, ADD), t, t2))
    VT = SF
    bf = lambda q, c: BB[:, q, 128 * c:128 * c + 128]
    vt = []
    for c in range(4):
        b, fr = ps.take(1)
        for h in range(4):
            t = p.tr(p.PSUM[:, b, h * 128:h * 128 + 128], IF[:, h, 128 * c:128 * c + 128], 128, fr, tk[(2, 3)], mark=(h == 3))
        t = p.copy(S, VT[:, c, :], p.PSUM[:, b, :], t, gb)
        ps.give(b, 1, t)
        vt.append(t)
    taps = [(q, i) for i in range(31) for q in range(4)]
    ctok = {}

    def conv(n):
        for _ in range(n):
            if not taps:
                return
            q, i = taps.pop(0)
            wcol = p.col("conv_w_2", i * 4 + q)
            src = CVI[:, q, i:i + 512]
            if i == 0:
                ctok[q] = p.ts(V, CVO[:, q], src, wcol, MUL, p.col("conv_b_2", q), ADD, tk[(6, q)])
            else:
                ctok[q] = p.stt(CVO[:, q], src, wcol, CVO[:, q], MUL, ADD, ctok[q])

    ob = [ps.take(1) for _ in range(4)]
    first = [True] * 4
    lfree, kfree = None, None
    wfree = [None] * 4
    wi = 0
    for lev in range(8):
        if lev < 7:
            m = 64 >> lev
            nbk = 512 // (2 * m)
            zq = p.zero(G, QL, lfree)
            zk = p.zero(G, KL, lfree)
            tl = []
            for h in range(4):
                B = BB[:, h].rearrange("p (n m) -> p n m", m=2 * m)
                ref = B[:, :, m - 1:m].broadcast_to([128, nbk, m])
                ql = QL[:, h].rearrange("p (n m) -> p n m", m=2 * m)[:, :, m:]
                kl = KL[:, h].rearrange("p (n m) -> p n m", m=2 * m)[:, :, :m]
                t1 = p.tt(V, ql, B[:, :, m:], ref, SUB, zq, gb)
                t2 = p.tt(V, kl, ref, B[:, :, :m], SUB, zk)
                t1 = p.act(ql, ql, ACT.Exp, t1)
                t2 = p.act(kl, kl, ACT.Exp, t2)
                t1 = p.tt(V, ql, ql, QF[:, h].rearrange("p (n m) -> p n m", m=2 * m)[:, :, m:], MUL, t1, tk[(0, 3)])
                t2 = p.tt(V, kl, kl, KF[:, h].rearrange("p (n m) -> p n m", m=2 * m)[:, :, :m], MUL, t2)
                tl += [t1, t2]
            qs, ks = QL, KL
        else:
            qs, ks, tl = QF, KF, []
        for h in range(4):
            b, fr = ps.take_from(4, 8)
            for c in range(4):
                t = p.mm(p.PSUM[:, b, 128 * c:128 * c + 128], ks[:, h, 128 * c:128 * c + 128], qs[:, h, 128 * c:128 * c + 128],
                         True, True, fr, tl, mark=(c == 3))
            W = WK[wi % 4].rearrange("p (c t) -> p c t", c=4)
            mk = p.c("hm")[:, lev * 128:lev * 128 + 128].unsqueeze(1).broadcast_to([128, 4, 128])
            mt = p.tt(V, W, p.PSUM[:, b, :].rearrange("p (c t) -> p c t", c=4), mk, MUL, t, wfree[wi % 4])
            ps.give(b, 1, mt)
            for c in range(4):
                t2 = p.mm(p.PSUM[:, ob[h][0], 128 * c:128 * c + 128], VT[:, c, h * 128:h * 128 + 128], W[:, c],
                          first[h] and c == 0, False, mt, vt, ob[h][1], mark=(c == 3))
            first[h] = False
            wfree[wi % 4] = t2
            wi += 1
            conv(4)
        lfree = P.last()
    tq = []
    for h in range(4):
        t = p.act(QL[:, h], BB[:, h], ACT.Exp, lfree)
        tq.append(p.tt(V, QL[:, h], QL[:, h], QF[:, h], MUL, t))
    DE = p.small[:, 0:16].rearrange("p (a c) -> p a c", a=4)
    td = p.act(DE, BB[:, :, 127::128], ACT.Exp)
    tke = []
    for h in range(4):
        B = BB[:, h].rearrange("p (n m) -> p n m", m=128)
        k_ = KL[:, h].rearrange("p (n m) -> p n m", m=128)
        t = p.tt(V, k_, B[:, :, 127:128].broadcast_to([128, 4, 128]), B, SUB, lfree)
        t = p.act(k_, k_, ACT.Exp, t)
        tke.append(p.tt(V, KL[:, h], KL[:, h], KF[:, h], MUL, t))
    KT = IF
    kt = []
    for c in range(3):
        b, fr = ps.take_from(4, 8)
        for h in range(4):
            t = p.tr(p.PSUM[:, b, h * 128:h * 128 + 128], KL[:, h, 128 * c:128 * c + 128], 128, fr, tke, mark=(h == 3))
        t = p.copy(S, KT[:, c, :], p.PSUM[:, b, :], t, vt)
        ps.give(b, 1, t)
        kt.append(t)
    ST = [WK[i].rearrange("p (h v) -> p h v", h=4) for i in range(2)]
    st = None
    for c in range(1, 4):
        b, fr = ps.take_from(4, 8)
        for h in range(4):
            t = p.mm(p.PSUM[:, b, h * 128:h * 128 + 128], KT[:, c - 1, h * 128:h * 128 + 128],
                     VT[:, c - 1, h * 128:h * 128 + 128], True, True, fr, kt, mark=(h == 3))
        pvw = p.PSUM[:, b, :].rearrange("p (h v) -> p h v", h=4)
        cur, nxt = ST[(c - 1) % 2], ST[c % 2]
        if c == 1:
            st = p.copy(V, nxt, pvw, t, wfree)
        else:
            d = DE[:, :, c - 1:c].broadcast_to([128, 4, 128])
            x_ = p.tt(V, nxt, cur, d, MUL, st, td, wfree)
            st = p.tt(V, nxt, nxt, pvw, ADD, x_, t)
        ps.give(b, 1, st)
        for h in range(4):
            t2 = p.mm(p.PSUM[:, ob[h][0], 128 * c:128 * c + 128], nxt[:, h], QL[:, h, 128 * c:128 * c + 128],
                      False, c == 3, st, tq, mark=(h == 3))
        wfree = [t2]
    conv(200)
    sq = [p.act(KL[:, h], p.PSUM[:, ob[h][0], 0:512], ACT.Square, t2, kt) for h in range(4)]
    ha = []
    for h in range(4):
        b, fr = ps.take_from(4, 8)
        t = p.mm(p.PSUM[:, b, 0:512], p.c("one"), KL[:, h], True, True, fr, sq[h], mark=True)
        t = p.rstd(BB[:, h], b, 512, 1.0 / 128, 1e-5, t, tke, tq)
        t = p.stt(BB[:, h], BB[:, h], p.col("hgrn_norm_w_2"), OG[:, h], MUL, MUL, t, tk[(3, h)])
        t = p.tt(V, OO[:, h], p.PSUM[:, ob[h][0], 0:512], BB[:, h], MUL, t)
        ha.append(t)
    for h in range(4):
        ps.give(ob[h][0], 1, ha[h], sq[h])
    hb = p.ln(lambda k: CVO[:, k], lambda k: QF[:, k], 4, lambda i: WK[2 + i], RS, [ctok[q] for q in range(4)] ,
              lambda k: p.col("conv_ln_g_2", k), lambda k: p.col("conv_ln_b_2", k), 512, ACT.Silu)
    p.dump("ha", OO, ha)
    p.dump("hb", QF, hb)
    xt = []
    for m in range(8):
        if m % 2 == 0:
            (w,), wt, slot = p.slab([("w_out_2", (0,), 0, 8, m * 128, 256)])
        b, t = p.proj(w, (m % 2) * 128, lambda k, a, n: (OO if k < 4 else QF)[:, k % 4, a:a + n], 512, [wt, ha, hb])
        if m % 2 == 1:
            p.used(slot, t)
        q = p.ts(V, CVI[:, m % 4, 0:512], p.PSUM[:, b, 0:512], p.col("b_out_2", m), ADD, MOD[:, 16 + m:17 + m], MUL, t)
        ps.give(b, 1, q)
        xt.append(p.stt(XX[:, m], XX[:, m], ALPHA, CVI[:, m % 4, 0:512], MUL, ADD, q))
    p.all_wait()
    yt = p.ln(lambda k: XX[:, k], lambda k: UU[:, k], 8, lambda i: WK[i], RS, xt,
              lambda k: p.col("ln1_g_2", k), lambda k: p.col("ln1_b_2", k), 1024)
    p.all_wait()
    return yt


def moe(p, XX, UU, xtok, MOD):
    V, S, G, P, ps = p.V, p.S, p.G, p.P, p.ps
    A = p.arena
    o = 0

    def buf(n):
        nonlocal o
        o += n
        return A[:, o - n:o]

    YY = buf(4096).rearrange("p (a t) -> p a t", a=8)
    HE = [buf(2048).rearrange("p (a t) -> p a t", a=4) for _ in range(2)]
    SI = [buf(512) for _ in range(3)]
    CB = [buf(512) for _ in range(2)]
    CT = buf(512)
    WK = [buf(512) for _ in range(2)]
    RS = buf(512)
    R = [buf(64).rearrange("p (t g e) -> p t g e", t=4, g=4) for _ in range(10)]
    r4 = [buf(16).rearrange("p (t g) -> p t g", t=4) for _ in range(8)]
    r1 = [buf(4).rearrange("p (t g) -> p t g", t=4) for _ in range(4)]
    ut = p.ln(lambda k: XX[:, k], lambda k: UU[:, k], 8, lambda i: WK[i], RS, xtok,
              lambda k: MOD[:, 32 + k:33 + k], lambda k: MOD[:, 24 + k:25 + k], 1024)
    rw = p.colr("router_w_2", 0, 128).rearrange("p (k e) -> p k e", k=8)
    b, fr = ps.take(1)
    for i in range(4):
        for k in range(8):
            t = p.mm(p.PSUM[:, b, 16 * i:16 * i + 16], UU[:, k, 128 * i:128 * i + 128], rw[:, k, :], k == 0, k == 7,
                     fr, ut, mark=(k == 7))
    s, sb, rank, cmpb, inv, sel, cmb = R[0], R[1], R[2], R[3], R[4], R[5], R[6]
    f = lambda x: x.rearrange("p t g e -> p (t g e)")
    t = p.act(f(s), p.PSUM[:, b, 0:64], ACT.Sigmoid, t)
    ps.give(b, 1, t)
    bias = p.colr("router_bias_2", 0, 16).unsqueeze(1).broadcast_to([128, 4, 16])
    t = p.tt(V, sb.rearrange("p t g e -> p t (g e)"), s.rearrange("p t g e -> p t (g e)"), bias, ADD, t)
    G0, tp = r4[0], r4[1]
    pairs = [(i, j) for i in range(4) for j in range(i + 1, 4)]
    for n, (i, j) in enumerate(pairs):
        d = G0 if n == 0 else tp
        t = p.tt(V, d, sb[:, :, :, i], sb[:, :, :, j], ADD, t)
        if n:
            t = p.tt(V, G0, G0, tp, MAX, t)
    gm = r1[0]
    t = V.do(lambda e: e.tensor_reduce(gm[:, :, 0], G0, AX.X, MAX), t)
    gs, left = r4[2], r1[1]
    t = p.tt(V, gs, G0, gm.broadcast_to([128, 4, 4]), ALU.is_ge, t)
    t = p.ts(V, left, gs[:, :, 0:1], -1.0, MUL, 1.0, ADD, t)
    for g in range(1, 4):
        t = p.tt(V, gs[:, :, g:g + 1], gs[:, :, g:g + 1], left, MUL, t)
        if g < 3:
            t = p.tt(V, left, left, gs[:, :, g:g + 1], SUB, t)
    t = p.zero(V, f(rank), t)
    for i, j in pairs:
        c1, c2 = r4[3], r4[4]
        t = p.tt(V, c1, sb[:, :, :, j], sb[:, :, :, i], ALU.is_gt, t)
        t = p.tt(V, rank[:, :, :, i], rank[:, :, :, i], c1, ADD, t)
        t = p.ts(V, c2, c1, -1.0, MUL, 1.0, ADD, t)
        t = p.tt(V, rank[:, :, :, j], rank[:, :, :, j], c2, ADD, t)
    t = p.ts(V, f(sel), f(rank), 1.5, ALU.is_lt, None, None, t)
    t = p.tt(V, sel, sel, gs.unsqueeze(3).broadcast_to([128, 4, 4, 4]), MUL, t)
    t = p.tt(V, f(cmb), f(sel), f(s), MUL, t)
    sm = r1[2]
    t = V.do(lambda e: e.tensor_reduce(sm[:, :, 0], cmb.rearrange("p t g e -> p t (g e)"), AX.X, ADD), t)
    t = p.recip(r1[3], sm, t)
    c3 = cmb.rearrange("p t g e -> p t (g e)")
    t = p.tt(V, c3, c3, r1[3].broadcast_to([128, 4, 16]), MUL, t)
    b, fr = ps.take(1)
    for i in range(4):
        t2 = p.tr(p.PSUM[0:16, b, 128 * i:128 * i + 128], c3[:, i, :], 128, fr, t, mark=(i == 3))
    tct = p.copy(S, CT[0:16, :], p.PSUM[0:16, b, :], t2)
    ps.give(b, 1, tct)
    p.dump("comb", CT, [tct])

    ux = lambda k, a, n: UU[:, k, a:a + n]
    hfree, cfree, sfree = [None, None], [None, None], [None] * 3
    yt = [None] * 8
    si = 0

    def down(e, htoks):
        i = e % 2
        for half in range(2):
            (w,), wt, slot = p.slab([("w_down_2", (0, e), 0, 4, 512 * half, 512)])
            for m4 in range(4):
                m = 4 * half + m4
                b, t = p.proj(w, 128 * m4, lambda k, a, n: HE[i][:, k, a:a + n], 512, [wt, htoks])
                if e == 0:
                    yt[m] = p.copy(V, YY[:, m], p.PSUM[:, b, 0:512], t)
                else:
                    yt[m] = p.tt(V, YY[:, m], p.PSUM[:, b, 0:512], YY[:, m], ADD, t, yt[m])
                ps.give(b, 1, yt[m])
            p.used(slot, t)
        hfree[i] = t

    prev = None
    for e in range(16):
        i = e % 2
        b, fr = ps.take(1)
        selr = p.c("id")[0:16, e:e + 1].broadcast_to([16, 128])
        t = p.mm(p.PSUM[:, b, 0:512], selr, CT[0:16, :], True, True, fr, tct, mark=True)
        tc = p.copy(S, CB[i], p.PSUM[:, b, 0:512], t, cfree[i])
        ps.give(b, 1, tc)
        ht = []
        for q in range(4):
            (gw, uw), wt, slot = p.slab([("w_gate_2", (0, e), 0, 8, q * 128, 128), ("w_up_2", (0, e), 0, 8, q * 128, 128)])
            b1, t1 = p.proj(gw, 0, ux, 512, [wt, ut])
            b2, t2 = p.proj(uw, 0, ux, 512, [])
            p.used(slot, t2)
            sbf = SI[si % 3]
            a1 = p.act(sbf, p.PSUM[:, b1, 0:512], ACT.Silu, t1, sfree[si % 3])
            ps.give(b1, 1, a1)
            a2 = p.tt(G, sbf, sbf, CB[i], MUL, a1, tc)
            h_ = p.tt(V, HE[i][:, q], p.PSUM[:, b2, 0:512], sbf, MUL, a2, t2, hfree[i])
            ps.give(b2, 1, h_)
            sfree[si % 3] = h_
            si += 1
            ht.append(h_)
        cfree[i] = a2
        if prev is not None:
            down(*prev)
        prev = (e, ht)
    down(*prev)
    xt = []
    for m in range(8):
        t = p.ts(V, YY[:, m], YY[:, m], MOD[:, 40 + m:41 + m], MUL, None, None, yt[m])
        xt.append(p.stt(YY[:, m], XX[:, m], ALPHA, YY[:, m], MUL, ADD, t))
    p.all_wait()
    ot = p.ln(lambda k: YY[:, k], lambda k: UU[:, k], 8, lambda i: WK[i], RS, xt,
              lambda k: p.col("ln2_g_2", k), lambda k: p.col("ln2_b_2", k), 1024)
    return ot


def build(nc, xin, cols, cst, outp, dumps=()):
    p = Program()
    ctx = ExitStack()
    with ctx:
        p.cat, nk = const_plan()
        p.cols_at, ncol = col_plan()
        sbt = lambda name, n: ctx.enter_context(nc.sbuf_tensor(name, [128, n], F32))
        Xs, Hs = sbt("X", 8 * T), sbt("H", 8 * T)
        X = Xs[:, :].rearrange("p (k t) -> p k t", k=8)
        H = Hs[:, :].rearrange("p (k t) -> p k t", k=8)
        p.COLS = sbt("COLS", ncol)[:, :]
        p.K = sbt("CST", nk)[:, :]
        p.ring = sbt("RING", NRING * SLAB)[:, :].rearrange("p (s n) -> p s n", s=NRING)
        MOD = sbt("MOD", 48)[:, :]
        p.small = sbt("SMALL", 700)[:, :]
        p.arena = sbt("ARENA", 26500)[:, :]
        p.PSUM = ctx.enter_context(nc.psum_tensor("PS", [128, 8, 512], F32))[:, :, :]

        def take_from(a, z):
            for _ in range(8):
                p.ps.at = p.ps.at % 8
                if a <= p.ps.at < z and not p.ps.busy[p.ps.at]:
                    return p.ps.take(1)
                p.ps.at += 1
            raise AssertionError("no bank")

        p.ps.take_from = take_from
        names = ["pe", "dve", "act", "pool", "sp", "in", "out"] + [f"w{i}" for i in range(NRING)]
        p.sems = {n: ctx.enter_context(nc.semaphore("s_" + n)) for n in names}
        ndump = [0]

        def dump(name, ap, toks):
            if name in dumps:
                d = dumps[name]
                p.D.need(toks)
                p.D.items.append((lambda e: e.dma_start(d, ap).then_inc(p.sems["out"], 16), False, None))
                ndump[0] += 1

        p.dump = dump
        for dst, src in ((Xs[:, :], xin), (p.COLS, cols), (p.K, cst)):
            p.D.items.append((lambda e, dst=dst, src=src: e.dma_start(dst, src).then_inc(p.sems["in"], 16), False, None))
        ready = ("in", 48)
        for q in (p.P, p.V, p.S, p.G):
            q.need(ready)
        z = p.zero(p.V, p.arena)
        z = p.zero(p.V, p.small)
        p.all_wait()
        mt = ada(p, MOD)
        p.all_wait()
        xt = [ready] * 8
        for l in range(2):
            xt = first_layer(p, l, X, H, xt)
        rs = p.small[:, 64:64 + 512]
        XX = Hs[:, 0:4096].rearrange("p (k t) -> p k t", k=8)
        UU = Xs[:, 0:4096].rearrange("p (k t) -> p k t", k=8)
        xt = p.rms(lambda k: X[:, k, 16:528], lambda k: XX[:, k], 512, "norm_final", None, xt, rs)
        p.dump("mid", XX, xt)
        p.all_wait()
        yt = mixer2(p, XX, UU, xt, MOD, mt)
        p.dump("mx", UU, yt)
        ot = moe(p, UU, XX, yt, MOD)
        p.D.need(ot)
        p.D.items.append((lambda e: e.dma_start(outp, Hs[:, 0:4096]).then_inc(p.sems["out"], 16), False, None))
        p.D.items.append((None, "out", 16 * (1 + ndump[0])))
        p.wts = nc.dram_tensor("wts", [p.slab_end], F32, kind="ExternalInput").ap()

        block = ctx.enter_context(nc.Block())

        def emit(q):
            def body(eng):
                for fn, a, b in q.items:
                    if fn is None:
                        eng.wait_ge(p.sems[a], b)
                    else:
                        ins = fn(eng)
                        if a:
                            ins.then_inc(p.sems[q.name], 1)
            return body

        block.sync(emit(p.D))
        block.tensor(emit(p.P))
        block.vector(emit(p.V))
        block.scalar(emit(p.S))
        block.gpsimd(emit(p.G))
    return p.slabs


def pack_cols(inp):
    at, n = col_plan()
    c = np.zeros((128, n), np.float32)

    def put(key, a):
        a = np.reshape(a, (-1, 128))
        c[:, at[key]:at[key] + a.shape[0]] = a.T

    for l in range(2):
        for name in ("norm_mix", "norm_ffn", "pool_scale", "da_subln", "rw_mu", "rw_w0", "rw_a0", "rw_k_k",
                     "rw_k_a", "rw_r_k", "rw_lnx_w", "rw_lnx_b", "ffn_conv"):
            put((name, l), inp[name][l])
        o = at[("da_lambda", l)]
        c[0:64, o:o + 4] = inp["da_lambda"][l].T
    for name in ("norm_final", "c_2", "ada_b_2", "b_in_2", "hgrn_lb_2", "hgrn_norm_w_2", "conv_w_2", "conv_b_2",
                 "conv_ln_g_2", "conv_ln_b_2", "b_out_2", "ln1_g_2", "ln1_b_2", "ln2_g_2", "ln2_b_2"):
        put(name, inp[name])
    o = at["router_bias_2"]
    c[:, o:o + 16] = inp["router_bias_2"][None, :]
    o = at["router_w_2"]
    c[:, o:o + 128] = inp["router_w_2"].reshape(8, 128, 16).transpose(1, 0, 2).reshape(128, 128)
    return c


def pack_weights(slabs, inp):
    parts = []
    for pieces in slabs:
        cut = []
        for name, idx, k0, nk, c0, ncol in pieces:
            if name == "wa2":
                a = np.concatenate([inp["rw_w2"][idx[0]], inp["rw_a2"][idx[0]]], axis=0)
            elif name == "pool_w":
                a = inp["pool_w"][idx[0]].reshape(512, 128)
            else:
                a = inp[name]
                for i in idx:
                    a = a[i]
            a = a[k0 * 128:(k0 + nk) * 128, c0:c0 + ncol]
            cut.append(a.reshape(nk, 128, ncol).transpose(1, 0, 2).reshape(128, nk * ncol))
        parts.append(np.concatenate(cut, axis=1).reshape(-1))
    return np.concatenate(parts)


def kernel(**inputs):
    import concourse.bacc as _bacc
    from concourse.bass_utils import run_bass_kernel_spmd as _run

    inp = {k: np.asarray(v) for k, v in inputs.items()}
    nc = _bacc.Bacc("TRN2", target_bir_lowering=False, num_devices=1)
    cols, cst = pack_cols(inp), consts()
    x = np.concatenate([inp["meta_tokens"], inp["x"][0]], axis=0)
    x = np.ascontiguousarray(x.T.reshape(8, 128, T).transpose(1, 0, 2).reshape(128, 8 * T))
    dr = lambda name, shape, kind: nc.dram_tensor(name, shape, F32, kind=kind).ap()
    xin = dr("xin", x.shape, "ExternalInput")
    cin = dr("cols", cols.shape, "ExternalInput")
    kin = dr("cst", cst.shape, "ExternalInput")
    outp = dr("outp", (128, 4096), "ExternalOutput")
    slabs = build(nc, xin, cin, kin, outp)
    wts = pack_weights(slabs, inp)
    r = _run(nc, [{"xin": x, "cols": cols, "cst": cst, "wts": wts}], core_ids=[0])
    y = np.asarray(r.results[0]["outp"]).reshape(128, 8, 512)
    return y.transpose(2, 1, 0).reshape(1, 512, 1024)
```

```python
import math
import numpy as np
import concourse.bass as bass
from concourse import mybir
from contextlib import ExitStack

F32 = mybir.dt.float32
I32 = mybir.dt.int32
ALU = mybir.AluOpType
ACT = mybir.ActivationFunctionType
AX = mybir.AxisListType
MUL, ADD, SUB, MAX, MIN = ALU.mult, ALU.add, ALU.subtract, ALU.max, ALU.min

T = 528
TILES = [(0, 16), (16, 128), (144, 128), (272, 128), (400, 128)]
HALVES = {528: [(0, 264), (264, 264)], 512: [(0, 512)]}
ALPHA = 2.0 ** 0.25
NFF = 22
NB = 23



def col_plan():
    at, n = {}, 0

    def add(name, w):
        nonlocal n
        at[name] = n
        n += w

    for l in range(2):
        for name, w in (("norm_mix", 8), ("norm_ffn", 8), ("pool_scale", 4), ("da_subln", 1), ("rw_mu", 14),
                        ("rw_w0", 4), ("rw_a0", 4), ("rw_k_k", 4), ("rw_k_a", 4), ("rw_r_k", 4),
                        ("rw_lnx_w", 4), ("rw_lnx_b", 4), ("ffn_conv", 132), ("da_lambda", 4)):
            add((name, l), w)
    for name, w in (("norm_final", 8), ("c_2", 8), ("ada_b_2", 48), ("b_in_2", 24), ("hgrn_lb_2", 4),
                    ("hgrn_norm_w_2", 1), ("conv_w_2", 124), ("conv_b_2", 4), ("conv_ln_g_2", 4),
                    ("conv_ln_b_2", 4), ("b_out_2", 8), ("ln1_g_2", 8), ("ln1_b_2", 8), ("ln2_g_2", 8),
                    ("ln2_b_2", 8), ("router_bias_2", 16), ("router_w_2", 128)):
        add(name, w)
    return at, n


def const_plan():
    at, n = {}, 0
    for name, w in (("id", 128), ("one", 128), ("blk", 128), ("mA", 128), ("mAT", 128), ("mO", 128),
                    ("mUs", 128), ("mUi", 128), ("rot", 128), ("cos", T), ("sin", T), ("am", 64),
                    ("ic", 64), ("rs", T)):
        at[name] = (n, w)
        n += w
    m = at["cos"][0]
    for name, w in (("hrs", 512), ("hm", 1024), ("tri", 128), ("bi", NB)):
        at[name] = (m, w)
        m += w
    assert m <= n
    return at, n


def consts(block):
    at, n = const_plan()
    c = np.zeros((128, n), np.float32)

    def put(name, a):
        o, w = at[name]
        c[:, o:o + w] = a

    p = np.arange(128)[:, None]
    q = np.arange(128)[None, :]
    put("id", p == q)
    put("one", 1.0)
    put("blk", p // 64 == q // 64)
    put("mA", (q < p) & (p // 16 == q // 16))
    put("mAT", (q > p) & (p // 16 == q // 16))
    put("mO", (q < p) & (p // 16 != q // 16) & (p // 64 == q // 64))
    put("mUs", (q > p) & (p // 64 == q // 64))
    put("mUi", (q >= p) & (p // 64 == q // 64))
    d, m = p % 64, q % 64
    same = p // 64 == q // 64
    put("rot", -1.0 * (same & (m < 8) & (d == m + 8)) + 1.0 * (same & (m >= 8) & (m < 16) & (d == m - 8)))
    pos = np.arange(T, dtype=np.float32)
    inv = np.float32(500000.0) ** (-np.arange(0, 16, 2, dtype=np.float32) / np.float32(16))
    ang = pos[:, None] * inv[None, :].astype(np.float32)
    C = np.ones((128, T), np.float32)
    S = np.zeros((128, T), np.float32)
    for b in (0, 64):
        for i in range(16):
            C[b + i] = np.cos(ang[:, i % 8])
            S[b + i] = np.sin(ang[:, i % 8])
    if block == 0:
        put("cos", C)
        put("sin", S)
    put("am", np.where(p < 64, -1e30, 0.0))
    ic = np.zeros((4, 16), np.float32)
    for g, w in enumerate((2, 4, 8, 16)):
        ic[g] = np.float32(1) / np.minimum(np.arange(1, 17), w).astype(np.float32)
    put("ic", ic.reshape(1, 64))
    t = np.arange(T)
    put("rs", np.where((t == 0) | ((t >= 16) & ((t - 16) % 64 == 0)), 0.0, 1.0)[None, :])
    if block == 0:
        return c
    t = np.arange(512)
    put("hrs", np.where(t % 128 == 0, 0.0, 1.0)[None, :])
    hm = np.zeros((128, 8, 128))
    for i in range(7):
        m_ = 64 >> i
        hm[:, i] = (p // (2 * m_) == q // (2 * m_)) & (p % (2 * m_) < m_) & (q % (2 * m_) >= m_)
    hm[:, 7] = p == q
    put("hm", hm.reshape(128, 1024))
    put("tri", q > p)
    put("bi", np.arange(NB)[None, :])
    o = at["hrs"][0]
    return c[:, o:o + 1664 + NB].copy()




class Queue:

    def __init__(self, name):
        self.name, self.items, self.n, self.seen = name, [], 0, {}

    def need(self, *toks):
        for t in toks:
            if t is None:
                continue
            if isinstance(t, list):
                self.need(*t)
                continue
            s, v = t
            if self.seen.get(s, 0) < v:
                self.seen[s] = v
                self.items.append((None, s, v))

    def do(self, fn, *toks, mark=True):
        self.need(*toks)
        if mark:
            self.n += 1
        self.items.append((fn, mark, None))
        return (self.name, self.n)

    def last(self):
        return (self.name, self.n)


class Banks:

    def __init__(self):
        self.at, self.lim, self.free, self.busy = 0, 8, [[] for _ in range(8)], [False] * 8

    def take(self, n=1):
        if self.at + n > self.lim:
            self.at = 0
        b = self.at
        self.at = b + n
        return self.claim(b, n)

    def claim(self, b, n):
        for i in range(b, b + n):
            assert not self.busy[i], "bank still in use"
            self.busy[i] = True
        return b, [self.free[i] for i in range(b, b + n)]

    def give(self, b, n, *toks):
        for i in range(b, b + n):
            self.busy[i] = False
            self.free[i] = list(toks)


NRING = 9
SLAB = 1024


class Program:
    def __init__(self, stop=None):
        self.P, self.V, self.S, self.G, self.D = (Queue(n) for n in ("pe", "dve", "act", "pool", "sp"))
        self.ps = Banks()
        self.slabs = []
        self.slab_end = 0
        self.ring_use = [None] * NRING
        self.stop = stop
        self.bg = None

    def slab(self, pieces):
        i = len(self.slabs)
        slot = i % NRING
        assert self.ring_use[slot] != "open"
        n = sum(p[3] * p[5] for p in pieces)
        assert n <= SLAB
        off = self.slab_end
        self.slab_end += 128 * n
        self.slabs.append(pieces)
        freed = self.ring_use[slot]
        self.ring_use[slot] = "open"
        ring = self.ring
        w = self

        def load(eng, slot=slot, n=n, off=off):
            return eng.dma_start(ring[:, slot, 0:n],
                                 w.wts[off:off + 128 * n].rearrange("(p n) -> p n", n=n)).then_inc(w.sems[f"w{slot}"], 16)

        self.D.need(freed)
        self.D.items.append((load, False, None))
        tok = (f"w{slot}", 16 * (i // NRING + 1))
        views, o = [], 0
        for (_, _, _, nk, _, nc_) in pieces:
            views.append(ring[:, slot, o:o + nk * nc_].rearrange("p (k c) -> p k c", k=nk))
            o += nk * nc_
        return views, tok, slot

    def used(self, slot, tok):
        self.ring_use[slot] = tok

    def mm(self, out, lhsT, rhs, start, stop, *toks, mark=False):
        return self.P.do(lambda e: e.matmul(out, lhsT, rhs, start=start, stop=stop, skip_group_check=True), *toks, mark=mark)

    def tr(self, out, in_, k, *toks, mark=False):
        idn = self.c("id")[0:k, 0:k]
        return self.P.do(lambda e: e.transpose(out, in_, idn), *toks, mark=mark)

    def tt(self, E, out, a, b, op, *toks):
        return E.do(lambda e: e.tensor_tensor(out, a, b, op), *toks)

    def ts(self, E, out, a, s1, op0, s2=None, op1=None, *toks):
        if op1 is None:
            return E.do(lambda e: e.tensor_scalar(out, a, s1, None, op0), *toks)
        return E.do(lambda e: e.tensor_scalar(out, a, s1, s2, op0, op1), *toks)

    def stt(self, out, a, s, b, op0, op1, *toks):
        return self.V.do(lambda e: e.scalar_tensor_tensor(out=out, in0=a, scalar=s, in1=b, op0=op0, op1=op1), *toks)

    def act(self, out, a, f, *toks, bias=0.0, scale=1.0, accum=None):
        kw = {} if accum is None else {"accum_out": accum}
        return self.S.do(lambda e: e.activation(out, a, f, bias=bias, scale=scale, **kw), *toks)

    def copy(self, E, out, a, *toks):
        if E is self.S:
            return E.do(lambda e: e.copy(out, a), *toks)
        return E.do(lambda e: e.tensor_copy(out, a), *toks)

    def zero(self, E, out, *toks):
        return E.do(lambda e: e.memset(out, 0.0), *toks)

    def recip(self, out, a, *toks):
        return self.V.do(lambda e: e.reciprocal(out, a), *toks)

    def c(self, name):
        o, w = self.cat[name]
        return self.K[:, o:o + w]

    def col(self, name, i=0, l=None):
        o = self.cols_at[name if l is None else (name, l)] + i
        return self.COLS[:, o:o + 1]

    def colr(self, name, a, b, l=None):
        o = self.cols_at[name if l is None else (name, l)]
        return self.COLS[:, o + a:o + b]

    def pv(self, b, n):
        return self.PSUM[:, b:b + 2, 0:264] if n == T else self.PSUM[:, b, 0:n]

    def tv(self, ap, n):
        return ap.rearrange("p (a b) -> p a b", a=2) if n == T else ap

    def nb(self, n):
        return 2 if n == T else 1

    def proj(self, w, m0, rhs, n, toks, b=None, free=None, first=True, last=True):
        if b is None:
            b, free = self.ps.take(self.nb(n))
        nk = w.shape[1]
        tok = None
        for hi, (a, ln) in enumerate(HALVES[n]):
            for k in range(nk):
                tok = self.mm(self.PSUM[:, b + hi, 0:ln], w[:, k, m0:m0 + 128], rhs(k, a, ln),
                              first and k == 0, last and k == nk - 1, toks, free,
                              mark=(k == nk - 1 and hi == len(HALVES[n]) - 1))
        return b, tok

    def lin(self, name, idx, m, rhs, n, toks):
        (w,), wt, slot = self.slab([(name, idx, 0, 8, m * 128, 128)])
        b, t = self.proj(w, 0, rhs, n, [wt, toks])
        self.used(slot, t)
        return b, t

    def fill(self, n=1):
        for _ in range(n):
            if self.bg is None or next(self.bg, self) is self:
                self.bg = None
                return

    def mark(self, name):
        pass

    def fence(self):
        return [q.last() for q in (self.P, self.V, self.S, self.G)]

    def all_wait(self, toks=None):
        toks = toks or self.fence()
        for q in (self.P, self.V, self.S, self.G):
            q.need(toks)

    def colsum(self, mat, srcs, n, toks):
        b, free = self.ps.take(self.nb(n))
        tok = None
        for k, s in enumerate(srcs):
            for hi, (a, ln) in enumerate(HALVES[n]):
                tok = self.mm(self.PSUM[:, b + hi, 0:ln], mat, s[:, a:a + ln], k == 0, k == len(srcs) - 1,
                              toks[k], free, mark=(hi == len(HALVES[n]) - 1))
        return b, tok

    def rstd(self, out, b, n, scale, eps, tok, *toks):
        t = self.ts(self.V, self.tv(out, n), self.pv(b, n), scale, MUL, eps, ADD, tok, *toks)
        self.ps.give(b, self.nb(n), t)
        t = self.act(out, out, ACT.Sqrt, t)
        return self.recip(out, out, t)

    def rms(self, src, dst, n, gname, l, toks, rs):
        sq = [self.act(dst(k), src(k), ACT.Square, toks[k]) for k in range(8)]
        b, t = self.colsum(self.c("one"), [dst(k) for k in range(8)], n, sq)
        r = self.rstd(rs, b, n, 1.0 / 1024, 1e-6, t)
        return [self.stt(dst(k), src(k), self.col(gname, k, l), rs, MUL, MUL, r) for k in range(8)]

    def ln(self, src, dst, nt, tmp, rs, toks, scale, shift, width, func=None):
        b, t = self.colsum(self.c("one"), [src(k) for k in range(nt)], 512, toks)
        ctr, sqt = [], []
        bb, fr = None, None
        for k in range(nt):
            c_ = self.stt(dst(k), self.PSUM[:, b, 0:512], -1.0 / width, src(k), MUL, ADD, t)
            ctr.append(c_)
        self.ps.give(b, 1, ctr[-1])
        bb, fr = self.ps.take(1)
        done = [None, None]
        for k in range(nt):
            s_ = self.act(tmp(k % 2), dst(k), ACT.Square, ctr[k], done[k % 2])
            done[k % 2] = self.mm(self.PSUM[:, bb, 0:512], self.c("one"), tmp(k % 2), k == 0, k == nt - 1, s_, fr, mark=True)
        r = self.rstd(rs, bb, 512, 1.0 / width, 1e-5, done[(nt - 1) % 2])
        out = []
        for k in range(nt):
            m = self.tt(self.V, dst(k), dst(k), rs, MUL, r, ctr[k])
            out.append(self.act(dst(k), dst(k), func or ACT.Identity, m, scale=scale(k), bias=shift(k)))
        return out




def rwkv(p, l, hx, htok, work):
    V, S, G, P, ps = p.V, p.S, p.G, p.P, p.ps
    A = p.arena

    def R4(o):
        return A[:, o:o + 2112].rearrange("p (a t) -> p a t", a=4)

    oR, oK, oV, oBV, oAH, oBH, oT1, oLD, oAA, oT2, oT3, oBB, oWA, oGL = [2112 * i for i in range(12)] + [25344, 25872]
    Rf, Kf, Vf, BV, AH, BH, T1, LD, AA, T2, T3, BB = [R4(2112 * i) for i in range(12)]
    WA, GL = A[:, oWA:oWA + T], A[:, oGL:oGL + T]
    full = {i: A[:, 2112 * i:2112 * i + 2112] for i in range(12)}
    fR, fK, fV, fBV, fAH, fBH, fT1, fLD, fAA, fT2, fT3, fBB = [full[i] for i in range(12)]

    raw = [A[:, oT3 + 530 * i:oT3 + 530 * i + 529] for i in range(2)]
    dif = [A[:, oT2 + 530 * i:oT2 + 530 * i + T] for i in range(2)]
    z = [p.zero(V, raw[i][:, 0:1]) for i in range(2)]
    ptok = []
    dst = [Rf[:, i] for i in range(4)] + [Kf[:, i] for i in range(4)] + [Vf[:, i] for i in range(4)] + [WA, GL]
    mixed = [None, None]
    for m in range(14):
        b, t = p.lin("w_in", (l,), 16 + m, hx, T, htok)
        r = raw[m % 2]
        c1 = p.copy(S, p.tv(r[:, 1:529], T), p.pv(b, T), t, mixed[m % 2], z[m % 2])
        ps.give(b, 2, c1)
        d = p.tt(V, dif[m % 2], r[:, 0:T], r[:, 1:529], SUB, c1)
        o = p.stt(dst[m], dif[m % 2], p.col("rw_mu", m, l), r[:, 1:529], MUL, ADD, d)
        mixed[m % 2] = o
        ptok.append(o)
    tr_, tk_, tv_ = ptok[3], ptok[7], ptok[11]
    (ww,), wt, slot = p.slab([("wa2", (l,), 0, 1, 0, 512)])
    th = p.act(WA[0:64, :], WA[0:64, :], ACT.Tanh, ptok[12])
    gs = p.act(GL, GL, ACT.Sigmoid, ptok[13])
    sg, ag = [], []
    for n in range(4):
        for part, (lo, name, out, acc) in enumerate(((0, "rw_w0", LD, sg), (64, "rw_a0", AA, ag))):
            b, fr = ps.take(2)
            for hi, (a, ln) in enumerate(HALVES[T]):
                t = p.mm(p.PSUM[:, b + hi, 0:ln], ww[lo:lo + 64, 0, n * 128:n * 128 + 128], WA[lo:lo + 64, a:a + ln],
                         True, True, wt, fr, th, ptok[12], mark=True)
            s_ = p.act(p.tv(out[:, n], T), p.pv(b, T), ACT.Sigmoid, t, bias=p.col(name, n, l))
            ps.give(b, 2, s_)
            acc.append(s_)
    p.mark("rwlin")
    p.used(slot, t)
    p.bg = work
    ld = p.ts(V, fLD, fLD, -math.exp(-0.5), MUL, None, None, sg[-1])
    bt = [V.do(lambda e, n=n: e.tensor_tensor_scan(BB[:, n], p.c("rs"), LD[:, n], 0.0, MUL, ADD), ld) for n in range(4)][-1]
    kk = [p.ts(V, T1[:, n], Kf[:, n], p.col("rw_k_k", n, l), MUL, None, None, tk_) for n in range(4)]
    sq = [p.act(T2[:, n], T1[:, n], ACT.Square, kk[n], ptok[13]) for n in range(4)]
    mx = []
    p.fill(10)
    for n in range(4):
        b, t = p.colsum(p.c("blk"), [T2[:, n]], T, [sq[n]])
        t = p.ts(V, p.tv(T2[:, n], T), p.pv(b, T), 1e-24, MAX, None, None, t)
        ps.give(b, 2, t)
        mx.append(t)
    t = p.act(fT2, fT2, ACT.Sqrt, mx[-1])
    t = p.recip(fT2, fT2, t)
    kkn = p.tt(V, fT1, fT1, fT2, MUL, t)
    k1 = []
    for n in range(4):
        t = p.ts(V, T3[:, n], AA[:, n], -1.0, ADD, p.col("rw_k_a", n, l), MUL, ag[-1], mixed)
        k1.append(p.stt(Kf[:, n], T3[:, n], 1.0, Kf[:, n], ADD, MUL, t))
    p.fill(14)
    bo = []
    for n in range(4):
        t = p.stt(T2[:, n], Rf[:, n], p.col("rw_r_k", n, l), Kf[:, n], MUL, MUL, k1[n], kkn, tr_)
        b, t = p.colsum(p.c("blk"), [T2[:, n]], T, [t])
        t2 = p.tt(V, p.tv(BV[:, n], T), p.pv(b, T), p.tv(Vf[:, n], T), MUL, t, tv_)
        ps.give(b, 2, t2)
        bo.append(t2)
    p.fill(16)
    sb = p.tt(V, fT3, fBB, fLD, SUB, bt, k1[-1])
    e1 = p.act(fT3, fT3, ACT.Exp, sb)
    ah = p.stt(fAH, fT1, -1.0, fT3, MUL, MUL, e1, kkn)
    be = p.tt(V, fT1, fT1, fAA, MUL, ah)
    e2 = p.act(fT2, fBB, ACT.Exp, bo[-1], scale=-1.0)
    bh = p.tt(V, fBH, fT1, fT2, MUL, e2, be)
    kh = p.tt(V, fK, fK, fT2, MUL, e2, bo[-1])
    e3 = p.act(fLD, fBB, ACT.Exp, sb)
    rh = p.tt(V, fR, fR, fLD, MUL, e3, bo[-1])
    DE = p.small[:, 0:36].rearrange("p (a c) -> p a c", a=4)
    de = p.copy(V, DE, LD[:, :, 15::64], e3)
    ready = [ah, bh, kh, rh, de]

    p.mark("rwpre")
    o = oT1

    def buf(n=512):
        nonlocal o
        o += n
        return A[:, o - n:o]

    v4 = lambda x: x.rearrange("p (a t) -> p a t", a=4)
    bA, bAT, bO, bPT, bNT, bQT, bC, bD, bP, bQ, bE, bM = [v4(buf()) for _ in range(12)]
    bET = bM
    VT = v4(buf())
    BZ, KZ = [buf(1024).rearrange("p (g a t) -> p g a t", g=2, a=4) for _ in range(2)]
    BT, KT = [buf(1024).rearrange("p (c a t) -> p c a t", c=2, a=4) for _ in range(2)]
    U = [buf(1024).rearrange("p (a b c d) -> p a b c d", a=4, b=2, c=2) for i in range(2)]
    FT, HT, GT, Y0 = [v4(buf()) for x in range(4)]
    SB = [v4(buf()) for i in range(2)]
    if o > oGL:
        assert o <= 29600 - T
        GL2 = A[:, 29600 - T:29600]
        cg = p.copy(S, GL2, GL, gs)
    else:
        GL2, cg = GL, gs
    p.all_wait()

    def bc(ap, n):
        return ap.unsqueeze(1).broadcast_to([ap.shape[0], 4, n])

    st = p.zero(G, SB[0])
    zz = [p.zero(G, BZ), p.zero(G, KZ), p.zero(G, BT), p.zero(G, KT)]
    cur = 0
    last_mm = None
    for j, (t0, n) in enumerate(TILES):
        tk = slice(t0, t0 + n)
        ck = range(max(1, n // 64))
        cw = min(n, 64)

        def group4(pairs, *toks, fill=1):
            p.fill(fill)
            b, fr = ps.take(1)
            t = None
            for q in range(4):
                lst = pairs(q)
                for i, (lh, rh_) in enumerate(lst):
                    w_ = rh_.shape[-1] if len(rh_.shape) == 2 else rh_.shape[-1] * rh_.shape[-2]
                    t = p.mm(p.PSUM[0:lh.shape[-1], b, q * 128:q * 128 + w_], lh, rh_, i == 0, i == len(lst) - 1,
                             fr, *toks, mark=(q == 3 and i == len(lst) - 1))
            return b, t

        def view(b, m=n, w=n):
            return v4(p.PSUM[0:m, b, :])[:, :, 0:w]

        bz, kz = [], []
        for g in range(2):
            lo = 64 * g
            bz.append(p.copy(S, BZ[lo:lo + 64, g, :, 0:n], BH[lo:lo + 64, :, tk], ready, zz, last_mm))
            kz.append(p.copy(V, KZ[lo:lo + 64, g, :, 0:n], Kf[lo:lo + 64, :, tk], ready, zz, last_mm))
        tmt = []
        for src, kind in ((BH, 0), (Kf, 1), (Vf, 2), (AH, 3)):
            b, fr = ps.take(1)
            for q in range(4):
                t = p.tr(p.PSUM[0:n, b, q * 128:q * 128 + 128], src[:, q, tk], 128, fr, ready, tv_, mark=(q == 3))
            if kind < 2:
                tc = []
                for c in ck:
                    rows = slice(64 * c, 64 * c + cw)
                    tc.append(p.copy(S, (BT, KT)[kind][rows, c], v4(p.PSUM[rows, b, :]), t, zz, last_mm))
                t = tc
            elif kind == 2:
                t = p.copy(S, VT[0:n], view(b, n, 128), t, last_mm)
            else:
                for g in range(2):
                    t = p.copy(V, U[0][0:n, :, 0, g, :], view(b, n, 128)[:, :, 64 * g:64 * g + 64], t, last_mm)
            ps.give(b, 1, t)
            tmt.append(t)
        gt_last = []
        for g in range(2):
            lo = 64 * g
            pr = P.last()
            b, t = group4(lambda q: [(BZ[:, g, q, 0:n], AH[:, q, tk])], bz)
            tM = p.tt(V, bM[0:n, :, 0:n], view(b), bc(p.c("mUs")[0:n, 0:n], n), MUL, t, pr)
            tAT = p.tt(V, bAT[0:n, :, 0:n], view(b), bc(p.c("mAT")[0:n, 0:n], n), MUL, t)
            ps.give(b, 1, tAT)
            b, t = group4(lambda q: [(KZ[:, g, q, 0:n], AH[:, q, tk])], kz, fill=0)
            tNT = p.tt(V, bNT[0:n, :, 0:n], view(b), bc(p.c("mUs")[0:n, 0:n], n), MUL, t)
            ps.give(b, 1, tNT)
            p.fill(1)
            b, fr = ps.take(1)
            for q in range(4):
                t = p.tr(p.PSUM[0:n, b, q * 128:q * 128 + n], bM[0:n, q, 0:n], n, fr, tM, mark=(q == 3))
            tA = p.tt(V, bA[0:n, :, 0:n], view(b), bc(p.c("mA")[0:n, 0:n], n), MUL, t)
            tO = p.tt(V, bO[0:n, :, 0:n], view(b), bc(p.c("mO")[0:n, 0:n], n), MUL, t)
            ps.give(b, 1, tO)
            b, t = group4(lambda q: [(bNT[0:n, q, 0:n], VT[0:n, q, :])], tNT, tmt[2], fill=0)
            tnv = p.copy(S, U[0][0:n, :, 1, g, :], view(b, n, 128)[:, :, lo:lo + 64], t, last_mm)
            ps.give(b, 1, tnv)
            b1, t1 = group4(lambda q: [(bAT[0:n, q, 0:n], bA[0:n, q, 0:n])], tAT, tA)
            b2, t2 = group4(lambda q: [(bA[0:n, q, 0:n], bAT[0:n, q, 0:n])], fill=0)
            tC = p.copy(V, bC[0:n, :, 0:n], view(b1), t1)
            ps.give(b1, 1, tC)
            tD = p.copy(S, bD[0:n, :, 0:n], view(b2), t2)
            ps.give(b2, 1, tD)
            tP = p.tt(V, bP[0:n, :, 0:n], bAT[0:n, :, 0:n], bc(p.c("id")[0:n, 0:n], n), ADD, tAT)
            b, t = group4(lambda q: [(BZ[:, g, q, 0:n], Rf[:, q, tk])], fill=0)
            tPT = p.tt(V, bPT[0:n, :, 0:n], view(b), bc(p.c("mUi")[0:n, 0:n], n), MUL, t)
            ps.give(b, 1, tPT)
            b2, t2 = group4(lambda q: [(bD[0:n, q, 0:n], bC[0:n, q, 0:n])], tD, tC, fill=0)
            b1, t1 = group4(lambda q: [(bC[0:n, q, 0:n], bD[0:n, q, 0:n])], fill=0)
            b3, t3 = group4(lambda q: [(bC[0:n, q, 0:n], bP[0:n, q, 0:n])], tP, fill=0)
            tA4 = p.copy(V, bA[0:n, :, 0:n], view(b2), t2)
            ps.give(b2, 1, tA4)
            tAT4 = p.copy(S, bAT[0:n, :, 0:n], view(b1), t1, tP)
            ps.give(b1, 1, tAT4)
            tQ = p.tt(V, bQ[0:n, :, 0:n], view(b3), bP[0:n, :, 0:n], ADD, t3, tP)
            ps.give(b3, 1, tQ)
            b, t = group4(lambda q: [(KZ[:, g, q, 0:n], Rf[:, q, tk])], fill=0)
            tQT = p.tt(V, bQT[0:n, :, 0:n], view(b), bc(p.c("mUi")[0:n, 0:n], n), MUL, t)
            ps.give(b, 1, tQT)
            b2, t2 = group4(lambda q: [(bAT[0:n, q, 0:n], bA[0:n, q, 0:n])], tAT4, tA4, fill=0)
            b3, t3 = group4(lambda q: [(bA[0:n, q, 0:n], bQ[0:n, q, 0:n])], tQ, fill=0)
            tC = p.copy(S, bC[0:n, :, 0:n], view(b2), t2)
            ps.give(b2, 1, tC)
            tP = p.tt(V, bP[0:n, :, 0:n], view(b3), bQ[0:n, :, 0:n], ADD, t3, tQ)
            ps.give(b3, 1, tP)
            b3, t3 = group4(lambda q: [(bC[0:n, q, 0:n], bP[0:n, q, 0:n])], tC, tP, fill=1)
            tQ = p.tt(V, bQ[0:n, :, 0:n], view(b3), bP[0:n, :, 0:n], ADD, t3, tP)
            ps.give(b3, 1, tQ)
            rhs = lambda i: (lambda q: U[i][0:n, q, :, g, :])
            b1, t1 = group4(lambda q: [(bO[0:n, q, 0:n], bQ[0:n, q, 0:n])], tQ, tO, fill=1)
            b2, t2 = group4(lambda q: [(bQ[0:n, q, 0:n], bO[0:n, q, 0:n])], fill=0)
            b3, t3 = group4(lambda q: [(bQ[0:n, q, 0:n], rhs(0)(q))], tnv, tmt[3], fill=0)
            tET = p.copy(V, bET[0:n, :, 0:n], view(b1), t1)
            ps.give(b1, 1, tET)
            tE = p.copy(S, bE[0:n, :, 0:n], view(b2), t2, pr)
            ps.give(b2, 1, tE)
            uv = lambda b: p.PSUM[0:n, b, :].rearrange("p (a b d) -> p a b d", a=4, b=2)
            us = lambda i: U[i][0:n, :, :, g, :]
            tR = p.copy(S, us(1), uv(b3), t3, last_mm)
            ps.give(b3, 1, tR)
            b2, t2 = group4(lambda q: [(bE[0:n, q, 0:n], bET[0:n, q, 0:n])], tE, tET)
            tD = p.copy(V, bD[0:n, :, 0:n], view(b2), t2)
            ps.give(b2, 1, tD)
            b3, t3 = group4(lambda q: [(bD[0:n, q, 0:n], rhs(1)(q))], tD, tR, fill=1)
            tR2 = p.tt(V, us(0), uv(b3), us(1), ADD, t3, tR)
            ps.give(b3, 1, tR2)
            b3, t3 = group4(lambda q: [(bET[0:n, q, 0:n], rhs(0)(q))], tR2, fill=1)
            tR3 = p.tt(V, us(1), uv(b3), us(0), ADD, t3, tR2)
            ps.give(b3, 1, tR3)
            p.fill(1)
            b, fr = ps.take(1)
            for q in range(4):
                t = p.mm(p.PSUM[lo:lo + 64, b, q * 128:q * 128 + n], U[1][0:n, q, 0, g, :], bPT[0:n, q, 0:n],
                         True, True, fr, tR3, tPT, mark=True)
            pvw = v4(p.PSUM[lo:lo + 64, b, :])[:, :, 0:n]
            tG = p.tt(V, GT[lo:lo + 64, :, 0:n], pvw, Rf[lo:lo + 64, :, tk], ADD, t, last_mm)
            ps.give(b, 1, tG)
            b, fr = ps.take(1)
            for q in range(4):
                p.mm(p.PSUM[lo:lo + 64, b, q * 128:q * 128 + n], U[1][0:n, q, 1, g, :], bPT[0:n, q, 0:n], True, False, fr)
                t = p.mm(p.PSUM[lo:lo + 64, b, q * 128:q * 128 + n], VT[0:n, q, lo:lo + 64], bQT[0:n, q, 0:n],
                         False, True, tQT, mark=True)
            pvw = v4(p.PSUM[lo:lo + 64, b, :])[:, :, 0:n]
            tY = p.copy(S, Y0[lo:lo + 64, :, 0:n], pvw, t, last_mm)
            ps.give(b, 1, tY)
            gt_last = gt_last + [tG, tY, tR3]
        rows = slice(0, n)
        pair = lambda q, part: U[1][rows, q, part, :, :].rearrange("p g d -> p (g d)")
        for ci in ck:
            w = cw
            r0 = 64 * ci
            cidx = 0 if j == 0 else 2 * j - 1 + ci
            b, t = group4(lambda q: [(pair(q, 0), BT[rows, ci, q, :])], gt_last, tmt[0], fill=0)
            t = p.tt(V, FT, v4(p.PSUM[:, b, :]), bc(p.c("blk"), 128), MUL, t, last_mm)
            ps.give(b, 1, t)
            tF = p.tt(V, FT, FT, bc(p.c("id"), 128), ADD, t)
            b, t = group4(lambda q: [(BT[rows, ci, q, :], pair(q, 1)), (KT[rows, ci, q, :], VT[rows, q, :])],
                          tmt[1], tmt[2], fill=0)
            tH = p.tt(V, HT, v4(p.PSUM[:, b, :]), bc(p.c("blk"), 128), MUL, t)
            ps.give(b, 1, tH)
            b, t = group4(lambda q: [(SB[cur][:, q, :], GT[:, q, 0:n])], st, fill=1)
            ty = p.tt(V, AH[:, :, t0 + r0:t0 + r0 + w], v4(p.PSUM[:, b, :])[:, :, r0:r0 + w], Y0[:, :, r0:r0 + w], ADD, t)
            ps.give(b, 1, ty)
            b, t = group4(lambda q: [(FT[:, q, :], SB[cur][:, q, :])], tF, fill=0)
            nx = 1 - cur
            t1 = p.tt(V, SB[nx], v4(p.PSUM[:, b, :]), HT, ADD, t, tH)
            ps.give(b, 1, t1)
            dcol = DE[:, :, cidx:cidx + 1].broadcast_to([128, 4, 128])
            st = p.tt(V, SB[nx], SB[nx], dcol, MUL, t1)
            cur = nx
            last_mm = [P.last(), V.last()]
    p.mark("rwcore")
    p.all_wait()
    p.fill(4)
    Yf = AH
    p1 = []
    for n in range(4):
        b, t = p.colsum(p.c("blk"), [Yf[:, n]], T, [None])
        t = p.stt(p.tv(T1[:, n], T), p.pv(b, T), -1.0 / 64, p.tv(Yf[:, n], T), MUL, ADD, t)
        ps.give(b, 2, t)
        p1.append(t)
    sq = [p.act(T2[:, n], T1[:, n], ACT.Square, p1[n]) for n in range(4)]
    rr = []
    p.fill(3)
    for n in range(4):
        b, t = p.colsum(p.c("blk"), [T2[:, n]], T, [sq[n]])
        t = p.ts(V, p.tv(T3[:, n], T), p.pv(b, T), 1.0 / 64, MUL, 64e-5, ADD, t)
        ps.give(b, 2, t)
        rr.append(t)
    t = p.act(fT3, fT3, ACT.Sqrt, rr[-1])
    t = p.recip(fT3, fT3, t)
    yn = p.tt(V, fT1, fT1, fT3, MUL, t)
    outs = []
    (gw,), gwt, slot = p.slab([("rw_g2", (l,), 0, 1, 0, 512)])
    p.fill(14)
    for n in range(4):
        b, fr = ps.take(2)
        for hi, (a, ln) in enumerate(HALVES[T]):
            t = p.mm(p.PSUM[:, b + hi, 0:ln], gw[:, 0, n * 128:n * 128 + 128], GL2[:, a:a + ln], True, True, fr, cg, gwt, mark=True)
        u = p.ts(V, T1[:, n], T1[:, n], p.col("rw_lnx_w", n, l), MUL, p.col("rw_lnx_b", n, l), ADD, yn)
        u = p.tt(V, T1[:, n], T1[:, n], BV[:, n], ADD, u)
        u = p.tt(V, p.tv(Rf[:, n], T), p.pv(b, T), p.tv(T1[:, n], T), MUL, u, t)
        ps.give(b, 2, u)
        outs.append(u)
    p.used(slot, P.last())
    p.bg = None
    return Rf, outs[-1]


def attention(p, l, hx, htok, work):
    V, S, G, P, ps = p.V, p.S, p.G, p.P, p.ps
    A = p.arena
    o = 2112

    def buf(n):
        nonlocal o
        o += n
        return A[:, o - n:o]

    BD = buf(2112).rearrange("p (a t) -> p a t", a=4)
    Qf = buf(2112).rearrange("p (a t) -> p a t", a=4)
    KZ = buf(4224).rearrange("p (c a t) -> p c a t", c=2, a=4)
    KN = buf(2112).rearrange("p (a t) -> p a t", a=4)
    VT = buf(2560).rearrange("p (a t) -> p a t", a=5)
    raw = [buf(T) for _ in range(2)]
    rt = [buf(T) for _ in range(2)]
    EE = [buf(1056) for _ in range(2)]
    AB = [buf(T) for _ in range(2)]
    AT = [buf(640).rearrange("p (a t) -> p a t", a=5) for _ in range(2)]
    SC = buf(64)
    lam = p.small[:, 40:41]
    lp = p.small[:, 41:43]
    le = p.small[:, 43:45]
    lc = p.colr("da_lambda", 0, 4, l)
    t = p.tt(V, lp, lc[:, 0:4:2], lc[:, 1:4:2], MUL, V.last())
    b, fr = ps.take(1)
    t = p.mm(p.PSUM[:, b, 0:2], p.c("one"), lp, True, True, fr, t, mark=True)
    t = p.act(le, p.PSUM[:, b, 0:2], ACT.Exp, t)
    ps.give(b, 1, t)
    t = p.tt(V, lam, le[:, 0:1], le[:, 1:2], SUB, t)
    linit = 0.8 - 0.6 * math.exp(-0.3 * l)
    tlam = p.ts(V, lam, lam, linit, ADD, None, None, t)

    rdone = [None, None]
    qk = []
    zk = p.zero(G, KZ)
    for m in range(8):
        b, t = p.lin("w_in", (l,), 4 + m, hx, T, htok)
        i = m % 2
        c1 = p.copy(S, p.tv(raw[i], T), p.pv(b, T), t, rdone[i])
        ps.give(b, 2, c1)
        b, t = p.colsum(p.c("rot"), [raw[i]], T, [c1])
        d = p.tt(V, p.tv(rt[i], T), p.pv(b, T), p.tv(p.c("sin"), T), MUL, t)
        ps.give(b, 2, d)
        if m < 4:
            dst = Qf[:, m]
            e = p.tt(G, dst, raw[i], p.c("cos"), MUL, c1)
            rdone[i] = p.tt(V, dst, dst, rt[i], ADD, d, e)
        else:
            e = p.tt(G, raw[i], raw[i], p.c("cos"), MUL, c1, P.last())
            for c in range(2):
                h_ = slice(64 * c, 64 * c + 64)
                rdone[i] = p.tt(V, KZ[h_, c, m - 4], raw[i][h_], rt[i][h_], ADD, d, e, zk)
        qk.append(rdone[i])
    vt = []
    for half in range(2):
        ps.at = 0
        bk = [ps.take(1) for _ in range(5)]
        for kh in range(2):
            (w,), wt, slot = p.slab([("w_in", (l,), 4 * kh, 4, 1536 + half * 256, 256)])
            for j, (t0, n) in enumerate(TILES):
                b, fr = bk[j]
                for k in range(4):
                    t = p.mm(p.PSUM[0:n, b, 0:256], hx(4 * kh + k, t0, n), w[:, k, :], kh == 0 and k == 0,
                             kh == 1 and k == 3, wt, htok, fr, mark=(k == 3))
                if kh == 1:
                    c1 = p.copy(S if j % 2 else V, VT[0:n, j, half * 256:half * 256 + 256], p.PSUM[0:n, b, 0:256], t)
                    ps.give(b, 1, c1)
                    vt.append(c1)
            p.used(slot, t)

    p.mark("qkv")
    p.bg = work
    units = [(j, h) for j in range(5) for h in range(4)]
    e_free, a_free, at_free = [None, None], [None, None], [None, None]
    ot = []
    pend = None

    def scores(u):
        j, h = units[u]
        t0, n = TILES[j]
        nk = t0 + n
        nbk = 4 if nk > 512 else 2
        b, fr = ps.take(nbk)
        for c in range(2):
            for s in range(nbk // 2):
                w_ = nk // (nbk // 2)
                t = p.mm(p.PSUM[0:n, b + c * (nbk // 2) + s, 0:w_], Qf[:, h, t0:t0 + n],
                         KZ[:, c, h, s * w_:s * w_ + w_], True, True, fr, qk, zk, mark=True)
        return b, nbk, t

    def soft(u, b, nbk, t):
        j, h = units[u]
        t0, n = TILES[j]
        nk = t0 + n
        w_ = nk // (nbk // 2)
        i = u % 2
        sc = SC[:, 16 * i:16 * i + 16]
        if j > 0:
            vw = p.PSUM[0:64, b + nbk // 2 - 1:b + nbk:nbk // 2, w_ - 64:w_]
            m_ = p.c("am")[0:64, :].unsqueeze(1).broadcast_to([64, 2, 64])
            t = p.tt(V, vw, vw, m_, ADD, t)
        sv = p.PSUM[0:n, b:b + nbk, 0:w_]
        t = V.do(lambda e: e.tensor_reduce(sc[0:n, 0:nbk], sv, AX.X, MAX), t)
        if nbk == 4:
            t = p.tt(V, sc[0:n, 4:6], sc[0:n, 0:4:2], sc[0:n, 1:4:2], MAX, t)
            mxv = sc[0:n, 4:6]
        else:
            mxv = sc[0:n, 0:2]
        t = p.ts(V, sc[0:n, 6:8], mxv, -0.125, MUL, None, None, t)
        et = []
        for c in range(2):
            hb = nbk // 2
            src = p.PSUM[0:n, b + c * hb:b + c * hb + hb, 0:w_] if hb == 2 else p.PSUM[0:n, b + c, 0:w_]
            dst = EE[i][0:n, c * T:c * T + nk]
            if hb == 2:
                dst = dst.rearrange("p (a b) -> p a b", a=2)
            et.append(p.act(dst, src, ACT.Exp, t, e_free[i], bias=sc[0:n, 6 + c:7 + c], scale=0.125,
                            accum=sc[0:n, 8 + c:9 + c]))
        ps.give(b, nbk, et[-1])
        t = p.recip(sc[0:n, 10:12], sc[0:n, 8:10], et[-1])
        t = p.tt(V, sc[0:n, 12:13], sc[0:n, 11:12], lam[0:n, :], MUL, t, tlam)
        t = p.ts(V, EE[i][0:n, T:T + nk], EE[i][0:n, T:T + nk], sc[0:n, 12:13], MUL, None, None, t)
        t = p.stt(AB[i][0:n, 0:nk], EE[i][0:n, 0:nk], sc[0:n, 10:11], EE[i][0:n, T:T + nk], MUL, SUB, t, a_free[i])
        e_free[i] = t
        return t

    def pvs(u, t):
        j, h = units[u]
        t0, n = TILES[j]
        i = u % 2
        p.fill(2)
        b, fr = ps.take(2)
        for kt in range(j + 1):
            k0, kn = TILES[kt]
            out = p.PSUM[0:kn, b + 1, 0:n] if kt == 0 else p.PSUM[0:kn, b, (kt - 1) * 128:(kt - 1) * 128 + n]
            tq = p.tr(out, AB[i][0:n, k0:k0 + kn], n, fr, t, mark=(kt == j))
        a_free[i] = tq
        ca = p.copy(S, AT[i][0:16, 0, 0:n], p.PSUM[0:16, b + 1, 0:n], tq, at_free[i])
        if j > 0:
            src = p.PSUM[:, b, 0:128 * j].rearrange("p (a t) -> p a t", a=j)
            ca = [ca, p.copy(S, AT[i][:, 1:j + 1, 0:n], src, tq, at_free[i])]
        ps.give(b, 2, ca)
        p.fill(2)
        b, fr = ps.take(1)
        for kt in range(j + 1):
            kn = TILES[kt][1]
            tq = p.mm(p.PSUM[:, b, 0:n], VT[0:kn, kt, h * 128:h * 128 + 128], AT[i][0:kn, kt, 0:n],
                      kt == 0, kt == j, fr, ca, vt, mark=(kt == j))
        at_free[i] = tq
        c1 = p.copy(S, BD[:, h, t0:t0 + n], p.PSUM[:, b, 0:n], tq)
        ps.give(b, 1, c1)
        ot.append(c1)

    prev = None
    for u in range(len(units)):
        sb_ = scores(u)
        tx = soft(u, *sb_)
        if prev is not None:
            pvs(u - 1, prev)
        prev = tx
    pvs(len(units) - 1, prev)
    outs = []
    tb = ot[-1]
    sq = [p.act(Qf[:, h], BD[:, h], ACT.Square, tb, P.last()) for h in range(4)]
    for h in range(4):
        b, t = p.colsum(p.c("one"), [Qf[:, h]], T, [sq[h]])
        t = p.rstd(KN[:, h], b, T, 1.0 / 128, 1e-5, t)
        t = p.ts(V, KN[:, h], KN[:, h], p.col("da_subln", 0, l), MUL, 1.0 - linit, MUL, t)
        outs.append(p.tt(V, BD[:, h], BD[:, h], KN[:, h], MUL, t))
    return BD, outs[-1]


def pool_work(p, l, hx, htok, UU, W, outs):
    V, S, ps = p.V, p.S, p.ps
    z = [p.zero(V, x[:, 0:16]) for x in UU + W][-1]
    for g in range(4):
        (w,), wt, slot = p.slab([("w_in", (l,), 0, 8, g * 128, 128)])
        b, fr = ps.claim(6, 2)
        c = 0
        for hi, (a, ln) in enumerate(HALVES[T]):
            for k in range(8):
                t = p.mm(p.PSUM[:, b + hi, 0:ln], w[:, k, :], hx(k, a, ln), k == 0, k == 7, wt, fr, htok,
                         mark=(k == 7 and hi == 1))
                c += 1
                if c < 16 and c % 2 == 0:
                    yield
        p.used(slot, t)
        u = UU[g]
        c1 = p.copy(S, p.tv(u[:, 16:544], T), p.pv(b, T), t)
        ps.give(b, 2, c1)
        src, t = u, c1
        for s in range(g + 1):
            d = W[2 * (g % 2) + s % 2]
            sh = 1 << s
            t = p.tt(V, d[:, 16:544], src[:, 16:544], src[:, 16 - sh:544 - sh], ADD, t, z, outs[-2:])
            src = d
        dst = W[2 * (g % 2) + (g + 1) % 2]
        hd = p.tt(V, p.small[:, 640:656], src[:, 16:32], p.c("ic")[:, 16 * g:16 * g + 16], MUL, t)
        t = p.stt(dst[:, 16:544], src[:, 16:544], 1.0 / (2 << g), u[:, 16:544], MUL, SUB, t, hd)
        t = p.tt(V, dst[:, 16:32], p.small[:, 640:656], u[:, 16:32], SUB, t)
        yield
        yield
        (pw,), pwt, slot = p.slab([("pool_w", (l,), g, 1, 0, 128)])
        b, fr = ps.claim(6, 2)
        for hi, (a, ln) in enumerate(HALVES[T]):
            t2 = p.mm(p.PSUM[:, b + hi, 0:ln], pw[:, 0, :], dst[:, 16 + a:16 + a + ln], True, True, fr, t, pwt, mark=True)
        p.used(slot, t2)
        t = p.act(p.tv(u[:, 16:544], T), p.pv(b, T), ACT.Copy, t2, scale=p.col("pool_scale", g, l))
        ps.give(b, 2, t)
        outs.append(t)
        yield


def gate_work(p, l, hx, htok, done):
    P, S, ps = p.P, p.S, p.ps
    tok = None
    for i in range(24):
        n, m = i % 3, i // 3
        (w,), wt, slot = p.slab([("w_in", (l,), 0, 8, 3840 + n * 1024 + m * 128, 128)])
        b, fr = ps.claim(6, 2)
        c = 0
        for hi, (a, ln) in enumerate(HALVES[T]):
            for k in range(8):
                t = p.mm(p.PSUM[:, b + hi, 0:ln], w[:, k, :], hx(k, a, ln), k == 0, k == 7, wt, fr, htok,
                         mark=(k == 7 and hi == 1))
                c += 1
                if c == 16:
                    p.used(slot, t)
                    st = p.stage[:, i % 2]
                    stored = (f"gw{i % 2}", 16 * (12 * l + i // 2))
                    S.need(p.zeroed)
                    if i >= 2:
                        S.need(stored)
                    s_ = p.act(p.tv(st, T), p.pv(b, T), ACT.Sigmoid, t)
                    ps.give(b, 2, s_)
                    dst = p.gates[24 * l + i]
                    S.need(s_)
                    S.items.append((lambda e, st=st, dst=dst, q=f"gw{i % 2}": e.dma_start(dst, st).then_inc(p.sems[q], 16),
                                    False, None))
                    done.append((f"gw{i % 2}", 16 * (12 * l + i // 2 + 1)))
                if c % 2 == 0:
                    yield


def first_layer(p, l, X, H, xtok, ada_step):
    V, S, G, P, ps = p.V, p.S, p.G, p.P, p.ps
    A = p.arena
    rs = p.small[:, 64:64 + T]
    ht = p.rms(lambda k: X[:, k], lambda k: H[:, k], T, "norm_mix", l, xtok, rs)
    if l == 0:
        p.zero_rows(ht)
    hx = lambda k, a, n: H[:, k, a:a + n]
    gdone = []
    gwork = work = gate_work(p, l, hx, ht[-1], gdone)
    ps.lim, ps.at = 6, 0
    br, brt = rwkv(p, l, hx, ht[-1], work)
    p.mark("rwpost")
    p.dump(f"rw{l}", br, [brt])
    p.all_wait()
    UU = [A[:, 22000 + 544 * i:22544 + 544 * i] for i in range(4)]
    W = [A[:, 24176 + 544 * i:24720 + 544 * i] for i in range(4)]
    bpt = []

    def both():
        yield from gwork
        yield from pool_work(p, l, hx, ht[-1], UU, W, bpt)

    work = both()
    bd, bdt = attention(p, l, hx, ht[-1], work)
    p.mark("attn")
    p.dump(f"da{l}", bd, [bdt])
    p.fill(1000)
    p.mark("pool")
    o = 6336
    MG = A[:, o:o + 4224].rearrange("p (a t) -> p a t", a=8)
    o += 4224
    SG = [A[:, o + T * i:o + T * i + T] for i in range(3)]
    TM = [A[:, o + T * (3 + i):o + T * (3 + i) + T] for i in range(2)]
    ps.lim = 8
    p.all_wait()
    brs = (lambda k: UU[k][:, 16:544], lambda k: bd[:, k], lambda k: br[:, k])
    tfree = [None, None]
    sfree = [None, None, None]
    mt = []

    def reload(i):
        if i < 24:
            S.need(sfree[i % 3], gdone[i])
            S.items.append((lambda e: e.dma_start(SG[i % 3], p.gates[24 * l + i]).then_inc(p.sems[f"gr{i % 3}"], 16),
                            False, None))

    for i in range(3):
        reload(i)
    for m in range(8):
        for n in range(3):
            it = 3 * m + n
            (uw,), wt, slot = p.slab([("w_branch", (l, n), 0, 4, m * 128, 128)])
            b2, t2 = p.proj(uw, 0, lambda k, a, ln: brs[n](k)[:, a:a + ln], T, [wt, brt, bdt, bpt])
            p.used(slot, t2)
            s_ = (f"gr{it % 3}", 16 * (8 * l + it // 3 + 1))
            i = it % 2
            if n == 0:
                d = p.tt(V, p.tv(MG[:, m], T), p.pv(b2, T), p.tv(SG[it % 3], T), MUL, s_, t2)
                ps.give(b2, 2, d)
                last = d
            else:
                d = p.tt(V, p.tv(TM[i], T), p.pv(b2, T), p.tv(SG[it % 3], T), MUL, s_, t2, tfree[i])
                ps.give(b2, 2, d)
                last = p.tt(G, MG[:, m], MG[:, m], TM[i], ADD, d, last)
                tfree[i] = last
            sfree[it % 3] = d
            reload(it + 3)
        mt.append(last)
    xt = []
    for m in range(8):
        b, t = p.lin("w_out", (l,), m, lambda k, a, ln: MG[:, k, a:a + ln], T, mt)
        x_ = p.tt(V, p.tv(X[:, m], T), p.pv(b, T), p.tv(X[:, m], T), ADD, t)
        ps.give(b, 2, x_)
        xt.append(x_)
    p.mark("merge")
    p.dump(f"x{l}m", X, xt)
    p.all_wait()
    ht = p.rms(lambda k: X[:, k], lambda k: H[:, k], T, "norm_ffn", l, xt, rs)
    HF = A[:, 0:NFF * T].rearrange("p (a t) -> p a t", a=NFF)
    o = NFF * T
    RW = [[A[:, o + 530 * (2 * i + s):o + 530 * (2 * i + s) + 530] for s in range(2)] for i in range(2)]
    o += 4 * 530
    CV = [[A[:, o + T * (2 * i + s):o + T * (2 * i + s) + T] for s in range(2)] for i in range(2)]
    z = [p.zero(V, RW[i][s][:, 0:2]) for i in range(2) for s in range(2)][-1]
    rfree = [[None, None], [None, None]]
    cfree = [None, None]
    hf = []
    for f in range(NFF):
        i = f % 2
        cc = []
        ada_step(1)
        for s in range(2):
            b, t = p.lin("ffn_up", (l,), 22 * s + f, hx, T, ht[-1])
            r, cv = RW[i][s], CV[i][s]
            c1 = p.copy(S, p.tv(r[:, 2:530], T), p.pv(b, T), t, rfree[i][s], z)
            ps.give(b, 2, c1)
            tap = lambda q: p.col("ffn_conv", q * 44 + s * 22 + f, l)
            t3 = p.ts(V, cv, r[:, 2:530], tap(2), MUL, None, None, c1, cfree[i])
            t3 = p.stt(cv, r[:, 1:529], tap(1), cv, MUL, ADD, t3)
            t3 = p.stt(cv, r[:, 0:528], tap(0), cv, MUL, ADD, t3)
            rfree[i][s] = t3
            cc.append(t3)
        s_ = p.act(CV[i][0], CV[i][0], ACT.Silu, cc[0])
        cfree[i] = p.tt(G, HF[:, f], CV[i][0], CV[i][1], MUL, s_, cc[1])
        hf.append(cfree[i])
    ada_step(3 if l else 2)
    xt = []
    for m in range(8):
        b, fr = ps.take(2)
        for k0, nk in ((0, 8), (8, 8), (16, 6)):
            (w,), wt, slot = p.slab([("ffn_down", (l,), k0, nk, m * 128, 128)])
            _, t = p.proj(w, 0, lambda k, a, ln: HF[:, k0 + k, a:a + ln], T, [wt, hf], b, fr,
                          first=k0 == 0, last=k0 == 16)
            p.used(slot, t)
        x_ = p.tt(V, p.tv(X[:, m], T), p.pv(b, T), p.tv(X[:, m], T), ADD, t)
        ps.give(b, 2, x_)
        xt.append(x_)
    p.all_wait()
    p.mark("ffn")
    p.dump(f"x{l}", X, xt)
    return xt




def ada(p, MOD, CD):
    V, S, P, ps = p.V, p.S, p.P, p.ps
    t0 = p.act(CD, p.colr("c_2", 0, 8), ACT.Silu)
    free = [None, None]
    for s in range(48):
        (w,), wt, slot = p.slab([("ada_w_2", (0,), 0, 8, 128 * s, 128)])
        acc = p.adab[:, 128 * (s % 2):128 * (s % 2) + 128]
        t = p.ts(V, acc, w[:, 0, :], CD[:, 0:1], MUL, None, None, wt, t0, free[s % 2])
        for k in range(1, 8):
            t = p.stt(acc, w[:, k, :], CD[:, k:k + 1], acc, MUL, ADD, t)
        p.used(slot, t)
        yield
        b, fr = ps.take(1)
        m = p.mm(p.PSUM[:, b, 0:1], acc, p.c("one")[:, 0:1], True, True, fr, t, mark=True)
        free[s % 2] = m
        if 8 <= s < 16 or 32 <= s < 40:
            o = p.ts(V, MOD[:, s:s + 1], p.PSUM[:, b, 0:1], p.col("ada_b_2", s), ADD, 1.0, ADD, m)
        else:
            o = p.ts(V, MOD[:, s:s + 1], p.PSUM[:, b, 0:1], p.col("ada_b_2", s), ADD, None, None, m)
        ps.give(b, 1, o)


def mixer2(p, XX, UU, xtok, MOD, mtok):
    V, S, G, P, ps = p.V, p.S, p.G, p.P, p.ps
    A = p.arena
    o = 0

    def buf(n):
        nonlocal o
        o += n
        return A[:, o - n:o]

    def f4(n=512):
        return buf(4 * n).rearrange("p (a t) -> p a t", a=4)

    QF, SF, KF, IF, OG, BB = [f4() for _ in range(6)]
    CVI = f4(542)
    CVO = f4()
    OO = f4()
    QK = [(f4(), f4()) for _ in range(2)]
    WK = [buf(512) for _ in range(4)]
    RS = buf(512)
    NB = p.small[:, 610:620]
    ut = p.ln(lambda k: XX[:, k], lambda k: UU[:, k], 8, lambda i: WK[i], RS, xtok,
              lambda k: MOD[:, 8 + k:9 + k], lambda k: MOD[:, k:k + 1], 1024)
    LB = p.small[:, 620:640].rearrange("p (a c) -> p a c", a=5)
    lb0 = p.colr("hgrn_lb_2", 0, 4)
    t = p.tt(V, LB[:, 0], lb0, lb0, SUB)
    t = p.act(LB[:, 0], LB[:, 0], ACT.Exp, t)
    t = p.recip(LB[:, 1], LB[:, 0], t)
    t = p.tt(V, LB[:, 2], LB[:, 0], LB[:, 1], MUL, t)
    tlb = p.tt(V, LB[:, 3], LB[:, 2], LB[:, 2], SUB, t)
    t1lb = p.ts(V, LB[:, 4], LB[:, 3], -1.0, MUL, 1.0, ADD, tlb)
    tnb = p.ts(V, NB[:, 0:4], p.colr("b_in_2", 4, 8), -1.0, MUL)
    ux = lambda k, a, n: UU[:, k, a:a + n]
    z = p.zero(V, CVI[:, :, 0:30])
    tk = {}
    taps = [(q, i) for i in range(31) for q in range(4)]
    ctok = {}

    def conv(n):
        for _ in range(n):
            if not taps:
                return
            q, i = taps.pop(0)
            wcol = p.col("conv_w_2", i * 4 + q)
            src = CVI[:, q, i:i + 512]
            if i == 0:
                ctok[q] = p.ts(V, CVO[:, q], src, wcol, MUL, p.col("conv_b_2", q), ADD, tk[(6, q)])
            else:
                ctok[q] = p.stt(CVO[:, q], src, wcol, CVO[:, q], MUL, ADD, ctok[q])

    for m in list(range(16, 24)) + list(range(16)):
        b, t = p.lin("w_in_2", (0,), m, ux, 512, ut)
        src = p.PSUM[:, b, 0:512]
        bias = p.col("b_in_2", m)
        q, kind = m % 4, m // 4
        if kind == 0:
            r = p.act(QF[:, q], src, ACT.Silu, t, bias=bias)
        elif kind == 1:
            p.act(SF[:, q], src, ACT.Sigmoid, t, bias=bias)
            r = p.act(KF[:, q], src, ACT.Sigmoid, t, tnb, bias=NB[:, q:q + 1], scale=-1.0)
        elif kind == 2:
            r = p.ts(V, IF[:, q], src, bias, ADD, None, None, t)
        elif kind == 3:
            r = p.act(OG[:, q], src, ACT.Silu, t, bias=bias)
        elif kind == 4:
            r = p.ts(V, CVI[:, q, 30:542], src, bias, ADD, None, None, t, z)
        else:
            s_ = p.act(CVO[:, q], src, ACT.Sigmoid, t, bias=bias)
            r = s_
            cv = p.tt(V, CVI[:, q, 30:542], CVI[:, q, 30:542], CVO[:, q], MUL, s_, tk[(4, q)])
            tk[(6, q)] = cv
        ps.give(b, 1, r)
        tk[(kind, q)] = r
        if kind < 4:
            conv(6)
    p.mark("w_in2")
    gb = []
    for q in range(4):
        t = p.ts(V, SF[:, q], SF[:, q], LB[:, 4, q:q + 1], MUL, LB[:, 3, q:q + 1], ADD, tk[(1, q)], t1lb)
        t = p.ts(V, SF[:, q], SF[:, q], 2.0 ** -64, MAX, None, None, t)
        t2 = p.ts(V, KF[:, q], KF[:, q], LB[:, 4, q:q + 1], MUL, None, None, tk[(1, q)])
        t = p.act(SF[:, q], SF[:, q], ACT.Ln, t)
        gb.append(V.do(lambda e, q=q: e.tensor_tensor_scan(BB[:, q], p.c("hrs"), SF[:, q], 0.0, MUL, ADD), t, t2))
    VT = SF
    bf = lambda q, c: BB[:, q, 128 * c:128 * c + 128]
    vt = []
    for c in range(4):
        b, fr = ps.take(1)
        for h in range(4):
            t = p.tr(p.PSUM[:, b, h * 128:h * 128 + 128], IF[:, h, 128 * c:128 * c + 128], 128, fr, tk[(2, 3)], mark=(h == 3))
        t = p.copy(S, VT[:, c, :], p.PSUM[:, b, :], t, gb)
        ps.give(b, 1, t)
        vt.append(t)
    ps.at = 0
    ob = [ps.take(1) for _ in range(4)]
    first = [True] * 4
    lfree = [None, None]
    wfree = [None] * 4
    wi = 0
    def prepare(lev):
        m = 64 >> lev
        nbk = 512 // (2 * m)
        QL, KL = QK[lev % 2]
        zq = p.zero(G, QL, lfree[lev % 2])
        zk = p.zero(G, KL, lfree[lev % 2])
        tl = []
        for h in range(4):
            B = BB[:, h].rearrange("p (n m) -> p n m", m=2 * m)
            ref = B[:, :, m - 1:m].broadcast_to([128, nbk, m])
            ql = QL[:, h].rearrange("p (n m) -> p n m", m=2 * m)[:, :, m:]
            kl = KL[:, h].rearrange("p (n m) -> p n m", m=2 * m)[:, :, :m]
            t1 = p.tt(V, ql, B[:, :, m:], ref, SUB, zq, gb)
            t2 = p.tt(V, kl, ref, B[:, :, :m], SUB, zk)
            tl.append((ql, kl, p.act(ql, ql, ACT.Exp, t1), p.act(kl, kl, ACT.Exp, t2)))
        out = []
        for h, (ql, kl, t1, t2) in enumerate(tl):
            t1 = p.tt(V, ql, ql, QF[:, h].rearrange("p (n m) -> p n m", m=2 * m)[:, :, m:], MUL, t1, tk[(0, 3)])
            t2 = p.tt(V, kl, kl, KF[:, h].rearrange("p (n m) -> p n m", m=2 * m)[:, :, :m], MUL, t2)
            out.append([t1, t2])
        return QL, KL, out

    nxt_ = (QF, KF, [[], [], [], []])
    for lev in [7] + list(range(7)):
        qs, ks, tl = nxt_
        if lev == 7:
            nxt_ = prepare(0)
        elif lev < 6:
            nxt_ = prepare(lev + 1)
        wt_ = []

        def masked(h):
            nonlocal wi
            b, fr = ps.take_from(4, 8)
            for c in range(4):
                t = p.mm(p.PSUM[:, b, 128 * c:128 * c + 128], ks[:, h, 128 * c:128 * c + 128], qs[:, h, 128 * c:128 * c + 128],
                         True, True, fr, tl[h], gb, tk[(0, 3)], mark=(c == 3))
            W = WK[wi % 4].rearrange("p (c t) -> p c t", c=4)
            mk = p.c("hm")[:, lev * 128:lev * 128 + 128].unsqueeze(1).broadcast_to([128, 4, 128])
            mt = p.tt(V, W, p.PSUM[:, b, :].rearrange("p (c t) -> p c t", c=4), mk, MUL, t, wfree[wi % 4])
            ps.give(b, 1, mt)
            wi += 1
            return wi - 1, W, mt

        def gather(h, i, W, mt):
            for c in range(4):
                t2 = p.mm(p.PSUM[:, ob[h][0], 128 * c:128 * c + 128], VT[:, c, h * 128:h * 128 + 128], W[:, c],
                          first[h] and c == 0, False, mt, vt, ob[h][1], mark=(c == 3))
            first[h] = False
            wfree[i % 4] = t2

        held = []
        for h in range(4):
            held.append((h, *masked(h)))
            if h:
                gather(*held.pop(0))
            conv(1)
        gather(*held.pop(0))
        if lev < 7:
            lfree[lev % 2] = P.last()
    tq = []
    QL, KL = QK[1][0], QK[1][1]
    for h in range(4):
        t = p.act(QL[:, h], BB[:, h], ACT.Exp, lfree)
        tq.append(p.tt(V, QL[:, h], QL[:, h], QF[:, h], MUL, t))
    DE = p.small[:, 0:16].rearrange("p (a c) -> p a c", a=4)
    td = p.act(DE, BB[:, :, 127::128], ACT.Exp, gb)
    tke = []
    for h in range(4):
        B = BB[:, h].rearrange("p (n m) -> p n m", m=128)
        k_ = KL[:, h].rearrange("p (n m) -> p n m", m=128)
        t = p.tt(V, k_, B[:, :, 127:128].broadcast_to([128, 4, 128]), B, SUB, lfree)
        t = p.act(k_, k_, ACT.Exp, t)
        tke.append(p.tt(V, KL[:, h], KL[:, h], KF[:, h], MUL, t))
    KT = IF
    kt = []
    for c in range(3):
        b, fr = ps.take_from(4, 8)
        for h in range(4):
            t = p.tr(p.PSUM[:, b, h * 128:h * 128 + 128], KL[:, h, 128 * c:128 * c + 128], 128, fr, tke, mark=(h == 3))
        t = p.copy(S, KT[:, c, :], p.PSUM[:, b, :], t, vt)
        ps.give(b, 1, t)
        kt.append(t)
    ST = [WK[i].rearrange("p (h v) -> p h v", h=4) for i in range(2)]
    st = None
    for c in range(1, 4):
        b, fr = ps.take_from(4, 8)
        for h in range(4):
            t = p.mm(p.PSUM[:, b, h * 128:h * 128 + 128], KT[:, c - 1, h * 128:h * 128 + 128],
                     VT[:, c - 1, h * 128:h * 128 + 128], True, True, fr, kt, mark=(h == 3))
        pvw = p.PSUM[:, b, :].rearrange("p (h v) -> p h v", h=4)
        cur, nxt = ST[(c - 1) % 2], ST[c % 2]
        if c == 1:
            st = p.copy(V, nxt, pvw, t, wfree)
        else:
            d = DE[:, :, c - 1:c].broadcast_to([128, 4, 128])
            x_ = p.tt(V, nxt, cur, d, MUL, st, td, wfree)
            st = p.tt(V, nxt, nxt, pvw, ADD, x_, t)
        ps.give(b, 1, st)
        for h in range(4):
            t2 = p.mm(p.PSUM[:, ob[h][0], 128 * c:128 * c + 128], nxt[:, h], QL[:, h, 128 * c:128 * c + 128],
                      False, c == 3, st, tq, mark=(h == 3))
        wfree = [t2]
    conv(200)
    p.mark("hgrn")
    sq = [p.act(KL[:, h], p.PSUM[:, ob[h][0], 0:512], ACT.Square, t2, kt) for h in range(4)]
    ha = []
    for h in range(4):
        b, fr = ps.take_from(4, 8)
        t = p.mm(p.PSUM[:, b, 0:512], p.c("one"), KL[:, h], True, True, fr, sq[h], mark=True)
        t = p.rstd(BB[:, h], b, 512, 1.0 / 128, 1e-5, t, tke, tq)
        t = p.stt(BB[:, h], BB[:, h], p.col("hgrn_norm_w_2"), OG[:, h], MUL, MUL, t, tk[(3, h)])
        t = p.tt(V, OO[:, h], p.PSUM[:, ob[h][0], 0:512], BB[:, h], MUL, t)
        ha.append(t)
    for h in range(4):
        ps.give(ob[h][0], 1, ha[h], sq[h])
    hb = p.ln(lambda k: CVO[:, k], lambda k: QF[:, k], 4, lambda i: WK[2 + i], RS, [ctok[q] for q in range(4)] ,
              lambda k: p.col("conv_ln_g_2", k), lambda k: p.col("conv_ln_b_2", k), 512, ACT.Silu)
    p.dump("ha", OO, ha)
    p.dump("hb", QF, hb)
    xt = []
    for m in range(8):
        b, t = p.lin("w_out_2", (0,), m, lambda k, a, n: (OO if k < 4 else QF)[:, k % 4, a:a + n], 512, [ha, hb])
        q = p.ts(V, CVI[:, m % 4, 0:512], p.PSUM[:, b, 0:512], p.col("b_out_2", m), ADD, MOD[:, 16 + m:17 + m], MUL, t)
        ps.give(b, 1, q)
        xt.append(p.stt(XX[:, m], XX[:, m], ALPHA, CVI[:, m % 4, 0:512], MUL, ADD, q))
    p.all_wait()
    p.mark("wout2")
    yt = p.ln(lambda k: XX[:, k], lambda k: UU[:, k], 8, lambda i: WK[i], RS, xt,
              lambda k: p.col("ln1_g_2", k), lambda k: p.col("ln1_b_2", k), 1024)
    p.all_wait()
    return yt


def moe(p, XX, UU, xtok, MOD):
    V, S, G, P, ps = p.V, p.S, p.G, p.P, p.ps
    A = p.arena
    o = 0

    def buf(n):
        nonlocal o
        o += n
        return A[:, o - n:o]

    WK = [buf(512) for _ in range(2)]
    RS = buf(512)
    R = [buf(64).rearrange("p (t g e) -> p t g e", t=4, g=4) for _ in range(10)]
    r4 = [buf(16).rearrange("p (t g) -> p t g", t=4) for _ in range(8)]
    r1 = [buf(4).rearrange("p (t g) -> p t g", t=4) for _ in range(4)]
    ut = p.ln(lambda k: XX[:, k], lambda k: UU[:, k], 8, lambda i: WK[i], RS, xtok,
              lambda k: MOD[:, 32 + k:33 + k], lambda k: MOD[:, 24 + k:25 + k], 1024)
    rw = p.colr("router_w_2", 0, 128).rearrange("p (k e) -> p k e", k=8)
    b, fr = ps.take(1)
    for i in range(4):
        for k in range(8):
            t = p.mm(p.PSUM[:, b, 16 * i:16 * i + 16], UU[:, k, 128 * i:128 * i + 128], rw[:, k, :], k == 0, k == 7,
                     fr, ut, mark=(k == 7))
    s, sb, rank, cmpb, inv, sel, cmb = R[0], R[1], R[2], R[3], R[4], R[5], R[6]
    f = lambda x: x.rearrange("p t g e -> p (t g e)")
    t = p.act(f(s), p.PSUM[:, b, 0:64], ACT.Sigmoid, t)
    ps.give(b, 1, t)
    bias = p.colr("router_bias_2", 0, 16).unsqueeze(1).broadcast_to([128, 4, 16])
    t = p.tt(V, sb.rearrange("p t g e -> p t (g e)"), s.rearrange("p t g e -> p t (g e)"), bias, ADD, t)
    G0, tp = r4[0], r4[1]
    pairs = [(i, j) for i in range(4) for j in range(i + 1, 4)]
    for n, (i, j) in enumerate(pairs):
        d = G0 if n == 0 else tp
        t = p.tt(V, d, sb[:, :, :, i], sb[:, :, :, j], ADD, t)
        if n:
            t = p.tt(V, G0, G0, tp, MAX, t)
    gm = r1[0]
    t = V.do(lambda e: e.tensor_reduce(gm[:, :, 0], G0, AX.X, MAX), t)
    gs, left = r4[2], r1[1]
    t = p.tt(V, gs, G0, gm.broadcast_to([128, 4, 4]), ALU.is_ge, t)
    t = p.ts(V, left, gs[:, :, 0:1], -1.0, MUL, 1.0, ADD, t)
    for g in range(1, 4):
        t = p.tt(V, gs[:, :, g:g + 1], gs[:, :, g:g + 1], left, MUL, t)
        if g < 3:
            t = p.tt(V, left, left, gs[:, :, g:g + 1], SUB, t)
    t = p.zero(V, f(rank), t)
    for i, j in pairs:
        c1, c2 = r4[3], r4[4]
        t = p.tt(V, c1, sb[:, :, :, j], sb[:, :, :, i], ALU.is_gt, t)
        t = p.tt(V, rank[:, :, :, i], rank[:, :, :, i], c1, ADD, t)
        t = p.ts(V, c2, c1, -1.0, MUL, 1.0, ADD, t)
        t = p.tt(V, rank[:, :, :, j], rank[:, :, :, j], c2, ADD, t)
    t = p.ts(V, f(sel), f(rank), 1.5, ALU.is_lt, None, None, t)
    t = p.tt(V, sel, sel, gs.unsqueeze(3).broadcast_to([128, 4, 4, 4]), MUL, t)
    t = p.tt(V, f(cmb), f(sel), f(s), MUL, t)
    sm = r1[2]
    t = V.do(lambda e: e.tensor_reduce(sm[:, :, 0], cmb.rearrange("p t g e -> p t (g e)"), AX.X, ADD), t)
    t = p.recip(r1[3], sm, t)
    c3 = cmb.rearrange("p t g e -> p t (g e)")
    t = p.tt(V, c3, c3, r1[3].broadcast_to([128, 4, 16]), MUL, t)
    sf = f(sel)
    b, fr = ps.take(1)
    t1 = p.mm(p.PSUM[:, b, 0:64], p.c("tri"), sf, True, True, fr, t, mark=True)
    t2 = p.mm(p.PSUM[:, b, 128:192], p.c("one"), sf, True, True, mark=True)
    q3 = lambda x: x.rearrange("p t g e -> p t (g e)")
    slot, tot, cs, ra, rb = q3(R[7]), q3(R[8]), R[9], q3(R[3]), q3(R[4])
    t = p.copy(V, f(R[7]), p.PSUM[:, b, 0:64], t1, t2, t)
    t = p.copy(V, f(R[8]), p.PSUM[:, b, 128:192], t2, t)
    ps.give(b, 1, t)
    e16 = [buf(16) for _ in range(5)]
    run, nb_, ci, tmp, rst = e16
    m64 = buf(64)
    t = p.copy(V, run, tot[:, 0], t)
    for i in range(1, 4):
        t = p.tt(V, slot[:, i], slot[:, i], run, ADD, t)
        t = p.tt(V, run, run, tot[:, i], ADD, t)
    t = p.ts(V, nb_, run, 0.5, ALU.is_gt, None, None, t)
    for i in range(1, 4):
        t = p.ts(V, tmp, run, 128.0 * i + 0.5, ALU.is_gt, None, None, t)
        t = p.tt(V, nb_, nb_, tmp, ADD, t)
    t = V.do(lambda e: e.memset(rst, 1.0), t)
    t = V.do(lambda e: e.tensor_tensor_scan(ci, rst, nb_, 0.0, MUL, ADD), t)
    t = p.tt(V, tmp, ci, nb_, SUB, t)
    t = p.ts(V, tmp, tmp, 128.0, MUL, None, None, t)
    t = p.tt(V, slot, slot, tmp.unsqueeze(1).broadcast_to([128, 4, 16]), ADD, t)
    t = V.do(lambda e: e.memset(m64, 1.0), t)
    t = V.do(lambda e: e.memset(m64[:, 0:64:16], 0.0), t)
    t = V.do(lambda e: e.tensor_tensor_scan(f(cs), m64, sf, 0.0, MUL, ADD), t)
    CS = [buf(4) for _ in range(2)]
    SL = buf(8)
    for n in range(2):
        t = p.ts(V, f(R[3]), f(cs), float(n + 1), ALU.is_equal, None, None, t)
        t = p.tt(V, f(R[3]), f(R[3]), sf, MUL, t)
        t = p.tt(V, f(R[4]), f(R[3]), f(R[7]), MUL, t)
        t = V.do(lambda e, n=n: e.tensor_reduce(SL[:, 4 * n:4 * n + 4], rb, AX.X, ADD), t)
        t = p.tt(V, f(R[4]), f(R[3]), f(cmb), MUL, t)
        t = V.do(lambda e, n=n: e.tensor_reduce(CS[n], rb, AX.X, ADD), t)
    tix = p.copy(V, p.idx, SL, t)
    cmp3 = buf(NB * 16).rearrange("p (b e) -> p b e", b=NB)
    ebf = buf(NB)
    t = p.tt(V, cmp3, ci.unsqueeze(1).broadcast_to([128, NB, 16]), p.c("bi").unsqueeze(2).broadcast_to([128, NB, 16]),
             ALU.is_le, tix)
    t = V.do(lambda e: e.tensor_reduce(ebf, cmp3, AX.X, ADD), t)
    t = p.ts(V, ebf, ebf, 15.0, MIN, None, None, t)
    teb = p.copy(V, p.eb, ebf, t)

    rg = p.ring.rearrange("p s n -> p (s n)")
    G_ = [rg[:, 1024 * i:1024 * i + 1024] for i in range(2)]
    UB = [rg[:, 2048 + 1024 * i:3072 + 1024 * i].rearrange("p (k t) -> p k t", k=8) for i in range(2)]
    YB = [rg[:, 4096 + 1024 * i:5120 + 1024 * i] for i in range(2)]
    HB = [rg[:, 6144 + 512 * i:6656 + 512 * i] for i in range(2)]
    HT = [rg[:, 7168 + 512 * i:7680 + 512 * i].rearrange("p (k t) -> p k t", k=4) for i in range(2)]
    SI = [rg[:, 8192 + 512 * i:8704 + 512 * i] for i in range(2)]
    base = 5000
    assert o <= base
    WM = [A[:, base + 4096 * i:base + 4096 * i + 4096] for i in range(6)]
    sct = []
    gfree = [None, None]
    for i in range(4):
        b, fr = ps.take(2)
        for k in range(8):
            t = p.tr(p.PSUM[:, b + k // 4, (k % 4) * 128:(k % 4) * 128 + 128], UU[:, k, 128 * i:128 * i + 128], 128,
                     fr, ut, P.last(), mark=(k == 7))
        g = G_[i % 2]
        t = p.copy(S if i % 2 else V, g.rearrange("p (a t) -> p a t", a=2), p.PSUM[:, b:b + 2, :], t, gfree[i % 2])
        ps.give(b, 2, t)
        G.need(t, tix, p.zeroed)
        for n in range(2):
            G.items.append((lambda e, g=g, c=4 * n + i, q=f"sc{i % 2}": e.indirect_dma_start(
                p.ug, bass.IndirectOffsetOnAxis(ap=p.idx[:, c:c + 1], axis=0), g, None).then_inc(p.sems[q], 16),
                False, None))
        gfree[i % 2] = (f"sc{i % 2}", 32 * (i // 2 + 1))
    scattered = [("sc0", 64), ("sc1", 64)]
    D = p.D
    wfree = [None] * 6
    ufree = [None, None]
    p.D.need(teb, p.fence())

    def load_w(bk, parts):
        for part in parts:
            i = (3 * bk + part) % 6
            D.need(wfree[i])
            box = p.box

            def go(e, bk=bk, part=part, i=i):
                if part != 1:
                    box[0] = e.value_load(p.eb[0:1, bk:bk + 1], min_val=0, max_val=15)
                return e.dma_start(WM[i], p.wmoe[part, bass.ds(box[0], 1)].rearrange("a p n -> (a p) n")).then_inc(
                    p.sems[f"mw{i}"], 16)

            D.items.append((go, False, None))

    p.box = [None]

    def wtok(bk, part):
        i = (3 * bk + part) % 6
        return (f"mw{i}", 16 * ((3 * bk + part) // 6 + 1))

    def load_u(bk):
        i = bk % 2
        D.need(scattered, ufree[i])
        D.items.append((lambda e: e.dma_start(G_[i], p.ug[128 * bk:128 * bk + 128, :]).then_inc(p.sems[f"ug{i}"], 16),
                        False, None))

    ubf = [None, None]

    def turn_u(bk):
        i = bk % 2
        b, fr = ps.take(2)
        for k in range(8):
            t = p.tr(p.PSUM[:, b + k // 4, (k % 4) * 128:(k % 4) * 128 + 128], G_[i][:, 128 * k:128 * k + 128], 128,
                     fr, (f"ug{i}", 16 * (bk // 2 + 1)), mark=(k == 7))
        ufree[i] = t
        t1 = p.copy(S, UB[i][:, 0:4, :], p.PSUM[:, b, :].rearrange("p (k t) -> p k t", k=4), t, ubf[i])
        t2 = p.copy(V, UB[i][:, 4:8, :], p.PSUM[:, b + 1, :].rearrange("p (k t) -> p k t", k=4), t, ubf[i])
        ps.give(b, 2, t1, t2)
        return [t1, t2]

    yfree, hfree, htf, sif = [None, None], [None, None], [None, None], [None, None]

    def down(bk, th):
        i = bk % 2
        wd = WM[(3 * bk + 2) % 6].rearrange("p (k n) -> p k n", k=4)
        b, fr = ps.take(2)
        for hf_ in range(2):
            for k in range(4):
                t = p.mm(p.PSUM[:, b + hf_, :], HT[i][:, k, :], wd[:, k, 512 * hf_:512 * hf_ + 512], k == 0, k == 3,
                         fr, th, wtok(bk, 2), mark=(k == 3))
        wfree[(3 * bk + 2) % 6] = t
        htf[i] = t
        t1 = p.copy(S, YB[i][:, 0:512], p.PSUM[:, b, :], t, yfree[i])
        t2 = p.copy(V, YB[i][:, 512:1024], p.PSUM[:, b + 1, :], t, yfree[i])
        ps.give(b, 2, t1, t2)
        G.need(t1, t2)
        G.items.append((lambda e: e.dma_start(p.ys[128 * bk:128 * bk + 128, :], YB[i]).then_inc(p.sems[f"yo{i}"], 16),
                        False, None))
        yfree[i] = (f"yo{i}", 16 * (bk // 2 + 1))

    load_w(0, (0, 1, 2))
    load_u(0)
    load_u(1)
    load_w(1, (0, 1))
    tu = turn_u(0)
    prev = None
    XA = None
    for bk in range(NB):
        i = bk % 2
        wg = WM[(3 * bk) % 6].rearrange("p (k n) -> p k n", k=8)
        wu = WM[(3 * bk + 1) % 6].rearrange("p (k n) -> p k n", k=8)
        b1, fr = ps.take(1)
        for k in range(8):
            t1 = p.mm(p.PSUM[:, b1, :], UB[i][:, k, :], wg[:, k, :], k == 0, k == 7, fr, tu, wtok(bk, 0), mark=(k == 7))
        wfree[(3 * bk) % 6] = t1
        b2, fr = ps.take(1)
        for k in range(8):
            t2 = p.mm(p.PSUM[:, b2, :], UB[i][:, k, :], wu[:, k, :], k == 0, k == 7, fr, wtok(bk, 1), mark=(k == 7))
        wfree[(3 * bk + 1) % 6] = t2
        ubf[i] = t2
        s_ = p.act(SI[i], p.PSUM[:, b1, :], ACT.Silu, t1, sif[i])
        ps.give(b1, 1, s_)
        h_ = p.tt(V, HB[i], p.PSUM[:, b2, :], SI[i], MUL, s_, t2, hfree[i])
        ps.give(b2, 1, h_)
        sif[i] = h_
        if bk + 1 < NB:
            tu = turn_u(bk + 1)
        if prev is not None:
            down(*prev)
        if bk + 1 < NB:
            load_w(bk + 1, (2,))
        b, fr = ps.take(1)
        for k in range(4):
            t = p.tr(p.PSUM[:, b, 128 * k:128 * k + 128], HB[i][:, 128 * k:128 * k + 128], 128, fr, h_, mark=(k == 3))
        hfree[i] = t
        th = p.copy(S, HT[i], p.PSUM[:, b, :].rearrange("p (k t) -> p k t", k=4), t, htf[i])
        ps.give(b, 1, th)
        prev = (bk, th)
        if bk + 2 < NB:
            load_u(bk + 2)
            load_w(bk + 2, (0, 1))
    down(*prev)
    xa = [p.act(XX[:, k], XX[:, k], ACT.Copy, ut, scale=ALPHA) for k in range(8)]
    GB = [WM[j][:, 0:1024] for j in range(4)]
    gf = [None, None]
    xt = [None] * 8
    G.need(yfree[0], yfree[1], wfree)
    for i in range(4):
        for n in range(2):
            G.need(gf[i % 2])
            G.items.append((lambda e, dst=GB[2 * (i % 2) + n], c=4 * n + i, q=f"yg{i % 2}": e.indirect_dma_start(
                dst, None, p.ys, bass.IndirectOffsetOnAxis(ap=p.idx[:, c:c + 1], axis=0)).then_inc(p.sems[q], 16),
                False, None))
        ga, gb = GB[2 * (i % 2)], GB[2 * (i % 2) + 1]
        t = p.ts(V, ga, ga, CS[0][:, i:i + 1], MUL, None, None, (f"yg{i % 2}", 32 * (i // 2 + 1)))
        t = p.stt(ga, gb, CS[1][:, i:i + 1], ga, MUL, ADD, t)
        b, fr = ps.take(2)
        for k in range(8):
            t2 = p.tr(p.PSUM[:, b + k // 4, (k % 4) * 128:(k % 4) * 128 + 128], ga[:, 128 * k:128 * k + 128], 128,
                      fr, t, mark=(k == 7))
        gf[i % 2] = t2
        for k in range(8):
            xt[k] = p.stt(XX[:, k, 128 * i:128 * i + 128], p.PSUM[:, b + k // 4, (k % 4) * 128:(k % 4) * 128 + 128],
                          MOD[:, 40 + k:41 + k], XX[:, k, 128 * i:128 * i + 128], MUL, ADD, t2, xa)
        ps.give(b, 2, xt[7])
    p.all_wait()
    ot = p.ln(lambda k: XX[:, k], lambda k: UU[:, k], 8, lambda i: WK[i], RS, xt,
              lambda k: p.col("ln2_g_2", k), lambda k: p.col("ln2_b_2", k), 1024)
    return ot


def build(nc, xin, cols, cst, cst2, wmoe, outp, dumps=()):
    p = Program()
    ctx = ExitStack()
    with ctx:
        p.cat, nk = const_plan()
        p.cols_at, ncol = col_plan()
        sbt = lambda name, n: ctx.enter_context(nc.sbuf_tensor(name, [128, n], F32))
        Xs, Hs = sbt("X", 8 * T), sbt("H", 8 * T)
        X = Xs[:, :].rearrange("p (k t) -> p k t", k=8)
        H = Hs[:, :].rearrange("p (k t) -> p k t", k=8)
        p.COLS = sbt("COLS", ncol)[:, :]
        p.K = sbt("CST", nk)[:, :]
        p.ring = sbt("RING", NRING * SLAB)[:, :].rearrange("p (s n) -> p s n", s=NRING)
        MOD = sbt("MOD", 48)[:, :]
        p.small = sbt("SMALL", 700)[:, :]
        p.adab = sbt("ADAB", 256)[:, :]
        Sts = sbt("STAGE", 2 * T)
        p.stage = Sts[:, :].rearrange("p (a t) -> p a t", a=2)
        p.arena = sbt("ARENA", 29600)[:, :]
        p.gates = nc.dram_tensor("gates", [48, 128, T], F32).ap()
        p.PSUM = ctx.enter_context(nc.psum_tensor("PS", [128, 8, 512], F32))[:, :, :]

        def take_from(a, z):
            if not a <= p.ps.at < z:
                p.ps.at = a
            return p.ps.take(1)

        p.ps.take_from = take_from
        names = ["pe", "dve", "act", "pool", "sp", "in", "out", "gw0", "gw1", "gr0", "gr1", "gr2", "zr", "sc0", "sc1", "yg0", "yg1"] + \
            [f"mw{i}" for i in range(6)] + ["ug0", "ug1", "yo0", "yo1"] + [f"w{i}" for i in range(NRING)]
        p.sems = {n: ctx.enter_context(nc.semaphore("s_" + n)) for n in names}
        ndump = [0]

        def dump(name, ap, toks):
            if name in dumps:
                d = dumps[name]
                p.D.need(toks)
                p.D.items.append((lambda e: e.dma_start(d, ap).then_inc(p.sems["out"], 16), False, None))
                ndump[0] += 1

        p.dump = dump
        for dst, src in ((Xs[:, :], xin), (p.COLS, cols), (p.K, cst[:, 0:nk])):
            p.D.items.append((lambda e, dst=dst, src=src: e.dma_start(dst, src).then_inc(p.sems["in"], 16), False, None))
        ready = ("in", 48)
        for q in (p.P, p.V, p.S, p.G):
            q.need(ready)
        p.ug = nc.dram_tensor("ug", [NB * 128, 1024], F32).ap()
        p.ys = nc.dram_tensor("ys", [NB * 128, 1024], F32).ap()
        p.idx = ctx.enter_context(nc.sbuf_tensor("IDXI", [128, 8], I32))[:, :]
        p.eb = ctx.enter_context(nc.sbuf_tensor("EBI", [128, NB], I32))[:, :]
        zt = Sts[:, 0:1024]
        z = p.zero(p.G, zt)
        p.zeroed = ("zr", 16 * NB)

        def zero_rows(after):
            p.G.need(z, after)
            for i in range(NB):
                p.G.items.append((lambda e, i=i: e.dma_start(p.ug[128 * i:128 * i + 128, :], zt).then_inc(
                    p.sems["zr"], 16), False, None))

        p.zero_rows = zero_rows
        steps = ada(p, MOD, p.small[:, 600:608])

        def ada_step(n):
            for _ in range(n):
                next(steps, None)

        xt = [ready] * 8
        for l in range(2):
            xt = first_layer(p, l, X, H, xt, ada_step)
        rs = p.small[:, 64:64 + 512]
        XX = Hs[:, 0:4096].rearrange("p (k t) -> p k t", k=8)
        UU = Xs[:, 0:4096].rearrange("p (k t) -> p k t", k=8)
        xt = p.rms(lambda k: X[:, k, 16:528], lambda k: XX[:, k], 512, "norm_final", None, xt, rs)
        p.dump("mid", XX, xt)
        p.all_wait()
        assert next(steps, 0) == 0
        o2 = p.cat["hrs"][0]
        p.D.need(p.fence())
        p.D.items.append((lambda e: e.dma_start(p.K[:, o2:o2 + 1664 + NB], cst2).then_inc(p.sems["in"], 16), False, None))
        for q in (p.P, p.V):
            q.need(("in", 64))
        yt = mixer2(p, XX, UU, xt, MOD, None)
        p.dump("mx", UU, yt)
        ot = moe(p, UU, XX, yt, MOD)
        p.mark("moe")
        p.D.need(ot)
        p.D.items.append((lambda e: e.dma_start(outp, Hs[:, 0:4096]).then_inc(p.sems["out"], 16), False, None))
        p.D.items.append((None, "out", 16 * (1 + ndump[0])))
        p.wmoe = wmoe
        p.wts = nc.dram_tensor("wts", [p.slab_end], F32, kind="ExternalInput").ap()

        block = ctx.enter_context(nc.Block())

        def emit(q):
            def body(eng):
                for fn, a, b in q.items:
                    if fn is None:
                        eng.wait_ge(p.sems[a], b)
                    else:
                        ins = fn(eng)
                        if a:
                            ins.then_inc(p.sems[q.name], 1)
            return body

        block.sync(emit(p.D))
        block.tensor(emit(p.P))
        block.vector(emit(p.V))
        block.scalar(emit(p.S))
        block.gpsimd(emit(p.G))
    return p.slabs


def pack_cols(inp):
    at, n = col_plan()
    c = np.zeros((128, n), np.float32)

    def put(key, a):
        a = np.reshape(a, (-1, 128))
        c[:, at[key]:at[key] + a.shape[0]] = a.T

    for l in range(2):
        for name in ("norm_mix", "norm_ffn", "pool_scale", "da_subln", "rw_mu", "rw_w0", "rw_a0", "rw_k_k",
                     "rw_k_a", "rw_r_k", "rw_lnx_w", "rw_lnx_b", "ffn_conv"):
            put((name, l), inp[name][l])
        o = at[("da_lambda", l)]
        c[0:64, o:o + 4] = inp["da_lambda"][l].T
    for name in ("norm_final", "c_2", "ada_b_2", "b_in_2", "hgrn_lb_2", "hgrn_norm_w_2", "conv_w_2", "conv_b_2",
                 "conv_ln_g_2", "conv_ln_b_2", "b_out_2", "ln1_g_2", "ln1_b_2", "ln2_g_2", "ln2_b_2"):
        put(name, inp[name])
    o = at["router_bias_2"]
    c[:, o:o + 16] = inp["router_bias_2"][None, :]
    o = at["router_w_2"]
    c[:, o:o + 128] = inp["router_w_2"].reshape(8, 128, 16).transpose(1, 0, 2).reshape(128, 128)
    return c


def pack_weights(slabs, inp):
    parts = []
    for pieces in slabs:
        cut = []
        for name, idx, k0, nk, c0, ncol in pieces:
            if name == "wa2":
                a = np.concatenate([inp["rw_w2"][idx[0]], inp["rw_a2"][idx[0]]], axis=0)
            elif name == "pool_w":
                a = inp["pool_w"][idx[0]].reshape(512, 128)
            else:
                a = inp[name]
                for i in idx:
                    a = a[i]
            a = a[k0 * 128:(k0 + nk) * 128, c0:c0 + ncol]
            cut.append(a.reshape(nk, 128, ncol).transpose(1, 0, 2).reshape(128, nk * ncol))
        parts.append(np.concatenate(cut, axis=1).reshape(-1))
    return np.concatenate(parts)


def pack_experts(inp):
    a = [inp["w_gate_2"][0].reshape(16, 8, 128, 512), inp["w_up_2"][0].reshape(16, 8, 128, 512),
         inp["w_down_2"][0].reshape(16, 4, 128, 1024)]
    return np.stack([x.transpose(0, 2, 1, 3).reshape(16, 128, 4096) for x in a])


def kernel(**inputs):
    import concourse.bacc as _bacc
    from concourse.bass_utils import run_bass_kernel_spmd as _run

    inp = {k: np.asarray(v) for k, v in inputs.items()}
    nc = _bacc.Bacc("TRN2", target_bir_lowering=False, num_devices=1)
    cols, cst, cst2 = pack_cols(inp), consts(0), consts(1)
    x = np.concatenate([inp["meta_tokens"], inp["x"][0]], axis=0)
    x = np.ascontiguousarray(x.T.reshape(8, 128, T).transpose(1, 0, 2).reshape(128, 8 * T))
    dr = lambda name, shape, kind: nc.dram_tensor(name, shape, F32, kind=kind).ap()
    xin = dr("xin", x.shape, "ExternalInput")
    cin = dr("cols", cols.shape, "ExternalInput")
    kin = dr("cst", cst.shape, "ExternalInput")
    wm = dr("wmoe", (3, 16, 128, 4096), "ExternalInput")
    kin2 = dr("cst2", cst2.shape, "ExternalInput")
    outp = dr("outp", (128, 4096), "ExternalOutput")
    slabs = build(nc, xin, cin, kin, kin2, wm, outp)
    wts = pack_weights(slabs, inp)
    r = _run(nc, [{"xin": x, "cols": cols, "cst": cst, "cst2": cst2, "wmoe": pack_experts(inp), "wts": wts}], core_ids=[0])
    y = np.asarray(r.results[0]["outp"]).reshape(128, 8, 512)
    return y.transpose(2, 1, 0).reshape(1, 512, 1024)
```

```python
import math
import numpy as np
import concourse.bass as bass
from concourse import mybir
from contextlib import ExitStack

F32 = mybir.dt.float32
F32R = mybir.dt.float32r
I32 = mybir.dt.int32
ALU = mybir.AluOpType
ACT = mybir.ActivationFunctionType
AX = mybir.AxisListType
MUL, ADD, SUB, MAX, MIN = ALU.mult, ALU.add, ALU.subtract, ALU.max, ALU.min

T = 528
TILES = [(0, 16), (16, 128), (144, 128), (272, 128), (400, 128)]
HALVES = {528: [(0, 264), (264, 264)], 512: [(0, 512)]}
ALPHA = 2.0 ** 0.25
NFF = 22
NB = 23
MINB = 8



def col_plan():
    at, n = {}, 0

    def add(name, w):
        nonlocal n
        at[name] = n
        n += w

    for l in range(2):
        for name, w in (("norm_mix", 8), ("norm_ffn", 8), ("pool_scale", 4), ("da_subln", 1), ("rw_mu", 14),
                        ("rw_w0", 4), ("rw_a0", 4), ("rw_k_k", 4), ("rw_k_a", 4), ("rw_r_k", 4),
                        ("rw_lnx_w", 4), ("rw_lnx_b", 4), ("ffn_conv", 132), ("da_lambda", 4)):
            add((name, l), w)
    for name, w in (("norm_final", 8), ("c_2", 8), ("ada_b_2", 48), ("b_in_2", 24), ("hgrn_lb_2", 4),
                    ("hgrn_norm_w_2", 1), ("conv_w_2", 124), ("conv_b_2", 4), ("conv_ln_g_2", 4),
                    ("conv_ln_b_2", 4), ("b_out_2", 8), ("ln1_g_2", 8), ("ln1_b_2", 8), ("ln2_g_2", 8),
                    ("ln2_b_2", 8), ("router_bias_2", 16), ("router_w_2", 128)):
        add(name, w)
    return at, n


def const_plan():
    at, n = {}, 0
    for name, w in (("id", 128), ("one", 128), ("blk", 128), ("mA", 128), ("mAT", 128), ("mO", 128),
                    ("mUs", 128), ("mUi", 128), ("rot", 128), ("cos", T), ("sin", T), ("am", 64),
                    ("ic", 64), ("rs", T)):
        at[name] = (n, w)
        n += w
    m = at["cos"][0]
    for name, w in (("hrs", 512), ("hm", 1024), ("tri", 128), ("bi", NB)):
        at[name] = (m, w)
        m += w
    assert m <= n
    return at, n


def consts(block):
    at, n = const_plan()
    c = np.zeros((128, n), np.float32)

    def put(name, a):
        o, w = at[name]
        c[:, o:o + w] = a

    p = np.arange(128)[:, None]
    q = np.arange(128)[None, :]
    put("id", p == q)
    put("one", 1.0)
    put("blk", p // 64 == q // 64)
    put("mA", (q < p) & (p // 16 == q // 16))
    put("mAT", (q > p) & (p // 16 == q // 16))
    put("mO", (q < p) & (p // 16 != q // 16) & (p // 64 == q // 64))
    put("mUs", (q > p) & (p // 64 == q // 64))
    put("mUi", (q >= p) & (p // 64 == q // 64))
    d, m = p % 64, q % 64
    same = p // 64 == q // 64
    put("rot", -1.0 * (same & (m < 8) & (d == m + 8)) + 1.0 * (same & (m >= 8) & (m < 16) & (d == m - 8)))
    pos = np.arange(T, dtype=np.float32)
    inv = np.float32(500000.0) ** (-np.arange(0, 16, 2, dtype=np.float32) / np.float32(16))
    ang = pos[:, None] * inv[None, :].astype(np.float32)
    C = np.ones((128, T), np.float32)
    S = np.zeros((128, T), np.float32)
    for b in (0, 64):
        for i in range(16):
            C[b + i] = np.cos(ang[:, i % 8])
            S[b + i] = np.sin(ang[:, i % 8])
    if block == 0:
        put("cos", C)
        put("sin", S)
    put("am", np.where(p < 64, -1e30, 0.0))
    ic = np.zeros((4, 16), np.float32)
    for g, w in enumerate((2, 4, 8, 16)):
        ic[g] = np.float32(1) / np.minimum(np.arange(1, 17), w).astype(np.float32)
    put("ic", ic.reshape(1, 64))
    t = np.arange(T)
    put("rs", np.where((t == 0) | ((t >= 16) & ((t - 16) % 64 == 0)), 0.0, 1.0)[None, :])
    if block == 0:
        return c
    t = np.arange(512)
    put("hrs", np.where(t % 128 == 0, 0.0, 1.0)[None, :])
    hm = np.zeros((128, 8, 128))
    for i in range(7):
        m_ = 64 >> i
        hm[:, i] = (p // (2 * m_) == q // (2 * m_)) & (p % (2 * m_) < m_) & (q % (2 * m_) >= m_)
    hm[:, 7] = p == q
    put("hm", hm.reshape(128, 1024))
    put("tri", q > p)
    put("bi", np.arange(NB)[None, :])
    o = at["hrs"][0]
    return c[:, o:o + 1664 + NB].copy()




class Queue:

    def __init__(self, name):
        self.name, self.items, self.n, self.seen = name, [], 0, {}

    def need(self, *toks):
        for t in toks:
            if t is None:
                continue
            if isinstance(t, list):
                self.need(*t)
                continue
            s, v = t
            if self.seen.get(s, 0) < v:
                self.seen[s] = v
                self.items.append((None, s, v))

    def do(self, fn, *toks, mark=True):
        self.need(*toks)
        if mark:
            self.n += 1
        self.items.append((fn, mark, None))
        return (self.name, self.n)

    def dma(self, fn, sem):
        self.items.append((fn, False, sem))

    def last(self):
        return (self.name, self.n)


class Banks:

    def __init__(self):
        self.at, self.lim, self.free, self.busy = 0, 8, [[] for _ in range(8)], [False] * 8

    def take(self, n=1):
        if self.at + n > self.lim:
            self.at = 0
        b = self.at
        self.at = b + n
        return self.claim(b, n)

    def claim(self, b, n):
        for i in range(b, b + n):
            assert not self.busy[i], "bank still in use"
            self.busy[i] = True
        return b, [self.free[i] for i in range(b, b + n)]

    def give(self, b, n, *toks):
        for i in range(b, b + n):
            self.busy[i] = False
            self.free[i] = list(toks)


NRING = 5
NHIGH = 4
SLAB = 1024
ARENA_R = {"ML": (6336, 8 * T), "MH": (13200, 8 * T), "FL": (0, NFF * T), "FH": (NFF * T, 18 * T),
           "UL": (22000, 2176), "PH": (4224, 2112), "BL": (0, 4224), "BH": (17424, 4224),
           "OL": (16504, 2048), "QL": (0, 2048), "GH": (2048, 4096), "HH": (29600 - 8 * T, 8 * T), "UH": (22648, 4096)}


class Program:
    def __init__(self, plan=None):
        self.P, self.V, self.S, self.G, self.D = (Queue(n) for n in ("pe", "dve", "act", "pool", "sp"))
        self.ps = Banks()
        self.slabs, self.plan = [], plan
        self.loads = []
        self.slab_end = 0
        self.ring_use, self.high_use, self.nsplit = [None] * NRING, [None] * NHIGH, 0
        self.halvers = (self.S, self.V)
        self.bg, self.bg_open = None, False

    def slab(self, pieces, split=True):
        i = len(self.slabs)
        self.slabs.append((pieces, split))
        if self.plan is not None:
            assert self.plan[i] == (pieces, split)
        order = self.plan or self.slabs
        while len(self.loads) < min(i + 3, len(order)):
            self.load(*order[len(self.loads)])
        slot, hs, tok = self.loads[i]
        views, o = [], 0
        for (_, _, _, nk, _, nc_) in pieces:
            cut = lambda x: x[:, o:o + nk * nc_].rearrange("p (k c) -> p k c", k=nk)
            views.append((cut(self.highR[:, hs]), cut(self.ringR[:, slot])) if split else cut(self.ring[:, slot]))
            o += nk * nc_
        return views, tok, (slot, hs)

    def load(self, pieces, split):
        j = len(self.loads)
        slot = j % NRING
        assert self.ring_use[slot] != "open"
        n = sum(p[3] * p[5] for p in pieces)
        assert n <= SLAB
        off = self.slab_end
        self.slab_end += 128 * n
        raw, w = self.ring[:, slot, 0:n], self
        self.D.need(self.ring_use[slot])
        self.ring_use[slot] = "open"
        self.D.items.append((lambda eng: eng.dma_start(raw, w.wts[off:off + 128 * n].rearrange(
            "(p n) -> p n", n=n)).then_inc(w.sems[f"w{slot}"], 16), False, None))
        tok = (f"w{slot}", 16 * (j // NRING + 1))
        hs = None
        if split:
            hs = self.nsplit % NHIGH
            self.nsplit += 1
            assert self.high_use[hs] != "open"
            tok = self.halve(self.halvers, self.highR[:, hs, 0:n], self.ringR[:, slot, 0:n], raw, tok, self.high_use[hs])
            self.high_use[hs] = "open"
        self.loads.append((slot, hs, tok))

    def used(self, slot, tok):
        self.ring_use[slot[0]] = tok
        if slot[1] is not None:
            self.high_use[slot[1]] = tok

    def halve(self, engines, high, low, src, *toks):
        t = self.copy(engines[0], high, src, *toks)
        return [t, self.tt(engines[1], low, src, high.bitcast(F32), SUB, t)]

    def mm(self, out, lhsT, rhs, start, stop, *toks, mark=False):
        return self.P.do(lambda e: e.matmul(out, lhsT, rhs, start=start, stop=stop, skip_group_check=True), *toks, mark=mark)

    def tr(self, out, in_, k, *toks, mark=False):
        idn = self.c("id")[0:k, 0:k]
        return self.P.do(lambda e: e.transpose(out, in_, idn), *toks, mark=mark)

    def tt(self, E, out, a, b, op, *toks):
        return E.do(lambda e: e.tensor_tensor(out, a, b, op), *toks)

    def ts(self, E, out, a, s1, op0, s2=None, op1=None, *toks):
        if op1 is None:
            return E.do(lambda e: e.tensor_scalar(out, a, s1, None, op0), *toks)
        return E.do(lambda e: e.tensor_scalar(out, a, s1, s2, op0, op1), *toks)

    def stt(self, out, a, s, b, op0, op1, *toks):
        return self.V.do(lambda e: e.scalar_tensor_tensor(out=out, in0=a, scalar=s, in1=b, op0=op0, op1=op1), *toks)

    def act(self, out, a, f, *toks, bias=0.0, scale=1.0, accum=None):
        kw = {} if accum is None else {"accum_out": accum}
        return self.S.do(lambda e: e.activation(out, a, f, bias=bias, scale=scale, **kw), *toks)

    def copy(self, E, out, a, *toks):
        if E is self.S:
            return E.do(lambda e: e.copy(out, a), *toks)
        return E.do(lambda e: e.tensor_copy(out, a), *toks)

    def zero(self, E, out, *toks):
        return E.do(lambda e: e.memset(out, 0.0), *toks)

    def recip(self, out, a, *toks):
        return self.V.do(lambda e: e.reciprocal(out, a), *toks)

    def c(self, name):
        o, w = self.cat[name]
        return self.K[:, o:o + w]

    def col(self, name, i=0, l=None):
        o = self.cols_at[name if l is None else (name, l)] + i
        return self.COLS[:, o:o + 1]

    def colr(self, name, a, b, l=None):
        o = self.cols_at[name if l is None else (name, l)]
        return self.COLS[:, o + a:o + b]

    def pv(self, b, n):
        return self.PSUM[:, b:b + 2, 0:264] if n == T else self.PSUM[:, b, 0:n]

    def tv(self, ap, n):
        return ap.rearrange("p (a b) -> p a b", a=2) if n == T else ap

    def nb(self, n):
        return 2 if n == T else 1

    def proj(self, w, m0, rhs, n, toks, b=None, free=None, first=True, last=True):
        if b is None:
            b, free = self.ps.take(self.nb(n))
        nk = (w[0] if isinstance(w, tuple) else w).shape[1]
        tok = None
        for hi, (a, ln) in enumerate(HALVES[n]):
            for k in range(nk):
                x = rhs(k, a, ln)
                wk = tuple(v[:, k, m0:m0 + 128] for v in w) if isinstance(w, tuple) else w[:, k, m0:m0 + 128]
                tok = self.mm3(self.PSUM[:, b + hi, 0:ln], wk, x, first and k == 0, last and k == nk - 1, toks, free,
                               mark=(k == nk - 1 and hi == len(HALVES[n]) - 1))
        return b, tok

    def mm3(self, out, w, x, start, stop, *toks, mark=False):
        if not isinstance(w, tuple):
            return self.mm(out, w, x, start, stop, *toks, mark=mark)
        self.mm(out, w[0], x[0], start, False, *toks)
        self.mm(out, w[0], x[1], False, False)
        return self.mm(out, w[1], x[0], False, stop, mark=mark)

    def lin(self, name, idx, m, rhs, n, toks):
        (w,), wt, slot = self.slab([(name, idx, 0, 8, m * 128, 128)])
        b, t = self.proj(w, 0, rhs, n, [wt, toks])
        self.used(slot, t)
        return b, t

    def fill(self, n=1):
        for _ in range(n):
            if self.bg is None or next(self.bg, self) is self:
                self.bg = None
                return

    def mark(self, name):
        pass

    def fence(self):
        return [q.last() for q in (self.P, self.V, self.S, self.G)]

    def all_wait(self, toks=None):
        toks = toks or self.fence()
        for q in (self.P, self.V, self.S, self.G):
            q.need(toks)

    def when(self, k):
        for q in (self.P, self.V, self.S, self.G, self.D):
            q.items.append(("when", k, None))

    def over(self):
        for q in (self.P, self.V, self.S, self.G, self.D):
            q.items.append(("over", None, None))

    def colsum(self, mat, srcs, n, toks):
        b, free = self.ps.take(self.nb(n))
        tok = None
        for k, s in enumerate(srcs):
            for hi, (a, ln) in enumerate(HALVES[n]):
                tok = self.mm(self.PSUM[:, b + hi, 0:ln], mat, s[:, a:a + ln], k == 0, k == len(srcs) - 1,
                              toks[k], free, mark=(hi == len(HALVES[n]) - 1))
        return b, tok

    def rstd(self, out, b, n, scale, eps, tok, *toks):
        t = self.ts(self.V, self.tv(out, n), self.pv(b, n), scale, MUL, eps, ADD, tok, *toks)
        self.ps.give(b, self.nb(n), t)
        t = self.act(out, out, ACT.Sqrt, t)
        return self.recip(out, out, t)

    def rms(self, src, dst, n, gname, l, toks, rs):
        sq = [self.act(dst(k), src(k), ACT.Square, toks[k]) for k in range(8)]
        b, t = self.colsum(self.c("one"), [dst(k) for k in range(8)], n, sq)
        r = self.rstd(rs, b, n, 1.0 / 1024, 1e-6, t)
        return [self.stt(dst(k), src(k), self.col(gname, k, l), rs, MUL, MUL, r) for k in range(8)]

    def ln(self, src, dst, nt, tmp, rs, toks, scale, shift, width, func=None):
        b, t = self.colsum(self.c("one"), [src(k) for k in range(nt)], 512, toks)
        ctr, sqt = [], []
        bb, fr = None, None
        for k in range(nt):
            c_ = self.stt(dst(k), self.PSUM[:, b, 0:512], -1.0 / width, src(k), MUL, ADD, t)
            ctr.append(c_)
        self.ps.give(b, 1, ctr[-1])
        bb, fr = self.ps.take(1)
        done = [None, None]
        for k in range(nt):
            s_ = self.act(tmp(k % 2), dst(k), ACT.Square, ctr[k], done[k % 2])
            done[k % 2] = self.mm(self.PSUM[:, bb, 0:512], self.c("one"), tmp(k % 2), k == 0, k == nt - 1, s_, fr, mark=True)
        r = self.rstd(rs, bb, 512, 1.0 / width, 1e-5, done[(nt - 1) % 2])
        out = []
        for k in range(nt):
            m = self.tt(self.V, dst(k), dst(k), rs, MUL, r, ctr[k])
            out.append(self.act(dst(k), dst(k), func or ACT.Identity, m, scale=scale(k), bias=shift(k)))
        return out




def rwkv(p, l, hx, htok, work):
    V, S, G, P, ps = p.V, p.S, p.G, p.P, p.ps
    A = p.arena

    def R4(o):
        return A[:, o:o + 2112].rearrange("p (a t) -> p a t", a=4)

    oR, oK, oV, oBV, oAH, oBH, oT1, oLD, oAA, oT2, oT3, oBB, oWA, oGL = [2112 * i for i in range(12)] + [25344, 25872]
    Rf, Kf, Vf, BV, AH, BH, T1, LD, AA, T2, T3, BB = [R4(2112 * i) for i in range(12)]
    WA, GL = A[:, oWA:oWA + T], A[:, oGL:oGL + T]
    full = {i: A[:, 2112 * i:2112 * i + 2112] for i in range(12)}
    fR, fK, fV, fBV, fAH, fBH, fT1, fLD, fAA, fT2, fT3, fBB = [full[i] for i in range(12)]

    raw = [A[:, oT3 + 530 * i:oT3 + 530 * i + 529] for i in range(2)]
    dif = [A[:, oT2 + 530 * i:oT2 + 530 * i + T] for i in range(2)]
    z = [p.zero(V, raw[i][:, 0:1]) for i in range(2)]
    ptok = []
    dst = [Rf[:, i] for i in range(4)] + [Kf[:, i] for i in range(4)] + [Vf[:, i] for i in range(4)] + [WA, GL]
    mixed = [None, None]
    for m in range(14):
        b, t = p.lin("w_in", (l,), 16 + m, hx, T, htok)
        r = raw[m % 2]
        c1 = p.copy(S, p.tv(r[:, 1:529], T), p.pv(b, T), t, mixed[m % 2], z[m % 2])
        ps.give(b, 2, c1)
        d = p.tt(V, dif[m % 2], r[:, 0:T], r[:, 1:529], SUB, c1)
        o = p.stt(dst[m], dif[m % 2], p.col("rw_mu", m, l), r[:, 1:529], MUL, ADD, d)
        mixed[m % 2] = o
        ptok.append(o)
    tr_, tk_, tv_ = ptok[3], ptok[7], ptok[11]
    (ww,), wt, slot = p.slab([("wa2", (l,), 0, 1, 0, 512)], False)
    th = p.act(WA[0:64, :], WA[0:64, :], ACT.Tanh, ptok[12])
    gs = p.act(GL, GL, ACT.Sigmoid, ptok[13])
    sg, ag = [], []
    for n in range(4):
        for part, (lo, name, out, acc) in enumerate(((0, "rw_w0", LD, sg), (64, "rw_a0", AA, ag))):
            b, fr = ps.take(2)
            for hi, (a, ln) in enumerate(HALVES[T]):
                t = p.mm(p.PSUM[:, b + hi, 0:ln], ww[lo:lo + 64, 0, n * 128:n * 128 + 128], WA[lo:lo + 64, a:a + ln],
                         True, True, wt, fr, th, ptok[12], mark=True)
            s_ = p.act(p.tv(out[:, n], T), p.pv(b, T), ACT.Sigmoid, t, bias=p.col(name, n, l))
            ps.give(b, 2, s_)
            acc.append(s_)
    p.mark("rwlin")
    p.used(slot, t)
    p.bg = work
    p.halvers = (S, G)
    ld = p.ts(V, fLD, fLD, -math.exp(-0.5), MUL, None, None, sg[-1])
    bt = [V.do(lambda e, n=n: e.tensor_tensor_scan(BB[:, n], p.c("rs"), LD[:, n], 0.0, MUL, ADD), ld) for n in range(4)][-1]
    kk = [p.ts(V, T1[:, n], Kf[:, n], p.col("rw_k_k", n, l), MUL, None, None, tk_) for n in range(4)]
    sq = [p.act(T2[:, n], T1[:, n], ACT.Square, kk[n], ptok[13]) for n in range(4)]
    mx = []
    p.fill(10)
    for n in range(4):
        b, t = p.colsum(p.c("blk"), [T2[:, n]], T, [sq[n]])
        t = p.ts(V, p.tv(T2[:, n], T), p.pv(b, T), 1e-24, MAX, None, None, t)
        ps.give(b, 2, t)
        mx.append(t)
    t = p.act(fT2, fT2, ACT.Sqrt, mx[-1])
    t = p.recip(fT2, fT2, t)
    kkn = p.tt(V, fT1, fT1, fT2, MUL, t)
    k1 = []
    for n in range(4):
        t = p.ts(V, T3[:, n], AA[:, n], -1.0, ADD, p.col("rw_k_a", n, l), MUL, ag[-1], mixed)
        k1.append(p.stt(Kf[:, n], T3[:, n], 1.0, Kf[:, n], ADD, MUL, t))
    p.fill(14)
    bo = []
    for n in range(4):
        t = p.stt(T2[:, n], Rf[:, n], p.col("rw_r_k", n, l), Kf[:, n], MUL, MUL, k1[n], kkn, tr_)
        b, t = p.colsum(p.c("blk"), [T2[:, n]], T, [t])
        t2 = p.tt(V, p.tv(BV[:, n], T), p.pv(b, T), p.tv(Vf[:, n], T), MUL, t, tv_)
        ps.give(b, 2, t2)
        bo.append(t2)
    p.fill(16)
    sb = p.tt(V, fT3, fBB, fLD, SUB, bt, k1[-1])
    e1 = p.act(fT3, fT3, ACT.Exp, sb)
    ah = p.stt(fAH, fT1, -1.0, fT3, MUL, MUL, e1, kkn)
    be = p.tt(V, fT1, fT1, fAA, MUL, ah)
    e2 = p.act(fT2, fBB, ACT.Exp, bo[-1], scale=-1.0)
    bh = p.tt(V, fBH, fT1, fT2, MUL, e2, be)
    kh = p.tt(V, fK, fK, fT2, MUL, e2, bo[-1])
    e3 = p.act(fLD, fBB, ACT.Exp, sb)
    rh = p.tt(V, fR, fR, fLD, MUL, e3, bo[-1])
    DE = p.small[:, 0:36].rearrange("p (a c) -> p a c", a=4)
    de = p.copy(V, DE, LD[:, :, 15::64], e3)
    ready = [ah, bh, kh, rh, de]

    p.mark("rwpre")
    o = oT1

    def buf(n=512):
        nonlocal o
        o += n
        return A[:, o - n:o]

    v4 = lambda x: x.rearrange("p (a t) -> p a t", a=4)
    bA, bAT, bO, bPT, bNT, bQT, bC, bD, bP, bQ, bM = [v4(buf()) for _ in range(11)]
    bET = bM
    VT = v4(buf())
    BZ, KZ = [buf(1024).rearrange("p (g a t) -> p g a t", g=2, a=4) for _ in range(2)]
    BT, KT = [buf(1024).rearrange("p (c a t) -> p c a t", c=2, a=4) for _ in range(2)]
    U = [buf(1024).rearrange("p (a b c d) -> p a b c d", a=4, b=2, c=2) for i in range(3)]
    FT, HT, GT, Y0 = [v4(buf()) for x in range(4)]
    SB = [v4(buf()) for i in range(2)]
    if o > oGL:
        assert o <= 29600 - T
        GL2 = A[:, 29600 - T:29600]
        cg = p.copy(S, GL2, GL, gs)
    else:
        GL2, cg = GL, gs
    p.all_wait()

    def bc(ap, n):
        return ap.unsqueeze(1).broadcast_to([ap.shape[0], 4, n])

    st = p.zero(G, SB[0])
    zz = [p.zero(G, BZ), p.zero(G, KZ), p.zero(G, BT), p.zero(G, KT)]
    cur = 0
    last_mm = None
    for j, (t0, n) in enumerate(TILES):
        tk = slice(t0, t0 + n)
        ck = range(max(1, n // 64))
        cw = min(n, 64)

        def group4(pairs, *toks, fill=1):
            p.fill(fill)
            b, fr = ps.take(1)
            t = None
            for q in range(4):
                lst = pairs(q)
                for i, (lh, rh_) in enumerate(lst):
                    w_ = rh_.shape[-1] if len(rh_.shape) == 2 else rh_.shape[-1] * rh_.shape[-2]
                    t = p.mm(p.PSUM[0:lh.shape[-1], b, q * 128:q * 128 + w_], lh, rh_, i == 0, i == len(lst) - 1,
                             fr, *toks, mark=(q == 3 and i == len(lst) - 1))
            return b, t

        def view(b, m=n, w=n):
            return v4(p.PSUM[0:m, b, :])[:, :, 0:w]

        bz, kz = [], []
        for g in range(2):
            lo = 64 * g
            bz.append(p.copy(S, BZ[lo:lo + 64, g, :, 0:n], BH[lo:lo + 64, :, tk], ready, zz, last_mm))
            kz.append(p.copy(V, KZ[lo:lo + 64, g, :, 0:n], Kf[lo:lo + 64, :, tk], ready, zz, last_mm))
        tmt = []
        for src, kind in ((BH, 0), (Kf, 1), (Vf, 2), (AH, 3)):
            b, fr = ps.take(1)
            for q in range(4):
                t = p.tr(p.PSUM[0:n, b, q * 128:q * 128 + 128], src[:, q, tk], 128, fr, ready, tv_, mark=(q == 3))
            if kind < 2:
                tc = []
                for c in ck:
                    rows = slice(64 * c, 64 * c + cw)
                    tc.append(p.copy(S, (BT, KT)[kind][rows, c], v4(p.PSUM[rows, b, :]), t, zz, last_mm))
                t = tc
            elif kind == 2:
                t = p.copy(S, VT[0:n], view(b, n, 128), t, last_mm)
            else:
                for g in range(2):
                    t = p.copy(V, U[0][0:n, :, 0, g, :], view(b, n, 128)[:, :, 64 * g:64 * g + 64], t, last_mm)
            ps.give(b, 1, t)
            tmt.append(t)
        gt_last = []
        for g in range(2):
            lo = 64 * g
            pr = P.last()
            b, t = group4(lambda q: [(BZ[:, g, q, 0:n], AH[:, q, tk])], bz)
            tM = p.tt(V, bM[0:n, :, 0:n], view(b), bc(p.c("mUs")[0:n, 0:n], n), MUL, t, pr)
            tAT = p.tt(V, bAT[0:n, :, 0:n], view(b), bc(p.c("mAT")[0:n, 0:n], n), MUL, t)
            ps.give(b, 1, tAT)
            b, t = group4(lambda q: [(KZ[:, g, q, 0:n], AH[:, q, tk])], kz, fill=0)
            tNT = p.tt(V, bNT[0:n, :, 0:n], view(b), bc(p.c("mUs")[0:n, 0:n], n), MUL, t)
            ps.give(b, 1, tNT)
            p.fill(1)
            b, fr = ps.take(1)
            for q in range(4):
                t = p.tr(p.PSUM[0:n, b, q * 128:q * 128 + n], bM[0:n, q, 0:n], n, fr, tM, mark=(q == 3))
            tA = p.tt(V, bA[0:n, :, 0:n], view(b), bc(p.c("mA")[0:n, 0:n], n), MUL, t)
            tO = p.tt(V, bO[0:n, :, 0:n], view(b), bc(p.c("mO")[0:n, 0:n], n), MUL, t)
            ps.give(b, 1, tO)
            b, t = group4(lambda q: [(bNT[0:n, q, 0:n], VT[0:n, q, :])], tNT, tmt[2], fill=0)
            tnv = p.copy(S, U[0][0:n, :, 1, g, :], view(b, n, 128)[:, :, lo:lo + 64], t, last_mm)
            ps.give(b, 1, tnv)
            b1, t1 = group4(lambda q: [(bAT[0:n, q, 0:n], bA[0:n, q, 0:n])], tAT, tA)
            b2, t2 = group4(lambda q: [(bA[0:n, q, 0:n], bAT[0:n, q, 0:n])], fill=0)
            tC = p.copy(V, bC[0:n, :, 0:n], view(b1), t1)
            ps.give(b1, 1, tC)
            tD = p.copy(S, bD[0:n, :, 0:n], view(b2), t2)
            ps.give(b2, 1, tD)
            tP = p.tt(V, bP[0:n, :, 0:n], bAT[0:n, :, 0:n], bc(p.c("id")[0:n, 0:n], n), ADD, tAT)
            b, t = group4(lambda q: [(BZ[:, g, q, 0:n], Rf[:, q, tk])], fill=0)
            tPT = p.tt(V, bPT[0:n, :, 0:n], view(b), bc(p.c("mUi")[0:n, 0:n], n), MUL, t)
            ps.give(b, 1, tPT)
            b2, t2 = group4(lambda q: [(bD[0:n, q, 0:n], bC[0:n, q, 0:n])], tD, tC, fill=0)
            b1, t1 = group4(lambda q: [(bC[0:n, q, 0:n], bD[0:n, q, 0:n])], fill=0)
            b3, t3 = group4(lambda q: [(bC[0:n, q, 0:n], bP[0:n, q, 0:n])], tP, fill=0)
            tA4 = p.copy(V, bA[0:n, :, 0:n], view(b2), t2)
            ps.give(b2, 1, tA4)
            tAT4 = p.copy(S, bAT[0:n, :, 0:n], view(b1), t1, tP)
            ps.give(b1, 1, tAT4)
            tQ = p.tt(V, bQ[0:n, :, 0:n], view(b3), bP[0:n, :, 0:n], ADD, t3, tP)
            ps.give(b3, 1, tQ)
            b, t = group4(lambda q: [(KZ[:, g, q, 0:n], Rf[:, q, tk])], fill=0)
            tQT = p.tt(V, bQT[0:n, :, 0:n], view(b), bc(p.c("mUi")[0:n, 0:n], n), MUL, t)
            ps.give(b, 1, tQT)
            b2, t2 = group4(lambda q: [(bAT[0:n, q, 0:n], bA[0:n, q, 0:n])], tAT4, tA4, fill=0)
            b3, t3 = group4(lambda q: [(bA[0:n, q, 0:n], bQ[0:n, q, 0:n])], tQ, fill=0)
            tC = p.copy(S, bC[0:n, :, 0:n], view(b2), t2)
            ps.give(b2, 1, tC)
            tP = p.tt(V, bP[0:n, :, 0:n], view(b3), bQ[0:n, :, 0:n], ADD, t3, tQ)
            ps.give(b3, 1, tP)
            b3, t3 = group4(lambda q: [(bC[0:n, q, 0:n], bP[0:n, q, 0:n])], tC, tP, fill=1)
            tQ = p.tt(V, bQ[0:n, :, 0:n], view(b3), bP[0:n, :, 0:n], ADD, t3, tP)
            ps.give(b3, 1, tQ)
            rhs = lambda i: (lambda q: U[i][0:n, q, :, g, :])
            b1, t1 = group4(lambda q: [(bO[0:n, q, 0:n], bQ[0:n, q, 0:n])], tQ, tO, fill=1)
            b3, t3 = group4(lambda q: [(bQ[0:n, q, 0:n], rhs(0)(q))], tnv, tmt[3], fill=0)
            tET = p.copy(V, bET[0:n, :, 0:n], view(b1), t1)
            ps.give(b1, 1, tET)
            uv = lambda b: p.PSUM[0:n, b, :].rearrange("p (a b d) -> p a b d", a=4, b=2)
            us = lambda i: U[i][0:n, :, :, g, :]
            tR = p.copy(S, us(2), uv(b3), t3, last_mm)
            ps.give(b3, 1, tR)
            tx, src = tR, 2
            for dst in (1, 0, 1):
                b3, t3 = group4(lambda q: [(bET[0:n, q, 0:n], rhs(src)(q))], tET, tx, fill=1 if src == 2 else 1)
                tx = p.tt(V, us(dst), uv(b3), us(2), ADD, t3, tx, tR)
                ps.give(b3, 1, tx)
                src = dst
            tR3 = tx
            p.fill(1)
            b, fr = ps.take(1)
            for q in range(4):
                t = p.mm(p.PSUM[lo:lo + 64, b, q * 128:q * 128 + n], U[1][0:n, q, 0, g, :], bPT[0:n, q, 0:n],
                         True, True, fr, tR3, tPT, mark=True)
            pvw = v4(p.PSUM[lo:lo + 64, b, :])[:, :, 0:n]
            tG = p.tt(V, GT[lo:lo + 64, :, 0:n], pvw, Rf[lo:lo + 64, :, tk], ADD, t, last_mm)
            ps.give(b, 1, tG)
            b, fr = ps.take(1)
            for q in range(4):
                p.mm(p.PSUM[lo:lo + 64, b, q * 128:q * 128 + n], U[1][0:n, q, 1, g, :], bPT[0:n, q, 0:n], True, False, fr)
                t = p.mm(p.PSUM[lo:lo + 64, b, q * 128:q * 128 + n], VT[0:n, q, lo:lo + 64], bQT[0:n, q, 0:n],
                         False, True, tQT, mark=True)
            pvw = v4(p.PSUM[lo:lo + 64, b, :])[:, :, 0:n]
            tY = p.copy(S, Y0[lo:lo + 64, :, 0:n], pvw, t, last_mm)
            ps.give(b, 1, tY)
            gt_last = gt_last + [tG, tY, tR3]
        rows = slice(0, n)
        pair = lambda q, part: U[1][rows, q, part, :, :].rearrange("p g d -> p (g d)")
        for ci in ck:
            w = cw
            r0 = 64 * ci
            cidx = 0 if j == 0 else 2 * j - 1 + ci
            b, t = group4(lambda q: [(pair(q, 0), BT[rows, ci, q, :])], gt_last, tmt[0], fill=0)
            t = p.tt(V, FT, v4(p.PSUM[:, b, :]), bc(p.c("blk"), 128), MUL, t, last_mm)
            ps.give(b, 1, t)
            tF = p.tt(V, FT, FT, bc(p.c("id"), 128), ADD, t)
            b, t = group4(lambda q: [(BT[rows, ci, q, :], pair(q, 1)), (KT[rows, ci, q, :], VT[rows, q, :])],
                          tmt[1], tmt[2], fill=0)
            tH = p.tt(V, HT, v4(p.PSUM[:, b, :]), bc(p.c("blk"), 128), MUL, t)
            ps.give(b, 1, tH)
            b, t = group4(lambda q: [(SB[cur][:, q, :], GT[:, q, 0:n])], st, fill=1)
            ty = p.tt(V, AH[:, :, t0 + r0:t0 + r0 + w], v4(p.PSUM[:, b, :])[:, :, r0:r0 + w], Y0[:, :, r0:r0 + w], ADD, t)
            ps.give(b, 1, ty)
            b, t = group4(lambda q: [(FT[:, q, :], SB[cur][:, q, :])], tF, fill=0)
            nx = 1 - cur
            t1 = p.tt(V, SB[nx], v4(p.PSUM[:, b, :]), HT, ADD, t, tH)
            ps.give(b, 1, t1)
            dcol = DE[:, :, cidx:cidx + 1].broadcast_to([128, 4, 128])
            st = p.tt(V, SB[nx], SB[nx], dcol, MUL, t1)
            cur = nx
            last_mm = [P.last(), V.last()]
    p.mark("rwcore")
    p.all_wait()
    p.fill(4)
    Yf = AH
    p1 = []
    for n in range(4):
        b, t = p.colsum(p.c("blk"), [Yf[:, n]], T, [None])
        t = p.stt(p.tv(T1[:, n], T), p.pv(b, T), -1.0 / 64, p.tv(Yf[:, n], T), MUL, ADD, t)
        ps.give(b, 2, t)
        p1.append(t)
    sq = [p.act(T2[:, n], T1[:, n], ACT.Square, p1[n]) for n in range(4)]
    rr = []
    p.fill(3)
    for n in range(4):
        b, t = p.colsum(p.c("blk"), [T2[:, n]], T, [sq[n]])
        t = p.ts(V, p.tv(T3[:, n], T), p.pv(b, T), 1.0 / 64, MUL, 64e-5, ADD, t)
        ps.give(b, 2, t)
        rr.append(t)
    t = p.act(fT3, fT3, ACT.Sqrt, rr[-1])
    t = p.recip(fT3, fT3, t)
    yn = p.tt(V, fT1, fT1, fT3, MUL, t)
    outs = []
    p.fill(14)
    (gw,), gwt, slot = p.slab([("rw_g2", (l,), 0, 1, 0, 512)], False)
    for n in range(4):
        b, fr = ps.take(2)
        for hi, (a, ln) in enumerate(HALVES[T]):
            t = p.mm(p.PSUM[:, b + hi, 0:ln], gw[:, 0, n * 128:n * 128 + 128], GL2[:, a:a + ln], True, True, fr, cg, gwt, mark=True)
        u = p.ts(V, T1[:, n], T1[:, n], p.col("rw_lnx_w", n, l), MUL, p.col("rw_lnx_b", n, l), ADD, yn)
        u = p.tt(V, T1[:, n], T1[:, n], BV[:, n], ADD, u)
        u = p.tt(V, p.tv(Rf[:, n], T), p.pv(b, T), p.tv(T1[:, n], T), MUL, u, t)
        ps.give(b, 2, u)
        outs.append(u)
    p.used(slot, P.last())
    while p.bg_open:
        p.fill(1)
    p.bg = None
    p.halvers = (S, V)
    return Rf, outs[-1]


def attention(p, l, hx, htok, work):
    V, S, G, P, ps = p.V, p.S, p.G, p.P, p.ps
    A = p.arena
    o = 2112

    def buf(n):
        nonlocal o
        o += n
        return A[:, o - n:o]

    BD = buf(2112).rearrange("p (a t) -> p a t", a=4)
    Qf = buf(2112).rearrange("p (a t) -> p a t", a=4)
    KZ = buf(4224).rearrange("p (c a t) -> p c a t", c=2, a=4)
    KN = buf(2112).rearrange("p (a t) -> p a t", a=4)
    VT = buf(2560).rearrange("p (a t) -> p a t", a=5)
    raw = [buf(T) for _ in range(2)]
    rt = [buf(T) for _ in range(2)]
    EE = [buf(1056) for _ in range(2)]
    AB = [buf(T) for _ in range(2)]
    AT = [buf(640).rearrange("p (a t) -> p a t", a=5) for _ in range(2)]
    SC = buf(64)
    lam = p.small[:, 40:41]
    lp = p.small[:, 41:43]
    le = p.small[:, 43:45]
    lc = p.colr("da_lambda", 0, 4, l)
    t = p.tt(V, lp, lc[:, 0:4:2], lc[:, 1:4:2], MUL, V.last())
    b, fr = ps.take(1)
    t = p.mm(p.PSUM[:, b, 0:2], p.c("one"), lp, True, True, fr, t, mark=True)
    t = p.act(le, p.PSUM[:, b, 0:2], ACT.Exp, t)
    ps.give(b, 1, t)
    t = p.tt(V, lam, le[:, 0:1], le[:, 1:2], SUB, t)
    linit = 0.8 - 0.6 * math.exp(-0.3 * l)
    tlam = p.ts(V, lam, lam, linit, ADD, None, None, t)

    rdone = [None, None]
    qk = []
    zk = p.zero(G, KZ)
    for m in range(8):
        b, t = p.lin("w_in", (l,), 4 + m, hx, T, htok)
        i = m % 2
        c1 = p.copy(S, p.tv(raw[i], T), p.pv(b, T), t, rdone[i])
        ps.give(b, 2, c1)
        b, t = p.colsum(p.c("rot"), [raw[i]], T, [c1])
        d = p.tt(V, p.tv(rt[i], T), p.pv(b, T), p.tv(p.c("sin"), T), MUL, t)
        ps.give(b, 2, d)
        if m < 4:
            dst = Qf[:, m]
            e = p.tt(G, dst, raw[i], p.c("cos"), MUL, c1)
            rdone[i] = p.tt(V, dst, dst, rt[i], ADD, d, e)
        else:
            e = p.tt(G, raw[i], raw[i], p.c("cos"), MUL, c1, P.last())
            for c in range(2):
                h_ = slice(64 * c, 64 * c + 64)
                rdone[i] = p.tt(V, KZ[h_, c, m - 4], raw[i][h_], rt[i][h_], ADD, d, e, zk)
        qk.append(rdone[i])
    vt = []
    for half in range(2):
        ps.at = 0
        bk = [ps.take(1) for _ in range(5)]
        for kh in range(2):
            (w,), wt, slot = p.slab([("w_in", (l,), 4 * kh, 4, 1536 + half * 256, 256)])
            for j, (t0, n) in enumerate(TILES):
                b, fr = bk[j]
                for k in range(4):
                    t = p.mm3(p.PSUM[:, b, 0:256], hx(4 * kh + k, t0, 128), (w[0][:, k, :], w[1][:, k, :]),
                              kh == 0 and k == 0, kh == 1 and k == 3, wt, htok, fr, mark=(k == 3))
                if kh == 1:
                    c1 = p.copy(S if j % 2 else V, VT[0:n, j, half * 256:half * 256 + 256], p.PSUM[0:n, b, 0:256], t)
                    ps.give(b, 1, c1)
                    vt.append(c1)
            p.used(slot, t)

    p.mark("qkv")
    p.bg = work
    p.halvers = (S, G)
    units = [(j, h) for j in range(5) for h in range(4)]
    e_free, a_free, at_free = [None, None], [None, None], [None, None]
    ot = []
    pend = None

    def scores(u):
        j, h = units[u]
        t0, n = TILES[j]
        nk = t0 + n
        nbk = 4 if nk > 512 else 2
        b, fr = ps.claim(0, 4) if nbk == 4 else ps.claim(2 * (u % 2), 2)
        for c in range(2):
            for s in range(nbk // 2):
                w_ = nk // (nbk // 2)
                t = p.mm(p.PSUM[0:n, b + c * (nbk // 2) + s, 0:w_], Qf[:, h, t0:t0 + n],
                         KZ[:, c, h, s * w_:s * w_ + w_], True, True, fr, qk, zk, mark=True)
        return b, nbk, t

    def soft(u, b, nbk, t):
        j, h = units[u]
        t0, n = TILES[j]
        nk = t0 + n
        w_ = nk // (nbk // 2)
        i = u % 2
        sc = SC[:, 16 * i:16 * i + 16]
        if j > 0:
            vw = p.PSUM[0:64, b + nbk // 2 - 1:b + nbk:nbk // 2, w_ - 64:w_]
            m_ = p.c("am")[0:64, :].unsqueeze(1).broadcast_to([64, 2, 64])
            t = p.tt(V, vw, vw, m_, ADD, t)
        sv = p.PSUM[0:n, b:b + nbk, 0:w_]
        t = V.do(lambda e: e.tensor_reduce(sc[0:n, 0:nbk], sv, AX.X, MAX), t)
        if nbk == 4:
            t = p.tt(V, sc[0:n, 4:6], sc[0:n, 0:4:2], sc[0:n, 1:4:2], MAX, t)
            mxv = sc[0:n, 4:6]
        else:
            mxv = sc[0:n, 0:2]
        t = p.ts(V, sc[0:n, 6:8], mxv, -0.125, MUL, None, None, t)
        et = []
        for c in range(2):
            hb = nbk // 2
            src = p.PSUM[0:n, b + c * hb:b + c * hb + hb, 0:w_] if hb == 2 else p.PSUM[0:n, b + c, 0:w_]
            dst = EE[i][0:n, c * T:c * T + nk]
            if hb == 2:
                dst = dst.rearrange("p (a b) -> p a b", a=2)
            et.append(p.act(dst, src, ACT.Exp, t, e_free[i], bias=sc[0:n, 6 + c:7 + c], scale=0.125,
                            accum=sc[0:n, 8 + c:9 + c]))
        ps.give(b, nbk, et[-1])
        t = p.recip(sc[0:n, 10:12], sc[0:n, 8:10], et[-1])
        t = p.tt(V, sc[0:n, 12:13], sc[0:n, 11:12], lam[0:n, :], MUL, t, tlam)
        t = p.ts(V, EE[i][0:n, T:T + nk], EE[i][0:n, T:T + nk], sc[0:n, 12:13], MUL, None, None, t)
        t = p.stt(AB[i][0:n, 0:nk], EE[i][0:n, 0:nk], sc[0:n, 10:11], EE[i][0:n, T:T + nk], MUL, SUB, t, a_free[i])
        e_free[i] = t
        return t

    def turned(u, t):
        j, h = units[u]
        n = TILES[j][1]
        i = u % 2
        p.fill(2)
        b, fr = ps.claim(4, 2)
        for kt in range(j + 1):
            k0, kn = TILES[kt]
            out = p.PSUM[0:kn, b + 1, 0:n] if kt == 0 else p.PSUM[0:kn, b, (kt - 1) * 128:(kt - 1) * 128 + n]
            tq = p.tr(out, AB[i][0:n, k0:k0 + kn], n, fr, t, mark=(kt == j))
        a_free[i] = tq
        ca = p.copy(S, AT[i][0:16, 0, 0:n], p.PSUM[0:16, b + 1, 0:n], tq, at_free[i])
        if j > 0:
            src = p.PSUM[:, b, 0:128 * j].rearrange("p (a t) -> p a t", a=j)
            ca = [ca, p.copy(S, AT[i][:, 1:j + 1, 0:n], src, tq, at_free[i])]
        return ca

    def summed(u, ca):
        j, h = units[u]
        t0, n = TILES[j]
        i = u % 2
        p.fill(2)
        for kt in range(j + 1):
            kn = TILES[kt][1]
            tq = p.mm(p.PSUM[:, 4, 0:n], VT[0:kn, kt, h * 128:h * 128 + 128], AT[i][0:kn, kt, 0:n],
                      kt == 0, kt == j, ca, vt, mark=(kt == j))
        at_free[i] = tq
        c1 = p.copy(S, BD[:, h, t0:t0 + n], p.PSUM[:, 4, 0:n], tq)
        ps.give(4, 2, c1)
        ot.append(c1)

    prev = None
    for u in range(len(units) + 1):
        if u < len(units):
            sb_ = scores(u)
        if u:
            ca = turned(u - 1, prev)
        if u < len(units):
            prev = soft(u, *sb_)
        if u:
            summed(u - 1, ca)
    outs = []
    tb = ot[-1]
    sq = [p.act(Qf[:, h], BD[:, h], ACT.Square, tb, P.last()) for h in range(4)]
    for h in range(4):
        b, t = p.colsum(p.c("one"), [Qf[:, h]], T, [sq[h]])
        t = p.rstd(KN[:, h], b, T, 1.0 / 128, 1e-5, t)
        t = p.ts(V, KN[:, h], KN[:, h], p.col("da_subln", 0, l), MUL, 1.0 - linit, MUL, t)
        outs.append(p.tt(V, BD[:, h], BD[:, h], KN[:, h], MUL, t))
    return BD, outs[-1]


def pool_work(p, l, hx, htok, UU, W, outs):
    V, S, ps = p.V, p.S, p.ps
    z = [p.zero(V, x[:, 0:16]) for x in UU + W][-1]
    for g in range(4):
        (w,), wt, slot = p.slab([("w_in", (l,), 0, 8, g * 128, 128)])
        b, fr = ps.claim(6, 2)
        c = 0
        for hi, (a, ln) in enumerate(HALVES[T]):
            for k in range(8):
                t = p.mm3(p.PSUM[:, b + hi, 0:ln], (w[0][:, k, :], w[1][:, k, :]), hx(k, a, ln), k == 0, k == 7,
                          wt, fr, htok, mark=(k == 7 and hi == 1))
                c += 1
                if c < 16 and c % 2 == 0:
                    yield
        p.used(slot, t)
        u = UU[g]
        c1 = p.copy(S, p.tv(u[:, 16:544], T), p.pv(b, T), t)
        ps.give(b, 2, c1)
        src, t = u, c1
        for s in range(g + 1):
            d = W[2 * (g % 2) + s % 2]
            sh = 1 << s
            t = p.tt(V, d[:, 16:544], src[:, 16:544], src[:, 16 - sh:544 - sh], ADD, t, z, outs[-2:])
            src = d
        dst = W[2 * (g % 2) + (g + 1) % 2]
        hd = p.tt(V, p.small[:, 640:656], src[:, 16:32], p.c("ic")[:, 16 * g:16 * g + 16], MUL, t)
        t = p.stt(dst[:, 16:544], src[:, 16:544], 1.0 / (2 << g), u[:, 16:544], MUL, SUB, t, hd)
        t = p.tt(V, dst[:, 16:32], p.small[:, 640:656], u[:, 16:32], SUB, t)
        yield
        yield
        (pw,), pwt, slot = p.slab([("pool_w", (l,), g, 1, 0, 128)], False)
        b, fr = ps.claim(6, 2)
        for hi, (a, ln) in enumerate(HALVES[T]):
            t2 = p.mm(p.PSUM[:, b + hi, 0:ln], pw[:, 0, :], dst[:, 16 + a:16 + a + ln], True, True, fr, t, pwt, mark=True)
        p.used(slot, t2)
        t = p.act(p.tv(u[:, 16:544], T), p.pv(b, T), ACT.Copy, t2, scale=p.col("pool_scale", g, l))
        ps.give(b, 2, t)
        outs.append(t)
        yield


def gate_work(p, l, hx, htok, done):
    P, S, ps = p.P, p.S, p.ps
    tok = None
    for i in range(24):
        n, m = i % 3, i // 3
        (w,), wt, slot = p.slab([("w_in", (l,), 0, 8, 3840 + n * 1024 + m * 128, 128)])
        p.bg_open = True
        b, fr = ps.claim(6, 2)
        c = 0
        for hi, (a, ln) in enumerate(HALVES[T]):
            for k in range(8):
                t = p.mm3(p.PSUM[:, b + hi, 0:ln], (w[0][:, k, :], w[1][:, k, :]), hx(k, a, ln), k == 0, k == 7,
                          wt, fr, htok, mark=(k == 7 and hi == 1))
                c += 1
                if c == 16:
                    p.used(slot, t)
                    p.bg_open = False
                    st = p.stage[:, i % 2]
                    stored = (f"gw{i % 2}", 16 * (12 * l + i // 2))
                    S.need(p.zeroed, ("zy", 16 * (NB - MINB)) if l else None)
                    if i >= 2:
                        S.need(stored)
                    s_ = p.act(p.tv(st, T), p.pv(b, T), ACT.Sigmoid, t)
                    ps.give(b, 2, s_)
                    dst = p.gates[24 * l + i]
                    S.need(s_)
                    S.items.append((lambda e, st=st, dst=dst, q=f"gw{i % 2}": e.dma_start(dst, st).then_inc(p.sems[q], 16),
                                    False, None))
                    done.append((f"gw{i % 2}", 16 * (12 * l + i // 2 + 1)))
                if c % 2 == 0:
                    yield


def first_layer(p, l, X, XR, H, HR, xtok, ada_step):
    V, S, G, P, ps = p.V, p.S, p.G, p.P, p.ps
    A = p.arena
    rs = p.small[:, 64:64 + T]
    ht = p.rms(lambda k: X[:, k], lambda k: H[:, k], T, "norm_mix", l, xtok, rs)
    if l == 0:
        p.zero_rows(ht)
        kept = None
    else:
        S.need(xtok)
        S.items.append((lambda e: e.dma_start(p.xkeep, p.Xf).then_inc(p.sems["xs"], 16), False, None))
        kept = ("xs", 16)
    ht = [p.halve((S, V), XR[:, k], HR[:, k], H[:, k], ht, kept) for k in range(8)]
    ht = [ht]
    hx = lambda k, a, n: (XR[:, k, a:a + n], HR[:, k, a:a + n])
    gdone = []
    gwork = work = gate_work(p, l, hx, ht[-1], gdone)
    ps.lim, ps.at = 6, 0
    br, brt = rwkv(p, l, hx, ht[-1], work)
    p.mark("rwpost")
    p.dump(f"rw{l}", br, [brt])
    p.all_wait()
    UU = [A[:, 22000 + 544 * i:22544 + 544 * i] for i in range(4)]
    W = [A[:, 24176 + 544 * i:24720 + 544 * i] for i in range(4)]
    bpt = []

    def both():
        yield from gwork
        yield from pool_work(p, l, hx, ht[-1], UU, W, bpt)

    work = both()
    bd, bdt = attention(p, l, hx, ht[-1], work)
    p.mark("attn")
    p.dump(f"da{l}", bd, [bdt])
    p.fill(1000)
    p.mark("pool")
    o = 6336
    MG = A[:, o:o + 4224].rearrange("p (a t) -> p a t", a=8)
    o += 4224
    SG = [A[:, o + T * i:o + T * i + T] for i in range(3)]
    TM = [A[:, o + T * (3 + i):o + T * (3 + i) + T] for i in range(2)]
    ps.lim = 8
    p.halvers = (S, V)
    p.all_wait()
    S.items.append((lambda e: e.dma_start(p.Xf, p.xkeep if l else p.xin).then_inc(p.sems["xr"], 16), False, None))
    back = ("xr", 16 * (l + 1))
    MR = p.parts["ML"].rearrange("p (a t) -> p a t", a=8)
    MH = p.parts["MH"].rearrange("p (a t) -> p a t", a=8)
    UL = [p.parts["UL"][:, 544 * k + 16:544 * k + 544] for k in range(4)]
    UH = p.parts["PH"].rearrange("p (a t) -> p a t", a=4)
    BL = p.parts["BL"].rearrange("p (a t) -> p a t", a=8)
    BH = p.parts["BH"].rearrange("p (a t) -> p a t", a=8)
    bst = [[p.halve((S, V), UH[:, k], UL[k], UU[k][:, 16:544], bpt) for k in range(4)]]
    for n, x in ((1, bd), (0, br)):
        bst.append([p.halve((S, V), BH[:, 4 * n + k], BL[:, 4 * n + k], x[:, k], bdt, brt) for k in range(4)])
    brs = (lambda k: (UH[:, k], UL[k]), lambda k: (BH[:, 4 + k], BL[:, 4 + k]), lambda k: (BH[:, k], BL[:, k]))
    tfree = [None, None]
    sfree = [None, None, None]
    mt = []

    def reload(i):
        if i < 24:
            S.need(sfree[i % 3], gdone[i])
            S.items.append((lambda e: e.dma_start(SG[i % 3], p.gates[24 * l + i]).then_inc(p.sems[f"gr{i % 3}"], 16),
                            False, None))

    for i in range(3):
        reload(i)
    for m in range(8):
        for n in range(3):
            it = 3 * m + n
            (uw,), wt, slot = p.slab([("w_branch", (l, n), 0, 4, m * 128, 128)])
            b2, t2 = p.proj(uw, 0, lambda k, a, ln: tuple(v[:, a:a + ln] for v in brs[n](k)), T, [wt, bst[n]])
            p.used(slot, t2)
            s_ = (f"gr{it % 3}", 16 * (8 * l + it // 3 + 1))
            i = it % 2
            if n == 0:
                d = p.tt(V, p.tv(MG[:, m], T), p.pv(b2, T), p.tv(SG[it % 3], T), MUL, s_, t2)
                ps.give(b2, 2, d)
                last = d
            else:
                d = p.tt(V, p.tv(TM[i], T), p.pv(b2, T), p.tv(SG[it % 3], T), MUL, s_, t2, tfree[i])
                ps.give(b2, 2, d)
                last = p.tt(G, MG[:, m], MG[:, m], TM[i], ADD, d, last)
                tfree[i] = last
            sfree[it % 3] = d
            reload(it + 3)
        mt.append(p.halve((S, V), MH[:, m], MR[:, m], MG[:, m], last))
    xt = []
    for m in range(8):
        b, t = p.lin("w_out", (l,), m, lambda k, a, ln: (MH[:, k, a:a + ln], MR[:, k, a:a + ln]), T, mt)
        x_ = p.tt(V, p.tv(X[:, m], T), p.pv(b, T), p.tv(X[:, m], T), ADD, t, back)
        ps.give(b, 2, x_)
        xt.append(x_)
    p.mark("merge")
    p.dump(f"x{l}m", X, xt)
    p.all_wait()
    ht = p.rms(lambda k: X[:, k], lambda k: H[:, k], T, "norm_ffn", l, xt, rs)
    HF = A[:, 0:NFF * T].rearrange("p (a t) -> p a t", a=NFF)
    FL = p.parts["FL"].rearrange("p (a t) -> p a t", a=NFF)
    FH = p.parts["FH"].rearrange("p (a t) -> p a t", a=18)
    HH = p.parts["HH"].rearrange("p (a t) -> p a t", a=8)
    o = (NFF + 18) * T
    RW = [[A[:, o + 530 * (2 * i + s):o + 530 * (2 * i + s) + 530] for s in range(2)] for i in range(2)]
    o += 4 * 530
    CV = [[A[:, o + T * (2 * i + s):o + T * (2 * i + s) + T] for s in range(2)] for i in range(2)]
    assert o + 4 * T <= 29600 - 8 * T
    ht = [[p.halve((S, V), HH[:, k], HR[:, k], H[:, k], ht) for k in range(8)]]
    hx = lambda k, a, n: (HH[:, k, a:a + n], HR[:, k, a:a + n])
    if l == 0:
        G.need(gdone)
        p.zero_results()
    z = [p.zero(V, RW[i][s][:, 0:2]) for i in range(2) for s in range(2)][-1]
    rfree = [[None, None], [None, None]]
    cfree = [None, None]
    hf = []

    def gated(f, c0, c1):
        i = f % 2
        s_ = p.act(CV[i][0], CV[i][0], ACT.Silu, c0)
        cfree[i] = p.tt(G, HF[:, f], CV[i][0], CV[i][1], MUL, s_, c1)
        hf.append(cfree[i])

    def parted(f):
        if f < 18:
            hf[f] = p.halve((S, V), FH[:, f], FL[:, f], HF[:, f], hf[f])

    for f in range(NFF):
        i = f % 2
        cc = []
        ada_step(1)
        for s in range(2):
            b, t = p.lin("ffn_up", (l,), 22 * s + f, hx, T, ht[-1])
            r, cv = RW[i][s], CV[i][s]
            c1 = p.copy(S, p.tv(r[:, 2:530], T), p.pv(b, T), t, rfree[i][s], z)
            ps.give(b, 2, c1)
            tap = lambda q: p.col("ffn_conv", q * 44 + s * 22 + f, l)
            t3 = p.ts(V, cv, r[:, 2:530], tap(2), MUL, None, None, c1, cfree[i])
            t3 = p.stt(cv, r[:, 1:529], tap(1), cv, MUL, ADD, t3)
            t3 = p.stt(cv, r[:, 0:528], tap(0), cv, MUL, ADD, t3)
            rfree[i][s] = t3
            cc.append(t3)
        if f:
            gated(f - 1, *pend)
        if f > 1:
            parted(f - 2)
        pend = cc
    gated(NFF - 1, *pend)
    hf = hf[:18] + [p.halve((S, V), HH[:, f - 18], FL[:, f], HF[:, f], hf[f], P.last()) for f in range(18, NFF)]
    fx = lambda f, a, ln: ((FH[:, f] if f < 18 else HH[:, f - 18])[:, a:a + ln], FL[:, f, a:a + ln])
    ada_step(3 if l else 2)
    xt = []
    for m in range(8):
        b, fr = ps.take(2)
        for k0, nk in ((0, 8), (8, 8), (16, 6)):
            (w,), wt, slot = p.slab([("ffn_down", (l,), k0, nk, m * 128, 128)])
            _, t = p.proj(w, 0, lambda k, a, ln: fx(k0 + k, a, ln), T, [wt, hf[k0:k0 + nk]], b, fr,
                          first=k0 == 0, last=k0 == 16)
            p.used(slot, t)
        x_ = p.tt(V, p.tv(X[:, m], T), p.pv(b, T), p.tv(X[:, m], T), ADD, t)
        ps.give(b, 2, x_)
        xt.append(x_)
    p.all_wait()
    p.mark("ffn")
    p.dump(f"x{l}", X, xt)
    return xt




def ada(p, MOD, CD):
    V, S, P, ps = p.V, p.S, p.P, p.ps
    t0 = p.act(CD, p.colr("c_2", 0, 8), ACT.Silu)
    free = [None, None]
    for s in range(48):
        (w,), wt, slot = p.slab([("ada_w_2", (0,), 0, 8, 128 * s, 128)], False)
        acc = p.adab[:, 128 * (s % 2):128 * (s % 2) + 128]
        t = p.ts(V, acc, w[:, 0, :], CD[:, 0:1], MUL, None, None, wt, t0, free[s % 2])
        for k in range(1, 8):
            t = p.stt(acc, w[:, k, :], CD[:, k:k + 1], acc, MUL, ADD, t)
        p.used(slot, t)
        yield
        b, fr = ps.take(1)
        m = p.mm(p.PSUM[:, b, 0:1], acc, p.c("one")[:, 0:1], True, True, fr, t, mark=True)
        free[s % 2] = m
        if 8 <= s < 16 or 32 <= s < 40:
            o = p.ts(V, MOD[:, s:s + 1], p.PSUM[:, b, 0:1], p.col("ada_b_2", s), ADD, 1.0, ADD, m)
        else:
            o = p.ts(V, MOD[:, s:s + 1], p.PSUM[:, b, 0:1], p.col("ada_b_2", s), ADD, None, None, m)
        ps.give(b, 1, o)


def mixer2(p, XX, UU, UR, xtok, MOD):
    V, S, G, P, ps = p.V, p.S, p.G, p.P, p.ps
    A = p.arena
    o = 0

    def buf(n):
        nonlocal o
        o += n
        return A[:, o - n:o]

    def f4(n=512):
        return buf(4 * n).rearrange("p (a t) -> p a t", a=4)

    QF, SF, KF, IF, OG, BB = [f4() for _ in range(6)]
    CVI = f4(542)
    CVO = f4()
    OO = f4()
    QK = [(f4(), f4()) for _ in range(2)]
    assert o - 4096 == ARENA_R["UH"][0]
    UH = p.parts["UH"].rearrange("p (k t) -> p k t", k=8)
    WK = [buf(512) for _ in range(4)]
    RS = buf(512)
    NB = p.small[:, 610:620]
    ut = p.ln(lambda k: XX[:, k], lambda k: UU[:, k], 8, lambda i: WK[i], RS, xtok,
              lambda k: MOD[:, 8 + k:9 + k], lambda k: MOD[:, k:k + 1], 1024)
    LB = p.small[:, 620:640].rearrange("p (a c) -> p a c", a=5)
    lb0 = p.colr("hgrn_lb_2", 0, 4)
    t = p.tt(V, LB[:, 0], lb0, lb0, SUB)
    t = p.act(LB[:, 0], LB[:, 0], ACT.Exp, t)
    t = p.recip(LB[:, 1], LB[:, 0], t)
    t = p.tt(V, LB[:, 2], LB[:, 0], LB[:, 1], MUL, t)
    tlb = p.tt(V, LB[:, 3], LB[:, 2], LB[:, 2], SUB, t)
    t1lb = p.ts(V, LB[:, 4], LB[:, 3], -1.0, MUL, 1.0, ADD, tlb)
    tnb = p.ts(V, NB[:, 0:4], p.colr("b_in_2", 4, 8), -1.0, MUL)
    ut = [p.halve((S, V), UH[:, k], UR[:, k], UU[:, k], ut[k]) for k in range(8)]
    ux = lambda k, a, n: (UH[:, k, a:a + n], UR[:, k, a:a + n])
    z = p.zero(V, CVI[:, :, 0:30])
    tk = {}
    taps = [(q, i) for i in range(31) for q in range(4)]
    ctok = {}

    def conv(n):
        for _ in range(n):
            if not taps:
                return
            q, i = taps.pop(0)
            wcol = p.col("conv_w_2", i * 4 + q)
            src = CVI[:, q, i:i + 512]
            if i == 0:
                ctok[q] = p.ts(V, CVO[:, q], src, wcol, MUL, p.col("conv_b_2", q), ADD, tk[(6, q)])
            else:
                ctok[q] = p.stt(CVO[:, q], src, wcol, CVO[:, q], MUL, ADD, ctok[q])

    for m in list(range(16, 24)) + list(range(16)):
        b, t = p.lin("w_in_2", (0,), m, ux, 512, ut)
        src = p.PSUM[:, b, 0:512]
        bias = p.col("b_in_2", m)
        q, kind = m % 4, m // 4
        if kind == 0:
            r = p.act(QF[:, q], src, ACT.Silu, t, bias=bias)
        elif kind == 1:
            p.act(SF[:, q], src, ACT.Sigmoid, t, bias=bias)
            r = p.act(KF[:, q], src, ACT.Sigmoid, t, tnb, bias=NB[:, q:q + 1], scale=-1.0)
        elif kind == 2:
            r = p.ts(V, IF[:, q], src, bias, ADD, None, None, t)
        elif kind == 3:
            r = p.act(OG[:, q], src, ACT.Silu, t, bias=bias)
        elif kind == 4:
            r = p.ts(V, CVI[:, q, 30:542], src, bias, ADD, None, None, t, z)
        else:
            s_ = p.act(CVO[:, q], src, ACT.Sigmoid, t, bias=bias)
            r = s_
            cv = p.tt(V, CVI[:, q, 30:542], CVI[:, q, 30:542], CVO[:, q], MUL, s_, tk[(4, q)])
            tk[(6, q)] = cv
        ps.give(b, 1, r)
        tk[(kind, q)] = r
        if kind < 4:
            conv(6)
    in_read = P.last()
    p.mark("w_in2")
    gb = []
    for q in range(4):
        t = p.ts(V, SF[:, q], SF[:, q], LB[:, 4, q:q + 1], MUL, LB[:, 3, q:q + 1], ADD, tk[(1, q)], t1lb)
        t = p.ts(V, SF[:, q], SF[:, q], 2.0 ** -64, MAX, None, None, t)
        t2 = p.ts(V, KF[:, q], KF[:, q], LB[:, 4, q:q + 1], MUL, None, None, tk[(1, q)])
        t = p.act(SF[:, q], SF[:, q], ACT.Ln, t)
        gb.append(V.do(lambda e, q=q: e.tensor_tensor_scan(BB[:, q], p.c("hrs"), SF[:, q], 0.0, MUL, ADD), t, t2))
    VT = SF
    bf = lambda q, c: BB[:, q, 128 * c:128 * c + 128]
    vt = []
    for c in range(4):
        b, fr = ps.take(1)
        for h in range(4):
            t = p.tr(p.PSUM[:, b, h * 128:h * 128 + 128], IF[:, h, 128 * c:128 * c + 128], 128, fr, tk[(2, 3)], mark=(h == 3))
        t = p.copy(S, VT[:, c, :], p.PSUM[:, b, :], t, gb)
        ps.give(b, 1, t)
        vt.append(t)
    ps.at = 0
    ob = [ps.take(1) for _ in range(4)]
    first = [True] * 4
    lfree = [None, in_read]
    wfree = [None] * 4
    wi = 0
    def prepare(lev):
        m = 64 >> lev
        nbk = 512 // (2 * m)
        QL, KL = QK[lev % 2]
        zq = p.zero(G, QL, lfree[lev % 2])
        zk = p.zero(G, KL, lfree[lev % 2])
        tl = []
        for h in range(4):
            B = BB[:, h].rearrange("p (n m) -> p n m", m=2 * m)
            ref = B[:, :, m - 1:m].broadcast_to([128, nbk, m])
            ql = QL[:, h].rearrange("p (n m) -> p n m", m=2 * m)[:, :, m:]
            kl = KL[:, h].rearrange("p (n m) -> p n m", m=2 * m)[:, :, :m]
            t1 = p.tt(V, ql, B[:, :, m:], ref, SUB, zq, gb)
            t2 = p.tt(V, kl, ref, B[:, :, :m], SUB, zk)
            tl.append((ql, kl, p.act(ql, ql, ACT.Exp, t1), p.act(kl, kl, ACT.Exp, t2)))
        out = []
        for h, (ql, kl, t1, t2) in enumerate(tl):
            t1 = p.tt(V, ql, ql, QF[:, h].rearrange("p (n m) -> p n m", m=2 * m)[:, :, m:], MUL, t1, tk[(0, 3)])
            t2 = p.tt(V, kl, kl, KF[:, h].rearrange("p (n m) -> p n m", m=2 * m)[:, :, :m], MUL, t2)
            out.append([t1, t2])
        return QL, KL, out

    nxt_ = (QF, KF, [[], [], [], []])
    for lev in [7] + list(range(7)):
        qs, ks, tl = nxt_
        if lev == 7:
            nxt_ = prepare(0)
        elif lev < 6:
            nxt_ = prepare(lev + 1)
        wt_ = []

        def masked(h):
            nonlocal wi
            b, fr = ps.take_from(4, 8)
            for c in range(4):
                t = p.mm(p.PSUM[:, b, 128 * c:128 * c + 128], ks[:, h, 128 * c:128 * c + 128], qs[:, h, 128 * c:128 * c + 128],
                         True, True, fr, tl[h], gb, tk[(0, 3)], mark=(c == 3))
            W = WK[wi % 4].rearrange("p (c t) -> p c t", c=4)
            mk = p.c("hm")[:, lev * 128:lev * 128 + 128].unsqueeze(1).broadcast_to([128, 4, 128])
            mt = p.tt(V, W, p.PSUM[:, b, :].rearrange("p (c t) -> p c t", c=4), mk, MUL, t, wfree[wi % 4])
            ps.give(b, 1, mt)
            wi += 1
            return wi - 1, W, mt

        def gather(h, i, W, mt):
            for c in range(4):
                t2 = p.mm(p.PSUM[:, ob[h][0], 128 * c:128 * c + 128], VT[:, c, h * 128:h * 128 + 128], W[:, c],
                          first[h] and c == 0, False, mt, vt, ob[h][1], mark=(c == 3))
            first[h] = False
            wfree[i % 4] = t2

        held = []
        for h in range(4):
            held.append((h, *masked(h)))
            if h:
                gather(*held.pop(0))
            conv(1)
        gather(*held.pop(0))
        if lev < 7:
            lfree[lev % 2] = P.last()
    tq = []
    QL, KL = QK[1][0], QK[1][1]
    for h in range(4):
        t = p.act(QL[:, h], BB[:, h], ACT.Exp, lfree)
        tq.append(p.tt(V, QL[:, h], QL[:, h], QF[:, h], MUL, t))
    DE = p.small[:, 0:16].rearrange("p (a c) -> p a c", a=4)
    td = p.act(DE, BB[:, :, 127::128], ACT.Exp, gb)
    tke = []
    for h in range(4):
        B = BB[:, h].rearrange("p (n m) -> p n m", m=128)
        k_ = KL[:, h].rearrange("p (n m) -> p n m", m=128)
        t = p.tt(V, k_, B[:, :, 127:128].broadcast_to([128, 4, 128]), B, SUB, lfree)
        t = p.act(k_, k_, ACT.Exp, t)
        tke.append(p.tt(V, KL[:, h], KL[:, h], KF[:, h], MUL, t))
    KT = IF
    kt = []
    for c in range(3):
        b, fr = ps.take_from(4, 8)
        for h in range(4):
            t = p.tr(p.PSUM[:, b, h * 128:h * 128 + 128], KL[:, h, 128 * c:128 * c + 128], 128, fr, tke, mark=(h == 3))
        t = p.copy(S, KT[:, c, :], p.PSUM[:, b, :], t, vt)
        ps.give(b, 1, t)
        kt.append(t)
    ST = [WK[i].rearrange("p (h v) -> p h v", h=4) for i in range(2)]
    st = None
    for c in range(1, 4):
        b, fr = ps.take_from(4, 8)
        for h in range(4):
            t = p.mm(p.PSUM[:, b, h * 128:h * 128 + 128], KT[:, c - 1, h * 128:h * 128 + 128],
                     VT[:, c - 1, h * 128:h * 128 + 128], True, True, fr, kt, mark=(h == 3))
        pvw = p.PSUM[:, b, :].rearrange("p (h v) -> p h v", h=4)
        cur, nxt = ST[(c - 1) % 2], ST[c % 2]
        if c == 1:
            st = p.copy(V, nxt, pvw, t, wfree)
        else:
            d = DE[:, :, c - 1:c].broadcast_to([128, 4, 128])
            x_ = p.tt(V, nxt, cur, d, MUL, st, td, wfree)
            st = p.tt(V, nxt, nxt, pvw, ADD, x_, t)
        ps.give(b, 1, st)
        for h in range(4):
            t2 = p.mm(p.PSUM[:, ob[h][0], 128 * c:128 * c + 128], nxt[:, h], QL[:, h, 128 * c:128 * c + 128],
                      False, c == 3, st, tq, mark=(h == 3))
        wfree = [t2]
    conv(200)
    p.mark("hgrn")
    sq = [p.act(KL[:, h], p.PSUM[:, ob[h][0], 0:512], ACT.Square, t2, kt) for h in range(4)]
    ha = []
    for h in range(4):
        b, fr = ps.take_from(4, 8)
        t = p.mm(p.PSUM[:, b, 0:512], p.c("one"), KL[:, h], True, True, fr, sq[h], mark=True)
        t = p.rstd(BB[:, h], b, 512, 1.0 / 128, 1e-5, t, tke, tq)
        t = p.stt(BB[:, h], BB[:, h], p.col("hgrn_norm_w_2"), OG[:, h], MUL, MUL, t, tk[(3, h)])
        t = p.tt(V, OO[:, h], p.PSUM[:, ob[h][0], 0:512], BB[:, h], MUL, t)
        ha.append(t)
    for h in range(4):
        ps.give(ob[h][0], 1, ha[h], sq[h])
    hb = p.ln(lambda k: CVO[:, k], lambda k: QF[:, k], 4, lambda i: WK[2 + i], RS, [ctok[q] for q in range(4)] ,
              lambda k: p.col("conv_ln_g_2", k), lambda k: p.col("conv_ln_b_2", k), 512, ACT.Silu)
    p.dump("ha", OO, ha)
    p.dump("hb", QF, hb)
    high = p.parts["GH"].rearrange("p (k t) -> p k t", k=8)
    low = [p.parts[x].rearrange("p (k t) -> p k t", k=4) for x in ("OL", "QL")]
    assert o == ARENA_R["OL"][0] + 12800
    hx = [p.halve((S, V), high[:, k], low[k // 4][:, k % 4], (OO if k < 4 else QF)[:, k % 4],
                  ha[k] if k < 4 else hb[k - 4], ha) for k in range(8)]
    xt = []
    for m in range(8):
        b, t = p.lin("w_out_2", (0,), m, lambda k, a, n: (high[:, k, a:a + n], low[k // 4][:, k % 4, a:a + n]), 512, hx)
        q = p.ts(V, CVI[:, m % 4, 0:512], p.PSUM[:, b, 0:512], p.col("b_out_2", m), ADD, MOD[:, 16 + m:17 + m], MUL, t)
        ps.give(b, 1, q)
        xt.append(p.stt(XX[:, m], XX[:, m], ALPHA, CVI[:, m % 4, 0:512], MUL, ADD, q))
    p.all_wait()
    p.mark("wout2")
    yt = p.ln(lambda k: XX[:, k], lambda k: UU[:, k], 8, lambda i: WK[i], RS, xt,
              lambda k: p.col("ln1_g_2", k), lambda k: p.col("ln1_b_2", k), 1024)
    p.all_wait()
    return yt


def moe(p, XX, UU, xtok, MOD):
    V, S, G, P, ps = p.V, p.S, p.G, p.P, p.ps
    A = p.arena
    o = 0

    def buf(n):
        nonlocal o
        o += n
        return A[:, o - n:o]

    WK = [buf(512) for _ in range(2)]
    RS = buf(512)
    R = [buf(64).rearrange("p (t g e) -> p t g e", t=4, g=4) for _ in range(10)]
    r4 = [buf(16).rearrange("p (t g) -> p t g", t=4) for _ in range(8)]
    r1 = [buf(4).rearrange("p (t g) -> p t g", t=4) for _ in range(4)]
    ut = p.ln(lambda k: XX[:, k], lambda k: UU[:, k], 8, lambda i: WK[i], RS, xtok,
              lambda k: MOD[:, 32 + k:33 + k], lambda k: MOD[:, 24 + k:25 + k], 1024)
    rw = p.colr("router_w_2", 0, 128).rearrange("p (k e) -> p k e", k=8)
    b, fr = ps.take(1)
    for i in range(4):
        for k in range(8):
            t = p.mm(p.PSUM[:, b, 16 * i:16 * i + 16], UU[:, k, 128 * i:128 * i + 128], rw[:, k, :], k == 0, k == 7,
                     fr, ut, mark=(k == 7))
    s, sb, rank, cmpb, inv, sel, cmb = R[0], R[1], R[2], R[3], R[4], R[5], R[6]
    f = lambda x: x.rearrange("p t g e -> p (t g e)")
    t = p.act(f(s), p.PSUM[:, b, 0:64], ACT.Sigmoid, t)
    ps.give(b, 1, t)
    bias = p.colr("router_bias_2", 0, 16).unsqueeze(1).broadcast_to([128, 4, 16])
    t = p.tt(V, sb.rearrange("p t g e -> p t (g e)"), s.rearrange("p t g e -> p t (g e)"), bias, ADD, t)
    G0, tp = r4[0], r4[1]
    pairs = [(i, j) for i in range(4) for j in range(i + 1, 4)]
    for n, (i, j) in enumerate(pairs):
        d = G0 if n == 0 else tp
        t = p.tt(V, d, sb[:, :, :, i], sb[:, :, :, j], ADD, t)
        if n:
            t = p.tt(V, G0, G0, tp, MAX, t)
    gm = r1[0]
    t = V.do(lambda e: e.tensor_reduce(gm[:, :, 0], G0, AX.X, MAX), t)
    gs, left = r4[2], r1[1]
    t = p.tt(V, gs, G0, gm.broadcast_to([128, 4, 4]), ALU.is_ge, t)
    t = p.ts(V, left, gs[:, :, 0:1], -1.0, MUL, 1.0, ADD, t)
    for g in range(1, 4):
        t = p.tt(V, gs[:, :, g:g + 1], gs[:, :, g:g + 1], left, MUL, t)
        if g < 3:
            t = p.tt(V, left, left, gs[:, :, g:g + 1], SUB, t)
    t = p.zero(V, f(rank), t)
    for i, j in pairs:
        c1, c2 = r4[3], r4[4]
        t = p.tt(V, c1, sb[:, :, :, j], sb[:, :, :, i], ALU.is_gt, t)
        t = p.tt(V, rank[:, :, :, i], rank[:, :, :, i], c1, ADD, t)
        t = p.ts(V, c2, c1, -1.0, MUL, 1.0, ADD, t)
        t = p.tt(V, rank[:, :, :, j], rank[:, :, :, j], c2, ADD, t)
    t = p.ts(V, f(sel), f(rank), 1.5, ALU.is_lt, None, None, t)
    t = p.tt(V, sel, sel, gs.unsqueeze(3).broadcast_to([128, 4, 4, 4]), MUL, t)
    t = p.tt(V, f(cmb), f(sel), f(s), MUL, t)
    sm = r1[2]
    t = V.do(lambda e: e.tensor_reduce(sm[:, :, 0], cmb.rearrange("p t g e -> p t (g e)"), AX.X, ADD), t)
    t = p.recip(r1[3], sm, t)
    c3 = cmb.rearrange("p t g e -> p t (g e)")
    t = p.tt(V, c3, c3, r1[3].broadcast_to([128, 4, 16]), MUL, t)
    sf = f(sel)
    b, fr = ps.take(1)
    t1 = p.mm(p.PSUM[:, b, 0:64], p.c("tri"), sf, True, True, fr, t, mark=True)
    t2 = p.mm(p.PSUM[:, b, 128:192], p.c("one"), sf, True, True, mark=True)
    q3 = lambda x: x.rearrange("p t g e -> p t (g e)")
    slot, tot, cs, ra, rb = q3(R[7]), q3(R[8]), R[9], q3(R[3]), q3(R[4])
    t = p.copy(V, f(R[7]), p.PSUM[:, b, 0:64], t1, t2, t)
    t = p.copy(V, f(R[8]), p.PSUM[:, b, 128:192], t2, t)
    ps.give(b, 1, t)
    e16 = [buf(16) for _ in range(5)]
    run, nb_, ci, tmp, rst = e16
    m64 = buf(64)
    t = p.copy(V, run, tot[:, 0], t)
    for i in range(1, 4):
        t = p.tt(V, slot[:, i], slot[:, i], run, ADD, t)
        t = p.tt(V, run, run, tot[:, i], ADD, t)
    t = p.ts(V, nb_, run, 0.5, ALU.is_gt, None, None, t)
    for i in range(1, 4):
        t = p.ts(V, tmp, run, 128.0 * i + 0.5, ALU.is_gt, None, None, t)
        t = p.tt(V, nb_, nb_, tmp, ADD, t)
    t = V.do(lambda e: e.memset(rst, 1.0), t)
    t = V.do(lambda e: e.tensor_tensor_scan(ci, rst, nb_, 0.0, MUL, ADD), t)
    t = p.tt(V, tmp, ci, nb_, SUB, t)
    t = p.ts(V, tmp, tmp, 128.0, MUL, None, None, t)
    t = p.tt(V, slot, slot, tmp.unsqueeze(1).broadcast_to([128, 4, 16]), ADD, t)
    t = V.do(lambda e: e.memset(m64, 1.0), t)
    t = V.do(lambda e: e.memset(m64[:, 0:64:16], 0.0), t)
    t = V.do(lambda e: e.tensor_tensor_scan(f(cs), m64, sf, 0.0, MUL, ADD), t)
    CS = [buf(4) for _ in range(2)]
    SL = buf(8)
    for n in range(2):
        t = p.ts(V, f(R[3]), f(cs), float(n + 1), ALU.is_equal, None, None, t)
        t = p.tt(V, f(R[3]), f(R[3]), sf, MUL, t)
        t = p.tt(V, f(R[4]), f(R[3]), f(R[7]), MUL, t)
        t = V.do(lambda e, n=n: e.tensor_reduce(SL[:, 4 * n:4 * n + 4], rb, AX.X, ADD), t)
        t = p.tt(V, f(R[4]), f(R[3]), f(cmb), MUL, t)
        t = V.do(lambda e, n=n: e.tensor_reduce(CS[n], rb, AX.X, ADD), t)
    tix = p.copy(V, p.idx, SL, t)
    cmp3 = buf(NB * 16).rearrange("p (b e) -> p b e", b=NB)
    ebf = buf(NB)
    t = p.tt(V, cmp3, ci.unsqueeze(1).broadcast_to([128, NB, 16]), p.c("bi").unsqueeze(2).broadcast_to([128, NB, 16]),
             ALU.is_le, tix)
    t = V.do(lambda e: e.tensor_reduce(ebf, cmp3, AX.X, ADD), t)
    t = p.ts(V, ebf, ebf, 15.0, MIN, None, None, t)
    teb = p.copy(V, p.eb, ebf, t)
    tnb = p.copy(V, p.nused, ci[:, 15:16], teb)

    rg = p.ringf
    G_ = [rg[:, 1024 * i:1024 * i + 1024] for i in range(2)]
    UB = [rg[:, 2048 + 1024 * i:3072 + 1024 * i].rearrange("p (k t) -> p k t", k=8) for i in range(2)]
    YB = [rg[:, 4096 + 1024 * i:5120 + 1024 * i] for i in range(2)]
    HB = [rg[:, 6144 + 512 * i:6656 + 512 * i] for i in range(2)]
    HT = [rg[:, 7168 + 512 * i:7680 + 512 * i].rearrange("p (k t) -> p k t", k=4) for i in range(2)]
    SI = [rg[:, 8192 + 512 * i:8704 + 512 * i] for i in range(2)]
    base = 5000
    assert o <= base
    WM = [A[:, base + 4096 * i:base + 4096 * i + 4096] for i in range(6)]
    sct = []
    gfree = [None, None]
    for i in range(4):
        b, fr = ps.take(2)
        for k in range(8):
            t = p.tr(p.PSUM[:, b + k // 4, (k % 4) * 128:(k % 4) * 128 + 128], UU[:, k, 128 * i:128 * i + 128], 128,
                     fr, ut, P.last(), mark=(k == 7))
        g = G_[i % 2]
        t = p.copy(S if i % 2 else V, g.rearrange("p (a t) -> p a t", a=2), p.PSUM[:, b:b + 2, :], t, gfree[i % 2])
        ps.give(b, 2, t)
        G.need(t, tix, p.zeroed)
        for n in range(2):
            G.items.append((lambda e, g=g, c=4 * n + i, q=f"sc{i % 2}": e.indirect_dma_start(
                p.ug, bass.IndirectOffsetOnAxis(ap=p.idx[:, c:c + 1], axis=0), g, None).then_inc(p.sems[q], 16),
                False, None))
        gfree[i % 2] = (f"sc{i % 2}", 32 * (i // 2 + 1))
    scattered = [("sc0", 64), ("sc1", 64)]
    D = p.D
    wfree = [None] * 6
    ufree = [None, None]
    p.D.need(teb, p.fence())

    def load_w(bk):
        for part in range(3):
            i = (3 * bk + part) % 6
            D.need(wfree[i])
            box = p.box

            def go(e, bk=bk, part=part, i=i):
                if part == 0:
                    box[0] = e.value_load(p.eb[0:1, bk:bk + 1], min_val=0, max_val=15)
                return e.dma_start(WM[i], p.wmoe[part, bass.ds(box[0], 1)].rearrange("a p n -> (a p) n")).then_inc(
                    p.sems[f"mw{i}"], 16)

            D.dma(go, f"mw{i}")

    p.box = [None]

    def wtok(bk, part):
        i = (3 * bk + part) % 6
        return (f"mw{i}", 16 * ((3 * bk + part) // 6 + 1))

    def load_u(bk):
        i = bk % 2
        D.need(scattered, ufree[i])
        D.dma(lambda e: e.dma_start(G_[i], p.ug[128 * bk:128 * bk + 128, :]).then_inc(p.sems[f"ug{i}"], 16), f"ug{i}")

    ubf = [None, None]

    def turn_u(bk, part):
        i = bk % 2
        b, fr = ps.take(1)
        for k in range(4):
            t = p.tr(p.PSUM[:, b, k * 128:k * 128 + 128], G_[i][:, 512 * part + 128 * k:512 * part + 128 * k + 128], 128,
                     fr, (f"ug{i}", 16 * (bk // 2 + 1)), mark=(k == 3))
        ufree[i] = t
        t1 = p.copy((S, V)[part], UB[i][:, 4 * part:4 * part + 4, :], p.PSUM[:, b, :].rearrange("p (k t) -> p k t", k=4),
                    t, ubf[i])
        ps.give(b, 1, t1)
        return t1

    yfree, hfree, htf, sif = [None, None], [None, None], [None, None], [None, None]

    def down(bk, th):
        i = bk % 2
        wd = WM[(3 * bk + 2) % 6].rearrange("p (k n) -> p k n", k=4)
        b, fr = ps.take(2)
        for hf_ in range(2):
            for k in range(4):
                t = p.mm(p.PSUM[:, b + hf_, :], HT[i][:, k, :], wd[:, k, 512 * hf_:512 * hf_ + 512], k == 0, k == 3,
                         fr, th, wtok(bk, 2), mark=(k == 3))
        wfree[(3 * bk + 2) % 6] = t
        htf[i] = t
        t1 = p.copy(S, YB[i][:, 0:512], p.PSUM[:, b, :], t, yfree[i])
        t2 = p.copy(V, YB[i][:, 512:1024], p.PSUM[:, b + 1, :], t, yfree[i])
        ps.give(b, 2, t1, t2)
        S.need(t1, t2)
        S.dma(lambda e: e.dma_start(p.ys[128 * bk:128 * bk + 128, :], YB[i]).then_inc(p.sems[f"yo{i}"], 16), f"yo{i}")
        yfree[i] = (f"yo{i}", 16 * (bk // 2 + 1))

    load_u(0)
    load_w(0)
    load_u(1)
    load_w(1)
    tu = [turn_u(0, 0), turn_u(0, 1)]
    for q in (P, V, S, G, D):
        q.need(tnb)
        q.items.append(("blocks", None, None))
    for bk in range(NB):
        i = bk % 2
        if bk >= MINB:
            p.when(bk)
        wg = WM[(3 * bk) % 6].rearrange("p (k n) -> p k n", k=8)
        wu = WM[(3 * bk + 1) % 6].rearrange("p (k n) -> p k n", k=8)
        b1, fr = ps.take(1)
        for k in range(8):
            t1 = p.mm(p.PSUM[:, b1, :], UB[i][:, k, :], wg[:, k, :], k == 0, k == 7, fr, tu, wtok(bk, 0), mark=(k == 7))
        wfree[(3 * bk) % 6] = t1
        b2, fr = ps.take(1)
        for k in range(8):
            t2 = p.mm(p.PSUM[:, b2, :], UB[i][:, k, :], wu[:, k, :], k == 0, k == 7, fr, wtok(bk, 1), mark=(k == 7))
        wfree[(3 * bk + 1) % 6] = t2
        ubf[i] = t2
        s_ = p.act(SI[i], p.PSUM[:, b1, :], ACT.Silu, t1, sif[i])
        ps.give(b1, 1, s_)
        h_ = p.tt(V, HB[i], p.PSUM[:, b2, :], SI[i], MUL, s_, t2, hfree[i])
        ps.give(b2, 1, h_)
        sif[i] = h_
        if bk + 1 < NB:
            tu = [turn_u(bk + 1, 0)]
        b, fr = ps.take(1)
        for k in range(4):
            t = p.tr(p.PSUM[:, b, 128 * k:128 * k + 128], HB[i][:, 128 * k:128 * k + 128], 128, fr, h_, mark=(k == 3))
        hfree[i] = t
        th = p.copy(S, HT[i], p.PSUM[:, b, :].rearrange("p (k t) -> p k t", k=4), t, htf[i])
        ps.give(b, 1, th)
        if bk + 1 < NB:
            tu.append(turn_u(bk + 1, 1))
        down(bk, th)
        if bk >= MINB:
            p.over()
        if bk + 2 < NB:
            if bk + 2 >= MINB:
                p.when(bk + 2)
            load_u(bk + 2)
            load_w(bk + 2)
            if bk + 2 >= MINB:
                p.over()
    xa = [p.act(XX[:, k], XX[:, k], ACT.Copy, ut, scale=ALPHA) for k in range(8)]
    GB = [WM[j][:, 0:1024] for j in range(4)]
    gf = [None, None]
    xt = [None] * 8
    G.need(yfree[0], yfree[1], wfree)
    for i in range(4):
        for n in range(2):
            G.need(gf[i % 2])
            G.items.append((lambda e, dst=GB[2 * (i % 2) + n], c=4 * n + i, q=f"yg{i % 2}": e.indirect_dma_start(
                dst, None, p.ys, bass.IndirectOffsetOnAxis(ap=p.idx[:, c:c + 1], axis=0)).then_inc(p.sems[q], 16),
                False, None))
        ga, gb = GB[2 * (i % 2)], GB[2 * (i % 2) + 1]
        t = p.ts(V, ga, ga, CS[0][:, i:i + 1], MUL, None, None, (f"yg{i % 2}", 32 * (i // 2 + 1)))
        t = p.stt(ga, gb, CS[1][:, i:i + 1], ga, MUL, ADD, t)
        b, fr = ps.take(2)
        for k in range(8):
            t2 = p.tr(p.PSUM[:, b + k // 4, (k % 4) * 128:(k % 4) * 128 + 128], ga[:, 128 * k:128 * k + 128], 128,
                      fr, t, mark=(k == 7))
        gf[i % 2] = t2
        for k in range(8):
            xt[k] = p.stt(XX[:, k, 128 * i:128 * i + 128], p.PSUM[:, b + k // 4, (k % 4) * 128:(k % 4) * 128 + 128],
                          MOD[:, 40 + k:41 + k], XX[:, k, 128 * i:128 * i + 128], MUL, ADD, t2, xa)
        ps.give(b, 2, xt[7])
    p.all_wait()
    ot = p.ln(lambda k: XX[:, k], lambda k: UU[:, k], 8, lambda i: WK[i], RS, xt,
              lambda k: p.col("ln2_g_2", k), lambda k: p.col("ln2_b_2", k), 1024)
    return ot


def trace(p, cols, cst, cst2, outp, XRf, HRf, MOD, stage, dumps):
    X, H, XR, HR = [x.rearrange("p (k t) -> p k t", k=8) for x in (p.Xf, p.Hf, XRf, HRf)]

    def take_from(a, z):
        if not a <= p.ps.at < z:
            p.ps.at = a
        return p.ps.take(1)

    p.ps.take_from = take_from
    ndump = [0]

    def dump(name, ap, toks):
        if name in dumps:
            d = dumps[name]
            p.D.need(toks)
            p.D.items.append((lambda e: e.dma_start(d, ap).then_inc(p.sems["out"], 16), False, None))
            ndump[0] += 1

    p.dump = dump
    for dst, src in ((p.Xf, p.xin), (p.COLS, cols), (p.K, cst)):
        p.D.items.append((lambda e, dst=dst, src=src: e.dma_start(dst, src).then_inc(p.sems["in"], 16), False, None))
    ready = ("in", 48)
    for q in (p.P, p.V, p.S, p.G):
        q.need(ready)
    zt = stage[:, 0:1024]
    z = p.zero(p.G, zt)
    p.zeroed = ("zr", 16 * NB)

    def zero_rows(after):
        p.G.need(z, after)
        for i in range(NB):
            p.G.items.append((lambda e, i=i: e.dma_start(p.ug[128 * i:128 * i + 128, :], zt).then_inc(
                p.sems["zr"], 16), False, None))

    p.zero_rows = zero_rows

    def zero_results():
        t = p.zero(p.G, zt)
        p.G.need(t)
        for i in range(MINB, NB):
            p.G.items.append((lambda e, i=i: e.dma_start(p.ys[128 * i:128 * i + 128, :], zt).then_inc(
                p.sems["zy"], 16), False, None))

    p.zero_results = zero_results
    steps = ada(p, MOD, p.small[:, 600:608])

    def ada_step(n):
        for _ in range(n):
            next(steps, None)

    xt = [ready] * 8
    for l in range(2):
        xt = first_layer(p, l, X, XR, H, HR, xt, ada_step)
    rs = p.small[:, 64:64 + 512]
    XX = p.Hf[:, 0:4096].rearrange("p (k t) -> p k t", k=8)
    UU = p.Xf[:, 0:4096].rearrange("p (k t) -> p k t", k=8)
    UR = XRf[:, 0:4096].rearrange("p (k t) -> p k t", k=8)
    xt = p.rms(lambda k: X[:, k, 16:528], lambda k: XX[:, k], 512, "norm_final", None, xt, rs)
    p.dump("mid", XX, xt)
    p.all_wait()
    assert next(steps, 0) == 0
    o2 = p.cat["hrs"][0]
    p.D.need(p.fence())
    p.D.items.append((lambda e: e.dma_start(p.K[:, o2:o2 + 1664 + NB], cst2).then_inc(p.sems["in"], 16), False, None))
    for q in (p.P, p.V):
        q.need(("in", 64))
    yt = mixer2(p, XX, UU, UR, xt, MOD)
    p.dump("mx", UU, yt)
    ot = moe(p, UU, XX, yt, MOD)
    p.mark("moe")
    p.D.need(ot)
    p.D.items.append((lambda e: e.dma_start(outp, p.Hf[:, 0:4096]).then_inc(p.sems["out"], 16), False, None))
    p.D.items.append((None, "out", 16 * (1 + ndump[0])))


def build(nc, xin, cols, cst, cst2, wmoe, outp, dumps=()):
    ctx = ExitStack()
    with ctx:
        cat, nk = const_plan()
        cols_at, ncol = col_plan()
        sbt = lambda name, n: ctx.enter_context(nc.sbuf_tensor(name, [128, n], F32))[:, :]
        COLS, K, MOD = sbt("COLS", ncol), sbt("CST", nk), sbt("MOD", 48)
        small, adab, stage = sbt("SMALL", 700), sbt("ADAB", 256), sbt("STAGE", 2 * T)
        base = (nc.sbuf_base + 63) // 64 * 64
        nb = (NRING + NHIGH) * SLAB
        size = 16 * T + nb + 29600
        ctx.enter_context(nc.sbuf_tensor("MEM", [128, size + 16], F32))
        at = lambda name, kind, a, n: nc.alloc_sbuf_tensor_at(name, [128, n], kind, offset=base + 4 * a)[:, :]
        Xf, Hf = at("X", F32, 0, 8 * T), at("H", F32, 8 * T, 8 * T)
        XRf, HRf = at("XR", F32R, 0, 8 * T), at("HR", F32R, 8 * T, 8 * T)
        rg, ar = 16 * T, 16 * T + nb
        ringf, arena = at("RING", F32, rg, nb), at("ARENA", F32, ar, 29600)
        ringR, highR = at("RINGR", F32R, rg, NRING * SLAB), at("HIGHR", F32R, rg + NRING * SLAB, NHIGH * SLAB)
        parts = {name: at(name, F32R, ar + a, n) for name, (a, n) in ARENA_R.items()}
        gates = nc.dram_tensor("gates", [48, 128, T], F32).ap()
        xkeep = nc.dram_tensor("xkeep", [128, 8 * T], F32).ap()
        ug = nc.dram_tensor("ug", [NB * 128, 1024], F32).ap()
        ys = nc.dram_tensor("ys", [NB * 128, 1024], F32).ap()
        idx = ctx.enter_context(nc.sbuf_tensor("IDXI", [128, 8], I32))[:, :]
        nblk = ctx.enter_context(nc.sbuf_tensor("NBI", [128, 1], I32))[:, :]
        eb = ctx.enter_context(nc.sbuf_tensor("EBI", [128, NB], I32))[:, :]
        PSUM = ctx.enter_context(nc.psum_tensor("PS", [128, 8, 512], F32))[:, :, :]
        names = ["pe", "dve", "act", "pool", "sp", "in", "out", "gw0", "gw1", "gr0", "gr1", "gr2", "zr", "zy", "sc0", "sc1", "yg0", "yg1"] + \
            [f"mw{i}" for i in range(6)] + ["ug0", "ug1", "yo0", "yo1", "xs", "xr"] + [f"w{i}" for i in range(NRING)]
        sems = {n: ctx.enter_context(nc.semaphore("s_" + n)) for n in names}
        plan = None
        for _ in range(2):
            p = Program(plan)
            p.cat, p.cols_at, p.COLS, p.K, p.small, p.adab = cat, cols_at, COLS, K, small, adab
            p.stage = stage.rearrange("p (a t) -> p a t", a=2)
            p.gates, p.xkeep, p.xin, p.ug, p.ys, p.idx, p.eb, p.nused = gates, xkeep, xin, ug, ys, idx, eb, nblk
            p.PSUM, p.sems, p.wmoe = PSUM, sems, wmoe
            p.Xf, p.Hf, p.ringf, p.arena, p.parts = Xf, Hf, ringf, arena, parts
            p.ring = ringf[:, 0:NRING * SLAB].rearrange("p (s n) -> p s n", s=NRING)
            p.ringR = ringR.rearrange("p (s n) -> p s n", s=NRING)
            p.highR = highR.rearrange("p (s n) -> p s n", s=NHIGH)
            trace(p, cols, cst, cst2, outp, XRf, HRf, MOD, stage, dumps)
            plan = p.slabs
        p.wts = nc.dram_tensor("wts", [p.slab_end], F32, kind="ExternalInput").ap()

        block = ctx.enter_context(nc.Block())

        def emit(q):
            def run(eng, items):
                for fn, a, b in items:
                    if fn is None:
                        eng.wait_ge(sems[a], b)
                    else:
                        ins = fn(eng)
                        if a:
                            ins.then_inc(sems[q.name], 1)

            def skip(eng, items, at):
                own = 0

                def flush():
                    if own:
                        eng.wait_ge(sems[q.name], at[q.name])
                        eng.sem_inc(sems[q.name], own)

                for fn, a, b in items:
                    if fn is None:
                        flush()
                        at[q.name] += own
                        own = 0
                        eng.wait_ge(sems[a], b)
                    elif b is not None:
                        eng.wait_ge(sems[b], at.get(b, 0))
                        eng.sem_inc(sems[b], 16)
                        at[b] = at.get(b, 0) + 16
                    elif a:
                        own += 1
                flush()

            def body(eng):
                at, region, nblocks = {q.name: 0}, None, None
                for it in q.items:
                    fn, a, b = it
                    if fn == "blocks":
                        nblocks = eng.value_load(nblk[0:1, 0:1], min_val=MINB, max_val=NB)
                    elif fn == "when":
                        region, k = [], a
                    elif fn == "over":
                        if region:
                            with eng.If(nblocks > k):
                                run(eng, region)
                            with eng.Else():
                                skip(eng, region, dict(at))
                            for f, a_, b_ in region:
                                if f is not None and b_ is not None:
                                    at[b_] = at.get(b_, 0) + 16
                                elif f is not None and a_:
                                    at[q.name] += 1
                        region = None
                    elif region is not None:
                        region.append(it)
                    else:
                        run(eng, [it])
                        if fn is not None and b is not None:
                            at[b] = at.get(b, 0) + 16
                        elif fn is not None and a:
                            at[q.name] += 1
            return body

        block.sync(emit(p.D))
        block.tensor(emit(p.P))
        block.vector(emit(p.V))
        block.scalar(emit(p.S))
        block.gpsimd(emit(p.G))
    return [pieces for pieces, _ in p.slabs]


def pack_cols(inp):
    at, n = col_plan()
    c = np.zeros((128, n), np.float32)

    def put(key, a):
        a = np.reshape(a, (-1, 128))
        c[:, at[key]:at[key] + a.shape[0]] = a.T

    for l in range(2):
        for name in ("norm_mix", "norm_ffn", "pool_scale", "da_subln", "rw_mu", "rw_w0", "rw_a0", "rw_k_k",
                     "rw_k_a", "rw_r_k", "rw_lnx_w", "rw_lnx_b", "ffn_conv"):
            put((name, l), inp[name][l])
        o = at[("da_lambda", l)]
        c[0:64, o:o + 4] = inp["da_lambda"][l].T
    for name in ("norm_final", "c_2", "ada_b_2", "b_in_2", "hgrn_lb_2", "hgrn_norm_w_2", "conv_w_2", "conv_b_2",
                 "conv_ln_g_2", "conv_ln_b_2", "b_out_2", "ln1_g_2", "ln1_b_2", "ln2_g_2", "ln2_b_2"):
        put(name, inp[name])
    o = at["router_bias_2"]
    c[:, o:o + 16] = inp["router_bias_2"][None, :]
    o = at["router_w_2"]
    c[:, o:o + 128] = inp["router_w_2"].reshape(8, 128, 16).transpose(1, 0, 2).reshape(128, 128)
    return c


def pack_weights(slabs, inp):
    parts = []
    for pieces in slabs:
        cut = []
        for name, idx, k0, nk, c0, ncol in pieces:
            if name == "wa2":
                a = np.concatenate([inp["rw_w2"][idx[0]], inp["rw_a2"][idx[0]]], axis=0)
            elif name == "pool_w":
                a = inp["pool_w"][idx[0]].reshape(512, 128)
            else:
                a = inp[name]
                for i in idx:
                    a = a[i]
            a = a[k0 * 128:(k0 + nk) * 128, c0:c0 + ncol]
            cut.append(a.reshape(nk, 128, ncol).transpose(1, 0, 2).reshape(128, nk * ncol))
        parts.append(np.concatenate(cut, axis=1).reshape(-1))
    return np.concatenate(parts)


def pack_experts(inp):
    a = [inp["w_gate_2"][0].reshape(16, 8, 128, 512), inp["w_up_2"][0].reshape(16, 8, 128, 512),
         inp["w_down_2"][0].reshape(16, 4, 128, 1024)]
    return np.stack([x.transpose(0, 2, 1, 3).reshape(16, 128, 4096) for x in a])


def kernel(**inputs):
    import concourse.bacc as _bacc
    from concourse.bass_utils import run_bass_kernel_spmd as _run

    inp = {k: np.asarray(v) for k, v in inputs.items()}
    nc = _bacc.Bacc("TRN2", target_bir_lowering=False, num_devices=1)
    cols, cst, cst2 = pack_cols(inp), consts(0), consts(1)
    x = np.concatenate([inp["meta_tokens"], inp["x"][0]], axis=0)
    x = np.ascontiguousarray(x.T.reshape(8, 128, T).transpose(1, 0, 2).reshape(128, 8 * T))
    dr = lambda name, shape, kind: nc.dram_tensor(name, shape, F32, kind=kind).ap()
    xin = dr("xin", x.shape, "ExternalInput")
    cin = dr("cols", cols.shape, "ExternalInput")
    kin = dr("cst", cst.shape, "ExternalInput")
    wm = dr("wmoe", (3, 16, 128, 4096), "ExternalInput")
    kin2 = dr("cst2", cst2.shape, "ExternalInput")
    outp = dr("outp", (128, 4096), "ExternalOutput")
    slabs = build(nc, xin, cin, kin, kin2, wm, outp)
    wts = pack_weights(slabs, inp)
    r = _run(nc, [{"xin": x, "cols": cols, "cst": cst, "cst2": cst2, "wmoe": pack_experts(inp), "wts": wts}], core_ids=[0])
    y = np.asarray(r.results[0]["outp"]).reshape(128, 8, 512)
    return y.transpose(2, 1, 0).reshape(1, 512, 1024)
```
